# Optimizing a Trainium2 kernel written in Bass

```python
import jax, jax.numpy as jnp
from jax import lax
import numpy as np

D_MODEL = 1024
BATCH = 1
SEQ = 1024
DEPTH = 1

LRU_WIDTH = 5 * D_MODEL // 4
LRU_BLOCKS = 16
LRU_BLOCK = LRU_WIDTH // LRU_BLOCKS
CONV_WIDTH = 4
LRU_C = 8.0
RW_HEAD = 64
RW_WIDTH = D_MODEL
RW_HEADS = RW_WIDTH // RW_HEAD
RW_DECAY_LORA = 64
RW_AAA_LORA = 64
RW_MV_LORA = 32
RW_GATE_LORA = 160
RW_LN_EPS = 64e-5
ATT_HEAD = 64
ATT_HEADS = D_MODEL // ATT_HEAD
ATT_KV_HEADS = ATT_HEADS // 4
ATT_GROUP = ATT_HEADS // ATT_KV_HEADS
ATT_WIDTH = ATT_HEADS * ATT_HEAD
KV_WIDTH = ATT_KV_HEADS * ATT_HEAD
WINDOW = 128
BLOCK = 128
D_FF = -(-8 * D_MODEL // (3 * 256)) * 256
N_BRANCH = 3
RMS_EPS = 1e-6
QK_EPS = 1e-6
NEG_INF = -1e30

RW_SIZES = (RW_WIDTH, RW_WIDTH, RW_WIDTH, RW_DECAY_LORA, RW_AAA_LORA, RW_GATE_LORA)
RW_COLS = sum(RW_SIZES)
RW_POINTS = tuple(int(v) for v in np.cumsum(RW_SIZES)[:-1])
IN_SIZES = (LRU_WIDTH, LRU_WIDTH, RW_COLS, ATT_WIDTH, KV_WIDTH, KV_WIDTH, N_BRANCH * D_MODEL)
IN_COLS = sum(IN_SIZES)
IN_POINTS = tuple(int(v) for v in np.cumsum(IN_SIZES)[:-1])

kernel_name = "hybrid_rglru_rwkv7_swa_parallel"

def rms_norm(x):
    xf = x.astype(jnp.float32)
    return (xf * lax.rsqrt(jnp.mean(xf * xf, -1, keepdims=True) + RMS_EPS)).astype(x.dtype)

def shift_right(t):
    return jnp.concatenate([jnp.zeros_like(t[:, :1]), t[:, :-1]], axis=1)

def causal_conv(x, w, b):
    S = x.shape[1]
    K = w.shape[0]
    xp = jnp.pad(x, ((0, 0), (K - 1, 0), (0, 0)))
    out = b
    for j in range(K):
        out = out + xp[:, j:j + S] * w[j]
    return out

def rg_lru(x, w_a, b_a, w_x, b_x, lam):
    B, S, _ = x.shape
    xb = x.reshape(B, S, LRU_BLOCKS, LRU_BLOCK)
    gate_a = jax.nn.sigmoid(jnp.einsum('bsni,nij->bsnj', xb, w_a).reshape(B, S, LRU_WIDTH) + b_a)
    gate_x = jax.nn.sigmoid(jnp.einsum('bsni,nij->bsnj', xb, w_x).reshape(B, S, LRU_WIDTH) + b_x)
    log_a = -LRU_C * gate_a.astype(jnp.float32) * jax.nn.softplus(-lam.astype(jnp.float32))
    a = jnp.exp(log_a)
    mult = jnp.sqrt(1.0 - jnp.exp(2.0 * log_a))
    u = x.astype(jnp.float32) * gate_x.astype(jnp.float32) * mult

    def combine(left, right):
        a_l, b_l = left
        a_r, b_r = right
        return a_l * a_r, a_r * b_l + b_r

    _, h = lax.associative_scan(combine, (a, u), axis=1)
    return h.astype(x.dtype)

def rwkv7_scan(r, w, k, v, a, b):
    B, S, H, N = r.shape

    def step(state, inp):
        r_t, w_t, k_t, v_t, a_t, b_t = inp
        sa = jnp.einsum('bhvk,bhk->bhv', state, a_t)
        state = (state * w_t[:, :, None, :] + sa[..., None] * b_t[:, :, None, :]
                 + v_t[..., None] * k_t[:, :, None, :])
        return state, jnp.einsum('bhvk,bhk->bhv', state, r_t)

    xs = tuple(jnp.moveaxis(t, 1, 0) for t in (r, w, k, v, a, b))
    init = jnp.zeros((B, H, N, N), jnp.float32)
    _, ys = lax.scan(step, init, xs)
    return jnp.moveaxis(ys, 0, 1)

def rwkv7_time_mix(p_rw, mu, w0, w2, a0, a2, g2, k_k, k_a, r_k, ln_w, ln_b, v_first, v_mix):
    B, S, _ = p_rw.shape
    p = p_rw + (shift_right(p_rw) - p_rw) * mu
    r, k, v, wl, al, gl = jnp.split(p, RW_POINTS, axis=-1)
    w = -jax.nn.softplus(-(w0 + jnp.tanh(wl) @ w2)) - 0.5
    a = jax.nn.sigmoid(a0 + al @ a2)
    g = jax.nn.sigmoid(gl) @ g2
    if v_mix is not None:
        v = v + (v_first - v) * v_mix

    def heads(t):
        return t.reshape(B, S, RW_HEADS, RW_HEAD).astype(jnp.float32)

    kk = heads(k * k_k)
    kk = kk * lax.rsqrt(jnp.maximum(jnp.sum(kk * kk, -1, keepdims=True), 1e-24))
    k = k * (1 + (a - 1) * k_a)
    rh, kh, vh, ah = heads(r), heads(k), heads(v), heads(a)
    decay = jnp.exp(-jnp.exp(heads(w)))
    y = rwkv7_scan(rh, decay, kh, vh, -kk, kk * ah)
    mean = jnp.mean(y, -1, keepdims=True)
    var = jnp.mean(jnp.square(y - mean), -1, keepdims=True)
    y = ((y - mean) * lax.rsqrt(var + RW_LN_EPS)).reshape(B, S, RW_WIDTH) * ln_w + ln_b
    r_k_h = r_k.reshape(RW_HEADS, RW_HEAD).astype(jnp.float32)
    bonus = jnp.sum(rh * kh * r_k_h, -1, keepdims=True) * vh
    out = (y + bonus.reshape(B, S, RW_WIDTH)) * g
    return out.astype(p_rw.dtype), v

def head_rms(t, gain):
    tf = t.astype(jnp.float32)
    return (tf * lax.rsqrt(jnp.mean(tf * tf, -1, keepdims=True) + QK_EPS) * gain).astype(t.dtype)

def band(t):
    B, S = t.shape[:2]
    tb = t.reshape((B, S // BLOCK, BLOCK) + t.shape[2:])
    prev = jnp.concatenate([jnp.zeros_like(tb[:, :1]), tb[:, :-1]], axis=1)
    return jnp.concatenate([prev, tb], axis=2)

def sliding_window_attention(q, k, v, q_gain, k_gain, sinks):
    B, S, _ = q.shape
    NB = S // BLOCK
    q = head_rms(q.reshape(B, S, ATT_KV_HEADS, ATT_GROUP, ATT_HEAD), q_gain)
    k = head_rms(k.reshape(B, S, ATT_KV_HEADS, ATT_HEAD), k_gain)
    v = v.reshape(B, S, ATT_KV_HEADS, ATT_HEAD)
    qb = q.reshape(B, NB, BLOCK, ATT_KV_HEADS, ATT_GROUP, ATT_HEAD)
    kb, vb = band(k), band(v)
    s = jnp.einsum('bnqkgd,bnjkd->bkgnqj', qb, kb).astype(jnp.float32) * (ATT_HEAD ** -0.5)
    qi = jnp.arange(BLOCK)[:, None] + BLOCK
    kj = jnp.arange(2 * BLOCK)[None, :]
    local = (kj <= qi) & (qi - kj < WINDOW)
    valid = (jnp.arange(NB)[:, None, None] * BLOCK - BLOCK + kj[None]) >= 0
    mask = local[None] & valid
    s = jnp.where(mask, s, NEG_INF)
    sink = sinks.reshape(ATT_KV_HEADS, ATT_GROUP).astype(jnp.float32)[None, :, :, None, None, None]
    m = jnp.maximum(jnp.max(s, -1, keepdims=True), sink)
    e = jnp.exp(s - m)
    probs = e / (jnp.sum(e, -1, keepdims=True) + jnp.exp(sink - m))
    o = jnp.einsum('bkgnqj,bnjkd->bnqkgd', probs.astype(v.dtype), vb)
    return o.reshape(B, S, ATT_WIDTH)

def swiglu(h, w_in, w_out):
    gate, up = jnp.split(h @ w_in, 2, axis=-1)
    return (jax.nn.silu(gate) * up) @ w_out

def setup_inputs(seed: int = 0) -> dict:
    key = jax.random.key(seed)
    ks = jax.random.split(key, 40)
    f32 = jnp.float32
    L = DEPTH

    def nrm(k, shape, scale):
        return jax.random.normal(k, shape, f32) * scale

    a_init = jax.random.uniform(ks[11], (L, LRU_WIDTH), f32, 0.9, 0.999)
    s_init = a_init ** (1.0 / LRU_C)
    lam = jnp.log(s_init) - jnp.log1p(-s_init)
    return {
        "x": nrm(ks[0], (BATCH, SEQ, D_MODEL), 1.0),
        "c": nrm(ks[1], (BATCH, D_MODEL), 1.0),
        "w_ada": nrm(ks[2], (L, D_MODEL, 6 * D_MODEL), 0.5 * D_MODEL ** -0.5),
        "b_ada": nrm(ks[3], (L, 6 * D_MODEL), 0.02),
        "w_in": nrm(ks[4], (L, D_MODEL, IN_COLS), D_MODEL ** -0.5),
        "conv_w": nrm(ks[5], (L, CONV_WIDTH, LRU_WIDTH), CONV_WIDTH ** -0.5),
        "conv_b": nrm(ks[6], (L, LRU_WIDTH), 0.02),
        "lru_wa": nrm(ks[7], (L, LRU_BLOCKS, LRU_BLOCK, LRU_BLOCK), LRU_BLOCK ** -0.5),
        "lru_ba": nrm(ks[8], (L, LRU_WIDTH), 0.02),
        "lru_wx": nrm(ks[9], (L, LRU_BLOCKS, LRU_BLOCK, LRU_BLOCK), LRU_BLOCK ** -0.5),
        "lru_bx": nrm(ks[10], (L, LRU_WIDTH), 0.02),
        "lru_lambda": lam,
        "w_lru_o": nrm(ks[12], (L, LRU_WIDTH, D_MODEL), LRU_WIDTH ** -0.5),
        "rw_mu": jax.random.uniform(ks[13], (L, RW_COLS), f32),
        "rw_w0": jax.random.uniform(ks[14], (L, RW_WIDTH), f32, -6.0, 0.0),
        "rw_w2": nrm(ks[15], (L, RW_DECAY_LORA, RW_WIDTH), 0.1 * RW_DECAY_LORA ** -0.5),
        "rw_a0": nrm(ks[16], (L, RW_WIDTH), 0.1),
        "rw_a2": nrm(ks[17], (L, RW_AAA_LORA, RW_WIDTH), 0.1 * RW_AAA_LORA ** -0.5),
        "rw_g2": nrm(ks[18], (L, RW_GATE_LORA, RW_WIDTH), RW_GATE_LORA ** -0.5),
        "rw_kk": 0.85 + nrm(ks[19], (L, RW_WIDTH), 0.05),
        "rw_ka": 1.0 + nrm(ks[20], (L, RW_WIDTH), 0.05),
        "rw_rk": nrm(ks[21], (L, RW_WIDTH), 0.1),
        "rw_ln_w": 1.0 + nrm(ks[22], (L, RW_WIDTH), 0.05),
        "rw_ln_b": nrm(ks[23], (L, RW_WIDTH), 0.02),
        "rw_v0": nrm(ks[24], (L - 1, RW_WIDTH), 0.1),
        "rw_v1": nrm(ks[25], (L - 1, D_MODEL, RW_MV_LORA), D_MODEL ** -0.5),
        "rw_v2": nrm(ks[26], (L - 1, RW_MV_LORA, RW_WIDTH), 0.1 * RW_MV_LORA ** -0.5),
        "w_rw_o": nrm(ks[27], (L, RW_WIDTH, D_MODEL), RW_WIDTH ** -0.5),
        "q_gain": 1.0 + nrm(ks[28], (L, ATT_HEAD), 0.05),
        "k_gain": 1.0 + nrm(ks[29], (L, ATT_HEAD), 0.05),
        "sinks": nrm(ks[30], (L, ATT_HEADS), 0.5),
        "w_att_o": nrm(ks[31], (L, ATT_WIDTH, D_MODEL), ATT_WIDTH ** -0.5),
        "w_out": nrm(ks[32], (L, D_MODEL, D_MODEL), D_MODEL ** -0.5),
        "w_ffn_in": nrm(ks[33], (L, D_MODEL, 2 * D_FF), D_MODEL ** -0.5),
        "w_ffn_out": nrm(ks[34], (L, D_FF, D_MODEL), D_FF ** -0.5),
    }

def reference(x, c, w_ada, b_ada, w_in, conv_w, conv_b, lru_wa, lru_ba, lru_wx, lru_bx,
              lru_lambda, w_lru_o, rw_mu, rw_w0, rw_w2, rw_a0, rw_a2, rw_g2, rw_kk, rw_ka,
              rw_rk, rw_ln_w, rw_ln_b, rw_v0, rw_v1, rw_v2, w_rw_o, q_gain, k_gain, sinks,
              w_att_o, w_out, w_ffn_in, w_ffn_out):
    c_act = jax.nn.silu(c)
    v_first = None
    for i in range(DEPTH):
        mod = (c_act @ w_ada[i] + b_ada[i])[:, None, :]
        sh1, sc1, g1, sh2, sc2, g2 = jnp.split(mod, 6, axis=-1)

        h = rms_norm(x) * (1 + sc1) + sh1
        proj = h @ w_in[i]
        lru_x, lru_y, p_rw, q, k, v, gates = jnp.split(proj, IN_POINTS, axis=-1)

        xa = causal_conv(lru_x, conv_w[i], conv_b[i])
        ha = rg_lru(xa, lru_wa[i], lru_ba[i], lru_wx[i], lru_bx[i], lru_lambda[i])
        o_a = (ha * jax.nn.gelu(lru_y)) @ w_lru_o[i]

        if i == 0:
            v_mix = None
        else:
            v_mix = jax.nn.sigmoid(rw_v0[i - 1] + (h @ rw_v1[i - 1]) @ rw_v2[i - 1])
        y_b, v_cur = rwkv7_time_mix(p_rw, rw_mu[i], rw_w0[i], rw_w2[i], rw_a0[i], rw_a2[i],
                                    rw_g2[i], rw_kk[i], rw_ka[i], rw_rk[i], rw_ln_w[i],
                                    rw_ln_b[i], v_first, v_mix)
        if i == 0:
            v_first = v_cur
        o_b = y_b @ w_rw_o[i]

        y_c = sliding_window_attention(q, k, v, q_gain[i], k_gain[i], sinks[i])
        o_c = y_c @ w_att_o[i]

        gate_a, gate_b, gate_c = jnp.split(jax.nn.sigmoid(gates), N_BRANCH, axis=-1)
        mixed = (gate_a * o_a + gate_b * o_b + gate_c * o_c) @ w_out[i]
        x = x + g1 * mixed

        h2 = rms_norm(x) * (1 + sc2) + sh2
        x = x + g2 * swiglu(h2, w_ffn_in[i], w_ffn_out[i])
    return x


_drawn_inputs = setup_inputs


def setup_inputs(seed=0):
    import zlib

    import numpy as np

    out = dict(_drawn_inputs(seed))
    spreads = {}
    factors = {'conv_b': 4.466,
     'lru_ba': 64.0,
     'lru_bx': 37.787,
     'rw_w2': 8.0,
     'rw_a0': 8.0,
     'rw_a2': 8.0,
     'rw_kk': 7.734,
     'rw_ka': 8.0,
     'rw_ln_w': 8.0,
     'rw_ln_b': 43.578,
     'q_gain': 8.0,
     'k_gain': 8.0,
     'sinks': 64.0}
    for name, (base, spread) in spreads.items():
        noise = np.random.default_rng([zlib.crc32(name.encode()), seed]).standard_normal(out[name].shape)
        drawn = base * np.exp(spread * noise) if base else spread * noise
        out[name] = __import__('jax').numpy.asarray(drawn.astype(out[name].dtype))
    for name, factor in factors.items():
        out[name] = (out[name] * factor).astype(out[name].dtype)
    return out
```

```python
import math
from contextlib import ExitStack

import numpy as np

import concourse.bass as bass
from concourse import mybir

F32 = mybir.dt.float32
F32R = mybir.dt.float32r
I32 = mybir.dt.int32
ALU = mybir.AluOpType
ACT = mybir.ActivationFunctionType
AX = mybir.AxisListType

P = 128
T = 1024
D = 1024
KT = D // P
LRU_W, LRU_BLK = 1280, 80
LRU_N = LRU_W // LRU_BLK
RW_W, RW_H = 1024, 64
PAIRS = RW_W // P
KV_HEADS, HEAD = 4, 64
FF = 2816
FF_GROUP = 2
CHUNK = 128
CHUNKS = T // CHUNK
LEVELS = int(math.log2(CHUNK))
DECAY = math.exp(-0.5)
NEG = -1e30

COL_LX, COL_LY = 0, LRU_W
COL_RW = 2 * LRU_W
COL_LORA = COL_RW + 3 * RW_W
COL_Q = COL_LORA + 288
COL_K = COL_Q + 1024
COL_V = COL_K + 256
COL_G = COL_V + 256

PR_W0, PR_A0, PR_KK, PR_KA, PR_RK, PR_LNW, PR_LNB, PR_MU = range(0, 64, 8)
PR_MU_WA, PR_MU_G0, PR_MU_G1, PR_ROWS = 80, 81, 82, 83
LP_CW, LP_CB, LP_BA, LP_BX, LP_LAM = 0, 64, 80, 96, 112
MOD_SH1, MOD_SC1, MOD_G1, MOD_SH2, MOD_SC2, MOD_G2, MOD_N = range(0, 56, 8)

C_ID, C_BD, C_ONE, C_ATT, C_AM, C_LV = 0, 128, 256, 384, 896, 1152
C_N = C_LV + 2 * LEVELS * P
C_KEEP = C_ATT

STREAM = [("ada1", 8, 2), ("lora", 1, 3), ("rwkv", PAIRS, 6), ("lru", LRU_N // 2, 4), ("att", 2, 6), ("ada2", 16, 2),
          ("oa1", 4, 2), ("oa2", 4, 2), ("oc", 4, 2), ("ob", 4, 2), ("wout", 4, 2), ("ffn", FF // P // FF_GROUP, 6)]
STREAM_START = 2
BASE, _at = {}, STREAM_START
for _name, _turns, _per in STREAM:
    BASE[_name] = _at
    _at += _turns * _per
TURNS = {n: t for n, t, _ in STREAM}
PER = {n: p for n, _, p in STREAM}


def constants():
    c = np.zeros((P, C_N), np.float32)
    r, k = np.arange(P)[:, None], np.arange(P)[None, :]
    c[:, C_ID:C_ID + P] = r == k
    c[:, C_BD:C_BD + P] = r // 64 == k // 64
    c[:, C_ONE:C_ONE + P] = 1
    kj = np.arange(2 * P)[None, :]
    local = (kj <= r + P) & (r + P - kj < P)
    c[:, C_ATT:C_ATT + 256] = np.where(local & (kj >= P), 0, NEG)
    c[:, C_ATT + 256:C_ATT + 512] = np.where(local, 0, NEG)
    c[:, C_AM:C_AM + P] = k > r
    c[:, C_AM + P:C_AM + 2 * P] = k >= r
    for lv in range(LEVELS):
        s = 2 ** lv
        low = (r // s % 2 == 1) & (k // s == r // s - 1)
        c[:, C_LV + 2 * lv * P:C_LV + (2 * lv + 1) * P] = low
        c[:, C_LV + (2 * lv + 1) * P:C_LV + (2 * lv + 2) * P] = low.T
    return c


class Block:

    def __init__(self, name, c, i=0):
        at = BASE[name] + c
        self.slot = at % 2
        self.before = i * PER[name] + at
        self.loads = i * (PER[name] // 2) + at // 2 - STREAM_START // 2


def build(nc, a, out):
    ctx = ExitStack()
    with ctx:
        def sb(name, shape, dt=F32):
            return ctx.enter_context(nc.sbuf_tensor(name, shape, dt))

        def sem(name):
            return ctx.enter_context(nc.semaphore(name))

        def dram(name, rows):
            return nc.dram_tensor(name, (rows, T), F32, kind="Internal").ap()

        y_a, y_b, y_c, gates = dram("y_a", LRU_W), dram("y_b", RW_W), dram("y_c", D), dram("gates_sig", 3 * D)

        x_hi = sb("x_hi", [P, KT, T], F32R)
        x_lo = sb("x_lo", [P, KT, T], F32R)
        w_raw = sb("w_raw", [P, 2, 1024])
        w_hi = sb("w_hi", [P, 2, 1024], F32R)
        w_lo = sb("w_lo", [P, 2, 1024], F32R)
        hid_hi = sb("hid_hi", [P, 2, T], F32R)
        hid_lo = sb("hid_lo", [P, 2, T], F32R)
        keep = sb("keep", [P, C_KEEP])
        rw_par = sb("rw_par", [P, P])
        lru_par = sb("lru_par", [P, P])
        mod = sb("mod", [P, 56])
        small = sb("small", [P, 96])
        c_hi = sb("c_hi", [P, KT, 2], F32R)
        c_lo = sb("c_lo", [P, KT, 2], F32R)
        ARENA = 25100
        arena = sb("arena", [P, ARENA])
        ps = ctx.enter_context(nc.psum_tensor("ps", [P, 8, 512], F32))

        ident = keep[:, C_ID:C_ID + P]
        headsum = keep[:, C_BD:C_BD + P]
        ones = keep[:, C_ONE:C_ONE + P]

        def carve(sizes):
            at, got = 0, {}
            for name, n in sizes:
                got[name] = arena[:, at:at + n]
                at += n
            assert at <= ARENA, at
            return got

        def pair_of(slot):
            return ps[:, 2 * slot:2 * slot + 2, :]

        def halves(ap):
            return ap.rearrange("p (h n) -> p h n", h=2)

        s_const = sem("constants_loaded")
        s_par = sem("parameters_loaded")
        s_w = [sem("weights_loaded_0"), sem("weights_loaded_1")]
        s_whi = sem("weights_high_part")
        s_wsplit = sem("weights_split")
        s_dense = sem("dense_done")

        s_yb, s_gst, s_ya, s_yc = (sem(n) for n in ("y_b_stored", "gate_stored", "y_a_stored", "y_c_stored"))
        stream_sems = [s_dense, s_whi, s_wsplit]
        engine_sems = {"pe": [s_dense], "act": [s_yb, s_gst, s_ya, s_yc], "dve": [], "pool": [s_whi, s_wsplit]}

        def made_by(engine, *names):
            got = [sem(n) for n in names]
            engine_sems[engine] += got
            return got if len(got) > 1 else got[0]

        s_x = sem("x_loaded")
        p0_pe, p0_act, p0_dve = made_by("pe", "start_pe"), made_by("act", "start_act"), made_by("dve", "start_dve")
        ada_out = made_by("dve", "mod_column_ready")
        ada_fix = made_by("dve", "mod_scales_ready")
        h_pe, h_tmp, h_hi, h_lo = made_by("pe", "xnT_done"), made_by("dve", "h_ready"), made_by("act", "h_high"), made_by("dve", "h_low")

        passed = {"SP": sem("sp_waits_passed"), "Pool": sem("pool_waits_passed"), "DVE": sem("dve_waits_passed")}

        def wait_alone(eng):
            eng.sem_inc(passed[eng.engine.name], 1)

        def upto(n):
            return max(n, 0) + 1 if isinstance(n, int) else n + 1

        def seed(eng, name):
            for s in engine_sems[name]:
                eng.sem_inc(s, 1 + STREAM_START if s in stream_sems else 1)

        def load_block(sp, blk, src, width):
            n = src.shape[1] * width
            dst = w_raw[:, blk.slot, 0:n].rearrange("p (k m) -> p k m", m=width)
            sp.wait_ge(s_wsplit, upto(blk.before - 1))
            wait_alone(sp)
            sp.dma_start(dst, src).then_inc(s_w[blk.slot], 16)

        def split_block(pool, blk, n):
            raw, hi, lo = (t[:, blk.slot, 0:n] for t in (w_raw, w_hi, w_lo))
            pool.wait_ge(s_w[blk.slot], blk.loads * 16 + 16)
            pool.wait_ge(s_dense, upto(blk.before - 1))
            wait_alone(pool)
            nc.gpsimd.tensor_copy(hi, raw).then_inc(s_whi, 1)
            pool.wait_ge(s_whi, upto(blk.before + 1))
            nc.gpsimd.tensor_tensor(lo, raw, hi.bitcast(F32), ALU.subtract).then_inc(s_wsplit, 1)

        def three_passes(dst, w, x, first, last):
            (wh, wl), (xh, xl) = w, x
            n = len(dst)
            for m, (wp, xp) in enumerate(((wh, xh), (wh, xl), (wl, xh))):
                for h in range(n):
                    ins = nc.tensor.matmul(dst[h], wp, xp[h], start=first and m == 0, stop=last and m == 2)
            return ins

        def dense(pe, blk, width=P, tiles=KT, rows=None):
            pe.wait_ge(s_wsplit, upto(blk.before + 1))
            dst = [ps[0:width, 2 * blk.slot + h, :] for h in range(2)]
            for k in range(tiles):
                w = [t[:, blk.slot, k * width:(k + 1) * width] for t in (w_hi, w_lo)]
                x = [[t[:, k, h * 512:(h + 1) * 512] for h in range(2)] for t in (x_hi, x_lo)]
                ins = three_passes(dst, w, x, k == 0, k == tiles - 1)
            ins.then_inc(s_dense, 1)

        def cols(w, c0, n):
            return w[:, bass.ds(c0, n)].rearrange("(k p) m -> p k m", p=P)

        st0 = carve([("row_rw", P), ("row_lru", P), ("row_mod", P), ("xs", 8 * D), ("tmp", 2 * T), ("sq", 2 * D)])
        row_rw, row_lru, row_mod = st0["row_rw"], st0["row_lru"], st0["row_mod"]
        xs = st0["xs"].rearrange("p (t d) -> p t d", t=8)
        h_tmpb = st0["tmp"].rearrange("p (s n) -> p s n", s=2)
        sq0 = st0["sq"].rearrange("p (s n) -> p s n", s=2)
        sumsq, rstd = small[:, 0:8], small[:, 8:16]
        sinks_b = small[:, 16:32]
        gains = small[:, 32:34]
        rate, rate2 = small[:, 34:50], small[:, 50:66]

        def load_parameters(sp):
            for src, dst in (("rw_w0", PR_W0), ("rw_a0", PR_A0), ("rw_kk", PR_KK), ("rw_ka", PR_KA), ("rw_rk", PR_RK),
                             ("rw_ln_w", PR_LNW), ("rw_ln_b", PR_LNB)):
                sp.dma_start(row_rw[dst:dst + 8, :], a[src][0].rearrange("(t p) -> t p", p=P)).then_inc(s_par, 16)
            mu = a["rw_mu"][0]
            sp.dma_start(row_rw[PR_MU:PR_MU_G1, :], mu[0:26 * P].rearrange("(t p) -> t p", p=P)).then_inc(s_par, 16)
            sp.dma_start(row_rw[PR_MU_G1:PR_ROWS, 0:32], mu[26 * P:26 * P + 32].rearrange("(t p) -> t p", t=1)).then_inc(s_par, 16)
            sp.dma_start(row_lru[0:64, 0:80], a["conv_w"][0].rearrange("j (b n) -> (j b) n", n=80)).then_inc(s_par, 16)
            for src, dst in (("conv_b", LP_CB), ("lru_ba", LP_BA), ("lru_bx", LP_BX), ("lru_lambda", LP_LAM)):
                sp.dma_start(row_lru[dst:dst + 16, 0:80], a[src][0].rearrange("(b n) -> b n", n=80)).then_inc(s_par, 16)
            sp.dma_start(row_mod[0:48, :], a["b_ada"][0].rearrange("(t p) -> t p", p=P)).then_inc(s_par, 16)
            sp.dma_start(row_mod[48:56, :], a["c"][0].rearrange("(t p) -> t p", p=P)).then_inc(s_par, 16)
            sp.dma_start(sinks_b, a["sinks"].broadcast_to([P, 16])).then_inc(s_par, 16)

        gain_sem = sem("gains_loaded")

        def load_gains(sp):
            for col, name in ((0, "q_gain"), (1, "k_gain")):
                for h in range(2):
                    sp.dma_start(gains[64 * h:64 * h + 64, col:col + 1], a[name].rearrange("a (n o) -> n (a o)", o=1)).then_inc(gain_sem, 16)

        rw = carve([("wa", T), ("g0", T), ("g1", T), ("xp", T + 8), ("A", T), ("t1", T), ("t2", T), ("sig", T), ("L", T),
                    ("ar", 2 * T), ("bn", T), ("kt", T), ("v", T), ("bv", T), ("g", T), ("gs", T),
                    ("lw", P), ("lg0", P), ("lg1", P), ("S", 2 * P), ("df", 16), ("ff", 8),
                    ("am", 2 * 1024), ("xx", 2 * 512), ("y1", 2 * 256), ("tk", 2 * 512), ("R", 2 * 256),
                    ("uw", 2 * 256), ("gt", 2 * 128), ("q", 2 * 128)])
        ar = rw["ar"].rearrange("p (c s n) -> p c s n", c=CHUNKS, s=2)
        al_v, rt_v = ar[:, :, 0, :], ar[:, :, 1, :]
        chunked = lambda ap: ap.rearrange("p (c n) -> p c n", c=CHUNKS)
        am = rw["am"].rearrange("p (s h q n) -> p s h q n", s=2, h=2, q=4)
        xx = rw["xx"].rearrange("p (s o h n) -> p s o h n", s=2, o=2, h=2)
        y1 = rw["y1"].rearrange("p (s h n) -> p s h n", s=2, h=2)
        tk = rw["tk"].rearrange("p (s q n) -> p s q n", s=2, q=4)
        RR = rw["R"].rearrange("p (s h n) -> p s h n", s=2, h=2)
        uw = rw["uw"].rearrange("p (s h n) -> p s h n", s=2, h=2)
        gt = rw["gt"].rearrange("p (s n) -> p s n", s=2)
        qq = rw["q"].rearrange("p (s n) -> p s n", s=2)
        SS = rw["S"].rearrange("p (s n) -> p s n", s=2)
        masks = hid_hi[:, :, :].rearrange("p a n -> p (a n)")
        am_mask = masks[:, 0:256]
        lv_mask = hid_lo[:, :, :].rearrange("p a n -> p (a n)")[:, 0:2 * LEVELS * P]
        s_mask, s_lw = sem("masks_loaded"), sem("lora_weights_loaded")
        mask_ready = made_by("dve", "masks_ready")
        (r_lwa, r_kks, r_g, r_bon, r_mean, r_var) = made_by("pe", "rw_lora_done", "rw_kk_sums", "rw_g_done", "rw_bonus_sums", "rw_mean_done", "rw_var_done")
        (r_tk, r_am, r_y1, r_xu, r_ak, r_uw, r_gq, r_s, r_y) = made_by(
            "pe", "tokens_major_done", "pair_products_done", "level_product_done", "level_update_done", "ak_v_done",
            "solve_done", "g_q_done", "state_done", "y_chunk_done")
        (a_xp, a_sa, a_sqk, a_gate, a_rk, a_g, a_exp, a_f, a_wa) = made_by(
            "act", "rw_stream_copied", "rw_sigmoids_ready", "rw_kk_squared", "gate_ready", "rw_kk_root", "rw_g_ready",
            "rw_exponentials", "rw_state_scale", "rw_lora_in_ready")
        (a_tk, a_xi, a_y1, a_ak, a_uw, a_y, a_ysq, a_yr) = made_by(
            "act", "tokens_major_ready", "inverse_started", "level_product_ready", "ak_v_ready", "solve_ready", "y_chunk_ready",
            "y_squared", "y_root")
        (v_mix, v_kk, v_c, v_fin, v_am, v_x0, v_xu, v_gt, v_q, v_s, v_post, v_zero, v_lora) = made_by(
            "dve", "rw_stream_mixed", "rw_kk_ready", "rw_prep", "rw_bonus_ready", "pair_products_ready", "level0_ready",
            "level_ready", "g_ready", "q_ready", "state_ready", "rw_post", "rw_zeroed", "lora_mixed")

        lr = carve([("xp", T + 8), ("xa", T), ("ga", T), ("gx", T), ("aa", T), ("a2", T), ("h", T), ("gy", T), ("ya", T),
                    ("wa", 2 * LRU_BLK), ("wx", 2 * LRU_BLK)])
        l_x, l_sa, l_rt, l_gy, l_exp = made_by("act", "lru_x_copied", "lru_gates_ready", "lru_root_ready", "lru_gelu_ready", "lru_decay_ready")
        l_pe = made_by("pe", "lru_gates_done")
        l_cv, l_sq, l_u, l_out, l_z = made_by("dve", "conv_steps", "decay_squared", "lru_input_steps", "lru_out_steps", "lru_zeroed")
        s_lw2 = [sem("lru_gate_weights_loaded_0"), sem("lru_gate_weights_loaded_1")]

        at_ = carve([("k", 2 * (T + P)), ("v", 2 * 9 * HEAD), ("kvt", T), ("t1", T), ("t2", T), ("q", 2 * T), ("yc", 2 * T),
                     ("mask", 512), ("s", 4 * 512), ("pT", 4 * 512), ("sm", 64)])
        ak = at_["k"].rearrange("p (g n) -> p g n", g=2)
        av = at_["v"].rearrange("p (g b d) -> p g b d", g=2, b=9)
        aq = at_["q"].rearrange("p (t n) -> p t n", t=2)
        ayc = at_["yc"].rearrange("p (t n) -> p t n", t=2)
        asc = at_["s"].rearrange("p (u h n) -> p u h n", u=4, h=2)
        apt = at_["pT"].rearrange("p (u m) -> p u m", u=4)
        asm = at_["sm"].rearrange("p (u m) -> p u m", u=4)
        s_am, s_kfirst = sem("attention_masks_loaded"), sem("k_half_loaded")
        t_ns, t_vt, t_sc, t_pt, t_o = made_by("pe", "norm_sums_done", "v_transposed", "scores_done", "probs_transposed", "attention_out_done")
        t_cp, t_sq, t_rt, t_v, t_e, t_ptc, t_oc, t_k2 = made_by(
            "act", "kv_copied", "head_squares", "head_root", "v_ready", "exp_done", "probs_t_ready", "attention_out_ready", "k_second_half")
        t_rc, t_n, t_d, t_m, t_p, t_z, t_dc = made_by("dve", "head_rsqrt", "head_normed", "softmax_steps", "neg_max_ready", "probs_ready", "att_zeroed", "denominator_steps")

        mg = carve([("x2", KT * T), ("mix", KT * T), ("yraw", 2 * T), ("gt", 2 * T), ("t", 2 * T)])
        x2 = mg["x2"].rearrange("p (k n) -> p k n", k=KT)
        mix = mg["mix"].rearrange("p (k n) -> p k n", k=KT)
        yraw = mg["yraw"].rearrange("p (s n) -> p s n", s=2)
        gtl = mg["gt"].rearrange("p (s n) -> p s n", s=2)
        mt = mg["t"].rearrange("p (s n) -> p s n", s=2)
        s_y = [sem("y_tile_loaded_0"), sem("y_tile_loaded_1")]
        s_g = [sem("gate_tile_loaded_0"), sem("gate_tile_loaded_1")]
        s_x2, s_out = sem("x_loaded_again"), sem("out_stored")
        m_hi, m_cp, m_sq, m_rt, m_sil, m_hh, m_o = made_by("act", "operand_high", "lru_part_ready", "x2_squared", "x2_root", "silu_ready", "hidden_high", "out_copied")
        m_lo, m_ev, m_xt, m_res, m_n, m_nh, m_act, m_hl, m_dn = made_by(
            "dve", "operand_low", "merge_steps", "xT_ready", "residual_ready", "x2_rstd", "h2_steps", "hidden_ready", "hidden_low", "down_added")
        m_pe, m_ss, m_dd, m_op = made_by("pe", "xT_done", "x2_sums_done", "down_done", "out_transposed")

        BR = [("oa1", 5, "w_lru_o", 0, y_a, 0), ("oa2", 5, "w_lru_o", 640, y_a, 0), ("oc", 8, "w_att_o", 0, y_c, 2), ("ob", 8, "w_rw_o", 0, y_b, 1)]
        YB0, _n = {}, 0
        for nm, kts, *_ in BR:
            YB0[nm] = _n
            _n += kts
        NY = _n

        lam_s = made_by("dve", "lambda_steps")
        bias_t = sb("bias_t", [P, 4])
        eps_qk, eps_rms, eps_ln, one_b = bias_t[:, 0:1], bias_t[:, 0:1], bias_t[:, 1:2], bias_t[:, 2:3]
        lsc = sb("lsc", [P, 32])
        SOFT = 5 + 16 + 5 + 3
        VC = 24
        VZ = 2
        XP0, XM0 = 3, 6
        N_PAR_DMA = 7 + 2 + 1 + 4 + 2 + 1
        nsinks = sb("nsinks", [P, 16])

        def nsink(gg, t):
            return nsinks[:, bass.ds(gg * 4 + 2 * t, 2)]

        def halves2(ap):
            return ap.rearrange("p o (h n) -> p (o h) n", h=2)

        def lv_count(i, cc, lv, s):
            return i * (4 * 2 * (LEVELS - 1)) + (cc * (LEVELS - 1) + lv - 1) * 2 + s

        def xu_count(i, cc, lv, s):
            last = LEVELS - 1
            turn = 2 * (2 * (LEVELS - 2) + 1)
            return i * (4 * turn) + cc * turn + ((lv - 1) * 4 + 2 * s if lv < last else (last - 1) * 4 + s)

        blockctx = ctx.enter_context(nc.Block())

        @blockctx.sync
        def _(sp):
            sp.dma_start(keep[:, :], a["consts"][:, 0:C_KEEP]).then_inc(s_const, 16)
            sp.wait_ge(p0_dve, upto(3))
            load_parameters(sp)
            for t in range(8):
                sp.dma_start(xs[:, t, :], a["x"][0, t * P:(t + 1) * P, :]).then_inc(s_x, 16)
            load_gains(sp)
            w_in, w_ada = a["w_in"][0], a["w_ada"][0]

            def ada(name, first):
                with sp.Fori(0, TURNS[name]) as i:
                    for c in range(2):
                        load_block(sp, Block(name, c, i), cols(w_ada, (first + c) * P + i * (2 * P), P), P)
            ada("ada1", 0)
            sp.wait_ge(h_lo, upto(KT))
            sp.dma_start(rw["ar"][:, 0:2 * LEVELS * P], a["consts"][:, C_LV:C_N]).then_inc(s_mask, 16)
            sp.dma_start(rw["bn"][:, 0:256], a["consts"][:, C_AM:C_AM + 256]).then_inc(s_mask, 16)
            for c, (c0, n) in enumerate(((0, P), (P, P), (2 * P, 32))):
                load_block(sp, Block("lora", c), cols(w_in, COL_LORA + c0, n), n)
            w2, a2, g2 = a["rw_w2"][0], a["rw_a2"][0], a["rw_g2"][0]
            with sp.Fori(0, PAIRS) as i:
                for c in range(3):
                    load_block(sp, Block("rwkv", c, i), cols(w_in, COL_RW + c * RW_W + i * P, P), P)
                sp.wait_ge(r_g, upto(i))
                wait_alone(sp)
                sp.dma_start(rw["lw"][0:64, :], w2[:, bass.ds(i * P, P)]).then_inc(s_lw, 16)
                sp.dma_start(rw["lw"][64:128, :], a2[:, bass.ds(i * P, P)]).then_inc(s_lw, 16)
                sp.dma_start(rw["lg0"], g2[0:P, bass.ds(i * P, P)]).then_inc(s_lw, 16)
                sp.dma_start(rw["lg1"][0:32, :], g2[P:160, bass.ds(i * P, P)]).then_inc(s_lw, 16)
                for c in range(3):
                    load_block(sp, Block("rwkv", 3 + c, i), cols(w_in, COL_G + c * D + i * P, P), P)
            sp.wait_ge(v_post, upto(PAIRS * 6))
            sp.wait_ge(s_yb, upto(PAIRS * 16))
            sp.wait_ge(s_gst, upto(PAIRS * 48))
            with sp.Fori(0, TURNS["lru"]) as i:
                for u in range(2):
                    for c, c0 in enumerate((COL_LX, COL_LY)):
                        load_block(sp, Block("lru", 2 * u + c, i), cols(w_in, c0 + u * 80 + i * 160, 80), 80)
                    sp.wait_ge(l_pe, upto(i * 2))
                    wait_alone(sp)
                    for nm, dst in (("lru_wa", lr["wa"]), ("lru_wx", lr["wx"])):
                        sp.dma_start(dst[0:80, 80 * u:80 * u + 80], a[nm][0, bass.ds(i * 2 + u, 1)].rearrange("o n m -> (o n) m")).then_inc(s_lw2[u], 16)
            sp.wait_ge(l_out, upto(LRU_N))
            sp.wait_ge(s_ya, upto(LRU_N * 16))
            sp.dma_start(at_["mask"], a["consts"][:, C_ATT:C_ATT + 512]).then_inc(s_am, 16)
            with sp.Fori(0, 2) as i:
                for g in range(2):
                    b = Block("att", 3 * g, i)
                    n = KT * P
                    dst = w_raw[:, b.slot, 0:n].rearrange("p (k s m) -> p k s m", k=KT, s=2)
                    sp.wait_ge(s_wsplit, upto(b.before - 1))
                    wait_alone(sp)
                    for s in range(2):
                        src = w_in[:, bass.ds(COL_K + 256 * s + 64 * g + i * 128, 64)].rearrange("(k p) m -> p k m", p=P)
                        sp.dma_start(dst[:, :, s, :], src).then_inc(s_w[b.slot] if s else s_kfirst, 16)
                    for t in range(2):
                        load_block(sp, Block("att", 3 * g + 1 + t, i), cols(w_in, COL_Q + 256 * g + P * t + i * 512, P), P)
            ada("ada2", 16)
            sp.wait_ge(s_yc, upto(8 * 16))
            yn, gn = 0, 0
            for nm, kts, wname, row0, y, gi in BR:
                for k in range(kts):
                    sp.wait_ge(m_lo, upto(yn - 1))
                    sp.dma_start(yraw[:, yn % 2, :], y[row0 + k * P:row0 + (k + 1) * P, :]).then_inc(s_y[yn % 2], 16)
                    yn += 1
                wv = a[wname][0][row0:row0 + kts * P, :]
                with sp.Fori(0, 4) as i:
                    for c in range(2):
                        load_block(sp, Block(nm, c, i), cols(wv, c * P + i * 2 * P, P), P)
                        if nm != "oa1":
                            sp.wait_ge(m_ev, upto(2 * (gn + c) + i * 4))
                            wait_alone(sp)
                            sp.dma_start(gtl[:, c, :], gates[bass.ds(gi * D + c * P + i * 2 * P, P), :]).then_inc(s_g[c], 16)
                if nm != "oa1":
                    gn += 8
            sp.wait_ge(m_lo, upto(NY + KT))
            for t in range(8):
                sp.dma_start(mix[:, t, :], a["x"][0, t * P:(t + 1) * P, :]).then_inc(s_x2, 16)
            with sp.Fori(0, TURNS["wout"]) as i:
                for c in range(2):
                    load_block(sp, Block("wout", c, i), cols(a["w_out"][0], c * P + i * 2 * P, P), P)
            wf, wo = a["w_ffn_in"][0], a["w_ffn_out"][0]
            with sp.Fori(0, TURNS["ffn"]) as i:
                for c in range(4):
                    load_block(sp, Block("ffn", c, i), cols(wf, (c % 2) * FF + (c // 2) * P + i * (2 * P), P), P)
                for c in range(2):
                    rows = wo[bass.ds(i * 2 * P, 2 * P), c * 512:(c + 1) * 512].rearrange("(k p) m -> p k m", p=P)
                    load_block(sp, Block("ffn", 4 + c, i), rows, 512)
            for t in range(8):
                sp.wait_ge(m_o, upto(t + 1))
                sp.dma_start(out[0, t * P:(t + 1) * P, :], mix[:, t, :]).then_inc(s_out, 16)
            sp.wait_ge(s_out, 8 * 16)

        @blockctx.gpsimd
        def _(pool):
            seed(pool, "pool")

            def split_turns(name, sizes):
                with pool.Fori(0, TURNS[name]) as i:
                    for c, n in enumerate(sizes):
                        split_block(pool, Block(name, c, i), n)
            split_turns("ada1", [1024] * 2)
            for c, n in enumerate((1024, 1024, 256)):
                split_block(pool, Block("lora", c), n)
            split_turns("rwkv", [1024] * 6)
            split_turns("lru", [640] * 4)
            with pool.Fori(0, TURNS["att"]) as i:
                for c in range(6):
                    if c % 3 == 0:
                        pool.wait_ge(s_kfirst, i * 32 + (c // 3 + 1) * 16)
                    split_block(pool, Block("att", c, i), 1024)
            split_turns("ada2", [1024] * 2)
            for nm, kts, *_ in BR:
                split_turns(nm, [kts * P] * 2)
            split_turns("wout", [1024] * 2)
            split_turns("ffn", [1024] * 6)

        @blockctx.tensor
        def _(pe):
            mm = nc.tensor.matmul
            seed(pe, "pe")

            pe.wait_ge(s_const, 16)
            pe.wait_ge(p0_dve, upto(3))
            pe.wait_ge(s_par, N_PAR_DMA * 16)
            for k, row in enumerate((row_rw, row_lru, row_mod)):
                pe.transpose(ps[:, 4 + k, 0:P], row, ident).then_inc(p0_pe, 1)
            pe.wait_ge(p0_dve, upto(3 + 3 + 2))

            def ada_turns(name, evacuated):
                with pe.Fori(0, TURNS[name]) as i:
                    for c in range(2):
                        b = Block(name, c, i)
                        pe.wait_ge(s_wsplit, upto(b.before + 1))
                        pe.wait_ge(ada_out, upto(evacuated + i * 2))
                        for k in range(KT):
                            for m, (w, x) in enumerate(((w_hi, c_hi), (w_hi, c_lo), (w_lo, c_hi))):
                                ins = mm(ps[:, 6 + c, 0:2], w[:, b.slot, k * P:(k + 1) * P], x[:, k, :],
                                         start=k == 0 and m == 0, stop=k == KT - 1 and m == 2)
                        ins.then_inc(s_dense, 1)
            pe.wait_ge(p0_dve, upto(3 + 3))
            ada_turns("ada1", 0)
            for k in range(KT):
                if k == 0:
                    pe.wait_ge(p0_dve, upto(18))
                if k >= 2:
                    pe.wait_ge(h_tmp, upto(k - 1))
                for t in range(8):
                    ins = pe.transpose(ps[:, 2 * (k % 2) + t // 4, (t % 4) * P:(t % 4 + 1) * P], xs[:, t, k * P:(k + 1) * P], ident)
                ins.then_inc(h_pe, 1)

            pe.wait_ge(h_lo, upto(KT))
            dense(pe, Block("lora", 0))
            dense(pe, Block("lora", 1))
            pe.wait_ge(a_xp, upto(1))
            dense(pe, Block("lora", 2), width=32)
            pe.wait_ge(a_wa, upto(3))

            def sums(dst_bank, lhs, x):
                for h in range(2):
                    ins = mm(ps[:, dst_bank + h, :], lhs, x[:, h * 512:(h + 1) * 512], start=True, stop=True)
                return ins

            with pe.Fori(0, PAIRS) as i:
                pe.wait_ge(a_y, upto(i * 8))
                pe.wait_ge(v_s, upto(i * 8))
                pe.wait_ge(v_post, upto(i * 6))
                dense(pe, Block("rwkv", 0, i))
                dense(pe, Block("rwkv", 1, i))
                pe.wait_ge(a_xp, upto(XP0 + i * 3 + 1))
                dense(pe, Block("rwkv", 2, i))
                pe.wait_ge(s_lw, i * 64 + 64)
                for h in range(2):
                    hs = slice(h * 512, (h + 1) * 512)
                    mm(ps[:, 4 + h, :], rw["lw"][0:64, :], rw["wa"][0:64, hs], start=True, stop=True)
                    ins = mm(ps[:, 6 + h, :], rw["lw"][64:128, :], rw["wa"][64:128, hs], start=True, stop=True)
                ins.then_inc(r_lwa, 1)
                pe.wait_ge(a_xp, upto(XP0 + i * 3 + 2))
                dense(pe, Block("rwkv", 3, i))
                pe.wait_ge(a_sa, upto(i * 2 + 1))
                pe.wait_ge(a_sqk, upto(i + 1))
                sums(4, headsum, rw["t2"]).then_inc(r_kks, 1)
                pe.wait_ge(a_xp, upto(XP0 + i * 3 + 3))
                dense(pe, Block("rwkv", 4, i))
                pe.wait_ge(a_sa, upto(i * 2 + 2))
                for h in range(2):
                    hs = slice(h * 512, (h + 1) * 512)
                    mm(ps[:, 6 + h, :], rw["lg0"], rw["g0"][:, hs], start=True, stop=False)
                    ins = mm(ps[:, 6 + h, :], rw["lg1"][0:32, :], rw["g1"][0:32, hs], start=False, stop=True)
                ins.then_inc(r_g, 1)
                pe.wait_ge(a_gate, upto(i * 3 + 1))
                dense(pe, Block("rwkv", 5, i))
                pe.wait_ge(a_rk, upto(i + 1))
                pe.wait_ge(v_c, upto(i * VC + 7))
                sums(4, headsum, rw["t1"]).then_inc(r_bon, 1)
                pe.wait_ge(v_c, upto(i * VC + VC))
                pe.wait_ge(v_fin, upto(i + 1))
                pe.wait_ge(a_g, upto(i + 1))
                pe.wait_ge(a_gate, upto(i * 3 + 3))
                for cc in range(CHUNKS // 2):
                    two = [(2 * cc + s, s, 4 * (1 - s)) for s in range(2)]
                    for c, s, b0 in two:
                        if c >= 2:
                            pe.wait_ge(a_y, upto(i * 8 + c - 1))
                            pe.wait_ge(v_s, upto(i * 8 + c - 1))
                        tok = slice(c * P, (c + 1) * P)
                        for q, src in enumerate((rw["v"][:, tok], al_v[:, c, :], rw["bn"][:, tok], rw["kt"][:, tok])):
                            ins = pe.transpose(ps[:, b0 + 2, q * P:(q + 1) * P], src, ident)
                        ins.then_inc(r_tk, 1)
                    for c, s, b0 in two:
                        tok = slice(c * P, (c + 1) * P)
                        for h in range(2):
                            hp = slice(64 * h, 64 * h + 64)
                            mm(ps[:, b0 + h, 0:256], rw["bn"][hp, tok], ar[hp, c, :, :], start=True, stop=True)
                            mm(ps[:, b0 + h, 256:512], rw["kt"][hp, tok], ar[hp, c, :, :], start=True, stop=True)
                        pe.wait_ge(a_tk, upto((i * 8 + c) * 2 + 2))
                        for h in range(2):
                            hp = slice(64 * h, 64 * h + 64)
                            ins = mm(ps[:, b0 + 2 + h, 0:P], al_v[hp, c, :], rw["bn"][hp, tok], start=True, stop=True)
                        ins.then_inc(r_am, 1)
                    for c, s, b0 in two:
                        pe.wait_ge(v_x0, upto((i * 8 + c) * 2 + 2))
                        for h in range(2):
                            ins = mm(ps[:, b0 + 3, h * 64:(h + 1) * 64], am[:, s, h, 2, :], tk[:, s, 0, 64 * h:64 * h + 64], start=True, stop=True)
                        ins.then_inc(r_ak, 1)
                    for lv in range(1, LEVELS):
                        for c, s, b0 in two:
                            if lv > 1:
                                pe.wait_ge(v_xu, upto(xu_count(i, cc, lv - 1, s) + 2))
                            for h in range(2):
                                ins = mm(ps[:, b0 + 2, h * P:(h + 1) * P], am[:, s, h, 0, :], xx[:, s, 0, h, :], start=True, stop=True)
                            ins.then_inc(r_y1, 1)
                        for c, s, b0 in two:
                            pe.wait_ge(a_y1, upto(lv_count(i, cc, lv, s) + 1))
                            for h in range(2):
                                if lv < LEVELS - 1:
                                    mm(ps[:, b0, h * P:(h + 1) * P], xx[:, s, 1, h, :], y1[:, s, h, :], start=True, stop=True)
                            for h in range(2):
                                ins = mm(ps[:, b0 + 1, h * P:(h + 1) * P], y1[:, s, h, :], xx[:, s, 1, h, :], start=True, stop=True)
                            ins.then_inc(r_xu, 1)
                    for c, s, b0 in two:
                        pe.wait_ge(v_xu, upto(xu_count(i, cc, LEVELS - 1, s) + 1))
                        pe.wait_ge(a_ak, upto(i * 8 + c + 1))
                        for h in range(2):
                            ins = mm(ps[:, b0 + 2, h * P:(h + 1) * P], xx[:, s, 1, h, :], RR[:, s, h, :], start=True, stop=True)
                        ins.then_inc(r_uw, 1)
                    for c, s, b0 in two:
                        pe.wait_ge(a_uw, upto(i * 8 + c + 1))
                        for h in range(2):
                            hp = slice(64 * h, 64 * h + 64)
                            mm(ps[hp, b0, 0:P], uw[:, s, h, 64:128], am[:, s, h, 1, :], start=True, stop=True)
                        for h in range(2):
                            hp = slice(64 * h, 64 * h + 64)
                            ins = mm(ps[hp, b0 + 1, hp], uw[:, s, h, 64:128], tk[:, s, 2, hp], start=True, stop=True)
                        ins.then_inc(r_gq, 1)
                    for c, s, b0 in two:
                        pe.wait_ge(v_q, upto((i * 8 + c) * 2 + 2))
                        if c == 0:
                            pe.wait_ge(v_zero, upto(VZ + i + 1))
                        else:
                            pe.wait_ge(v_s, upto(i * 8 + c))
                        mm(ps[:, b0 + 3, 0:P], qq[:, s, :], SS[:, c % 2, :], start=True, stop=False)
                        for h in range(2):
                            hp = slice(64 * h, 64 * h + 64)
                            mm(ps[hp, b0 + 3, hp], tk[:, s, 2, hp], uw[:, s, h, 0:64], start=False, stop=False)
                            ins = mm(ps[hp, b0 + 3, hp], tk[:, s, 3, hp], tk[:, s, 0, hp], start=False, stop=True)
                        ins.then_inc(r_s, 1)
                        mm(ps[:, b0 + 2, 0:P], SS[:, c % 2, :], gt[:, s, :], start=True, stop=False)
                        for h in range(2):
                            hp = slice(64 * h, 64 * h + 64)
                            mm(ps[hp, b0 + 2, 0:P], uw[:, s, h, 0:64], am[:, s, h, 1, :], start=False, stop=False)
                            ins = mm(ps[hp, b0 + 2, 0:P], tk[:, s, 0, hp], am[:, s, h, 3, :], start=False, stop=True)
                        ins.then_inc(r_y, 1)
                pe.wait_ge(a_y, upto(i * 8 + 8))
                pe.wait_ge(v_s, upto(i * 8 + 8))
                sums(4, headsum, rw["A"]).then_inc(r_mean, 1)
                pe.wait_ge(a_ysq, upto(i + 1))
                sums(6, headsum, rw["t1"]).then_inc(r_var, 1)

            pe.wait_ge(v_post, upto(PAIRS * 6))
            with pe.Fori(0, TURNS["lru"]) as i:
                for u in range(2):
                    n = i * 2 + u
                    pe.wait_ge(l_x, upto(n))
                    dense(pe, Block("lru", 2 * u, i), width=80)
                    pe.wait_ge(l_gy, upto(n))
                    dense(pe, Block("lru", 2 * u + 1, i), width=80)
                    pe.wait_ge(l_cv, upto(n * 4 + 4))
                    pe.wait_ge(l_sa, upto(n * 2))
                    pe.wait_ge(s_lw2[u], i * 32 + 32)
                    for q, w in enumerate(("wa", "wx")):
                        for h in range(2):
                            ins = mm(ps[0:80, 4 + 2 * q + h, :], lr[w][0:80, 80 * u:80 * u + 80], lr["xa"][0:80, h * 512:(h + 1) * 512], start=True, stop=True)
                    ins.then_inc(l_pe, 1)

            pe.wait_ge(l_out, upto(LRU_N))
            with pe.Fori(0, TURNS["att"]) as i:
                for g in range(2):
                    gg = i * 2 + g
                    for c in range(3):
                        pe.wait_ge(t_cp, upto(gg * 3 + c))
                        if c == 0:
                            pe.wait_ge(t_oc, upto(gg * 16))
                        dense(pe, Block("att", 3 * g + c, i))
                        if c == 0:
                            pe.wait_ge(t_cp, upto(gg * 3 + 1))
                            for n in range(8):
                                ins = pe.transpose(ps[:, 6 + n // 4, (n % 4) * P:(n % 4 + 1) * P], at_["kvt"][:, n * P:(n + 1) * P], ident)
                            ins.then_inc(t_vt, 1)
                        if c > 0:
                            pe.wait_ge(t_sq, upto(gg * 3 + c))
                            pe.wait_ge(t_rt, upto(gg * 3 + c - 1))
                            sums(4, headsum, at_["t1"]).then_inc(t_ns, 1)
                    pe.wait_ge(t_sq, upto(gg * 3 + 3))
                    pe.wait_ge(t_rt, upto(gg * 3 + 2))
                    sums(4, headsum, at_["t1"]).then_inc(t_ns, 1)
                    pe.wait_ge(t_rt, upto(gg * 3 + 3))
                    pe.wait_ge(t_n, upto(gg * 3 + 3))
                    pe.wait_ge(t_k2, upto(gg + 1))
                    pe.wait_ge(t_v, upto(gg + 1))
                    for tick in range(16 + 3):
                        if tick < 16:
                            u, t, n = tick, tick // 8, tick % 8
                            if u >= 2:
                                pe.wait_ge(t_d, upto((gg * 16 + u - 2) * 4 + 1))
                            for h in range(2):
                                hp = slice(64 * h, 64 * h + 64)
                                ins = mm(ps[:, 4 - 2 * (u % 2) + h, 0:256], aq[hp, t, n * P:(n + 1) * P], ak[hp, g, n * P:n * P + 256], start=True, stop=True)
                            ins.then_inc(t_sc, 1)
                        if 0 <= tick - 2 < 16:
                            u = tick - 2
                            pe.wait_ge(t_p, upto((gg * 16 + u) * 2 + 2))
                            if u >= 2:
                                pe.wait_ge(t_ptc, upto(gg * 16 + u - 1))
                            for h in range(2):
                                for kb in range(2):
                                    ins = pe.transpose(ps[:, 6 + u % 2, (2 * h + kb) * P:(2 * h + kb + 1) * P], asc[:, u % 4, h, kb * P:(kb + 1) * P], ident)
                            ins.then_inc(t_pt, 1)
                        if 0 <= tick - 3 < 16:
                            u, t, n = tick - 3, (tick - 3) // 8, (tick - 3) % 8
                            pe.wait_ge(t_ptc, upto(gg * 16 + u + 1))
                            if u >= 2:
                                pe.wait_ge(t_oc, upto(gg * 16 + u - 1))
                            for h in range(2):
                                hp = slice(64 * h, 64 * h + 64)
                                for kb in range(2):
                                    ins = mm(ps[hp, u % 2, 0:P], av[:, g, n + kb, :], apt[:, u % 4, (2 * h + kb) * P:(2 * h + kb + 1) * P], start=kb == 0, stop=kb == 1)
                            ins.then_inc(t_o, 1)

            pe.wait_ge(t_oc, upto(64))
            pe.wait_ge(t_ptc, upto(64))
            ada_turns("ada2", 16)

            yn, merged = 0, 0
            for nm, kts, *_ in BR:
                yn += kts
                pe.wait_ge(m_lo, upto(yn))
                with pe.Fori(0, 4) as i:
                    for c in range(2):
                        if nm == "oa1":
                            pe.wait_ge(m_cp, upto(i * 2))
                        elif nm == "oa2":
                            pe.wait_ge(m_cp, upto(8))
                            pe.wait_ge(m_ev, upto(i * 4))
                        if nm in ("oc", "ob"):
                            pe.wait_ge(m_ev, upto(merged * 2 + (i * 2 + c) * 2 - 2))
                        dense(pe, Block(nm, c, i), tiles=kts)
                merged += 0 if nm == "oa1" else 8
            pe.wait_ge(m_lo, upto(NY + KT))
            pe.wait_ge(s_x2, 8 * 16)
            for k in range(KT):
                if k >= 2:
                    pe.wait_ge(m_xt, upto(k - 1))
                for t in range(8):
                    ins = pe.transpose(ps[:, 4 + 2 * (k % 2) + t // 4, (t % 4) * P:(t % 4 + 1) * P], mix[:, t, k * P:(k + 1) * P], ident)
                ins.then_inc(m_pe, 1)
            pe.wait_ge(m_ev, upto(48))
            with pe.Fori(0, TURNS["wout"]) as i:
                for c in range(2):
                    pe.wait_ge(m_res, upto(i * 2))
                    dense(pe, Block("wout", c, i))
            for k in range(KT):
                pe.wait_ge(m_sq, upto(k + 1))
                for h in range(2):
                    ins = mm(ps[:, 4 + h, :], ones, mt[:, k % 2, h * 512:(h + 1) * 512], start=k == 0, stop=k == KT - 1)
                ins.then_inc(m_ss, 1)
            pe.wait_ge(m_nh, upto(KT * 3))
            with pe.Fori(0, TURNS["ffn"]) as i:
                for c in range(4):
                    if c == 0:
                        pe.wait_ge(m_dn, upto(i * 8))
                    elif c >= 2:
                        pe.wait_ge(m_sil if c == 2 else m_act, upto(i * 2 + 1))
                    dense(pe, Block("ffn", c, i))
                pe.wait_ge(m_hl, upto(i * 2 + 2))
                for m in range(8):
                    blk = Block("ffn", 4 + m // 4, i)
                    if m % 4 == 0:
                        pe.wait_ge(s_wsplit, upto(blk.before + 1))
                    if m < 2:
                        pe.wait_ge(m_sil, upto(i * 2 + 2))
                        pe.wait_ge(m_act, upto(i * 2 + 2))
                    else:
                        pe.wait_ge(m_dn, upto(i * 8 + m - 1))
                    dst = [ps[:, 2 * (m % 2) + h, :] for h in range(2)]
                    for k in range(FF_GROUP):
                        at = k * 512 + (m % 4) * P
                        w = [t[:, blk.slot, at:at + P] for t in (w_hi, w_lo)]
                        x = [[t[:, k, h * 512:(h + 1) * 512] for h in range(2)] for t in (hid_hi, hid_lo)]
                        ins = three_passes(dst, w, x, k == 0, k == FF_GROUP - 1)
                    ins.then_inc(s_dense if m % 4 == 3 else m_dd, 1)
            pe.wait_ge(m_dn, upto(TURNS["ffn"] * 8))
            for t in range(8):
                if t >= 2:
                    pe.wait_ge(m_o, upto(t - 1))
                for k in range(KT):
                    ins = pe.transpose(ps[:, 4 + 2 * (t % 2) + k // 4, (k % 4) * P:(k % 4 + 1) * P], x2[:, k, t * P:(t + 1) * P], ident)
                ins.then_inc(m_op, 1)

        @blockctx.scalar
        def _(act):
            fn = nc.scalar.activation
            seed(act, "act")
            for t in range(8):
                act.wait_ge(s_x, 16 * 8)
                if t >= 2:
                    act.wait_ge(p0_act, upto(t - 1))
                fn(sq0[:, t % 2, :], xs[:, t, :], ACT.Square, accum_out=sumsq[:, t:t + 1]).then_inc(p0_act, 1)
            act.wait_ge(p0_dve, upto(6))
            fn(mod[:, 48:56], mod[:, 48:56], ACT.Silu).then_inc(p0_act, 1)
            fn(rate2[0:80, :], rate[0:80, :], ACT.Exp, scale=-1.0).then_inc(p0_act, 1)
            act.wait_ge(p0_dve, upto(9))
            fn(rstd, rstd, ACT.Sqrt).then_inc(p0_act, 1)
            for k in range(KT):
                act.wait_ge(h_tmp, upto(k + 1))
                fn(x_hi[:, k, :], h_tmpb[:, k % 2, :], ACT.Copy).then_inc(h_hi, 1)

            xp = rw["xp"]

            def copy_stream(blk, count, mixed, width=P):
                act.wait_ge(s_dense, upto(blk.before + 1))
                act.wait_ge(v_mix, upto(mixed))
                fn(halves(xp[0:width, 1:T + 1]), ps[0:width, 2 * blk.slot:2 * blk.slot + 2, :], ACT.Copy).then_inc(a_xp, 1)

            act.wait_ge(v_zero, upto(VZ))
            for c, width in enumerate((P, P, 32)):
                copy_stream(Block("lora", c), c, 2 * c, width)
                act.wait_ge(v_mix, upto(2 * c + 2))
                if c == 0:
                    fn(rw["wa"][0:64, :], rw["wa"][0:64, :], ACT.Tanh).then_inc(a_wa, 1)
                else:
                    t = rw["g0"] if c == 1 else rw["g1"][0:32, :]
                    fn(t, t, ACT.Sigmoid).then_inc(a_wa, 1)

            with act.Fori(0, PAIRS) as i:
                par = lambda c: rw_par[:, bass.ds(i + c, 1)]
                for s in range(3):
                    copy_stream(Block("rwkv", s, i), None, XM0 + i * 6 + 2 * s)

                def gate(c):
                    blk = Block("rwkv", 3 + c, i)
                    act.wait_ge(s_dense, upto(blk.before + 1))
                    act.wait_ge(s_gst, upto(i * 48 + c * 16))
                    fn(halves(rw["gs"]), pair_of(blk.slot), ACT.Sigmoid).then_inc(a_gate, 1)
                    act.wait_ge(a_gate, upto(i * 3 + c + 1))
                    act.dma_start(gates[bass.ds(c * D + i * P, P), :], rw["gs"]).then_inc(s_gst, 16)

                act.wait_ge(r_lwa, upto(i + 1))
                fn(halves(rw["sig"]), ps[:, 4:6, :], ACT.Sigmoid, bias=par(PR_W0)).then_inc(a_sa, 1)
                fn(halves(rw["A"]), ps[:, 6:8, :], ACT.Sigmoid, bias=par(PR_A0)).then_inc(a_sa, 1)
                act.wait_ge(v_kk, upto(i + 1))
                act.wait_ge(s_yb, upto(i * 16))
                fn(rw["t2"], rw["t1"], ACT.Square).then_inc(a_sqk, 1)
                gate(0)
                act.wait_ge(r_kks, upto(i + 1))
                fn(halves(rw["t2"]), ps[:, 4:6, :], ACT.Sqrt).then_inc(a_rk, 1)
                gate(1)
                act.wait_ge(r_g, upto(i + 1))
                fn(halves(rw["g"]), ps[:, 6:8, :], ACT.Copy).then_inc(a_g, 1)
                act.wait_ge(v_c, upto(i * VC + 18))
                fn(rw["ff"], rw["df"][:, 0:8], ACT.Exp, scale=-DECAY).then_inc(a_f, 1)
                act.wait_ge(v_c, upto(i * VC + 20))
                fn(rw["sig"], rw["sig"], ACT.Exp, scale=-DECAY).then_inc(a_exp, 1)
                fn(rw["t2"], rw["L"], ACT.Exp, scale=-DECAY).then_inc(a_exp, 1)
                act.wait_ge(a_exp, upto(i * 3 + 2))
                fn(rw["L"], rw["L"], ACT.Exp, scale=DECAY).then_inc(a_exp, 1)
                gate(2)
                for cc in range(CHUNKS // 2):
                    two = [(2 * cc + s, s, 4 * (1 - s)) for s in range(2)]
                    for c, s, b0 in two:
                        act.wait_ge(r_tk, upto(i * 8 + c + 1))
                        fn(tk[:, s, :, :], ps[:, b0 + 2, :].rearrange("p (q n) -> p q n", q=4), ACT.Copy).then_inc(a_tk, 1)
                        fn(RR[:, s, :, 64:128], ps[:, b0 + 2, P:2 * P].rearrange("p (h n) -> p h n", h=2), ACT.Copy).then_inc(a_tk, 1)
                        fn(xx[:, s, :, :, :].rearrange("p o h n -> p (o h) n"), ident.unsqueeze(1).broadcast_to([P, 4, P]), ACT.Copy).then_inc(a_xi, 1)
                    for c, s, b0 in two:
                        act.wait_ge(r_ak, upto(i * 8 + c + 1))
                        fn(RR[:, s, :, 0:64], ps[:, b0 + 3, 0:P].rearrange("p (h n) -> p h n", h=2), ACT.Copy).then_inc(a_ak, 1)
                    for lv in range(1, LEVELS):
                        for c, s, b0 in two:
                            act.wait_ge(r_y1, upto(lv_count(i, cc, lv, s) + 1))
                            fn(y1[:, s, :, :], ps[:, b0 + 2, 0:256].rearrange("p (h n) -> p h n", h=2), ACT.Copy).then_inc(a_y1, 1)
                    for c, s, b0 in two:
                        act.wait_ge(r_uw, upto(i * 8 + c + 1))
                        fn(uw[:, s, :, :], ps[:, b0 + 2, 0:256].rearrange("p (h n) -> p h n", h=2), ACT.Copy).then_inc(a_uw, 1)
                    for c, s, b0 in two:
                        act.wait_ge(r_y, upto(i * 8 + c + 1))
                        fn(rw["A"][:, c * P:(c + 1) * P], ps[:, b0 + 2, 0:P], ACT.Copy).then_inc(a_y, 1)
                act.wait_ge(v_post, upto(i * 6 + 1))
                fn(rw["t1"], rw["t2"], ACT.Square).then_inc(a_ysq, 1)
                act.wait_ge(r_var, upto(i + 1))
                fn(halves(rw["t1"]), ps[:, 6:8, :], ACT.Sqrt, scale=1.0 / RW_H, bias=eps_ln).then_inc(a_yr, 1)
                act.wait_ge(v_post, upto(i * 6 + 6))
                act.dma_start(y_b[bass.ds(i * P, P), :], rw["t2"]).then_inc(s_yb, 16)

            with act.Fori(0, TURNS["lru"]) as i:
                for u in range(2):
                    n = i * 2 + u
                    lp = lambda c: lru_par[0:80, bass.ds(n + c, 1)]
                    act.wait_ge(s_dense, upto(Block("lru", 2 * u, i).before + 1))
                    act.wait_ge(l_cv, upto(n * 4))
                    act.wait_ge(l_z, upto(1))
                    fn(halves(lr["xp"][0:80, 3:T + 3]), pair_of(Block("lru", 2 * u, i).slot)[0:80], ACT.Copy).then_inc(l_x, 1)
                    act.wait_ge(l_pe, upto(n + 1))
                    act.wait_ge(l_u, upto(n * 3))
                    fn(halves(lr["ga"][0:80]), ps[0:80, 4:6, :], ACT.Sigmoid, bias=lp(LP_BA)).then_inc(l_sa, 1)
                    fn(halves(lr["gx"][0:80]), ps[0:80, 6:8, :], ACT.Sigmoid, bias=lp(LP_BX)).then_inc(l_sa, 1)
                    act.wait_ge(l_sa, upto(n * 2 + 2))
                    fn(lr["a2"][0:80], lr["ga"][0:80], ACT.Exp, scale=rate2[0:80, bass.ds(n, 1)]).then_inc(l_exp, 1)
                    fn(lr["aa"][0:80], lr["ga"][0:80], ACT.Exp, scale=rate[0:80, bass.ds(n, 1)]).then_inc(l_exp, 1)
                    act.wait_ge(l_sq, upto(n + 1))
                    fn(lr["a2"][0:80], lr["a2"][0:80], ACT.Sqrt, scale=-1.0, bias=one_b[0:80, :]).then_inc(l_rt, 1)
                    act.wait_ge(l_out, upto(n))
                    fn(halves(lr["gy"][0:80]), pair_of(Block("lru", 2 * u + 1, i).slot)[0:80], ACT.Gelu_apprx_tanh).then_inc(l_gy, 1)
                    act.wait_ge(l_out, upto(n + 1))
                    act.dma_start(y_a[bass.ds(n * 80, 80), :], lr["ya"][0:80]).then_inc(s_ya, 16)

            act.wait_ge(t_z, upto(4))
            t1, t2 = at_["t1"], at_["t2"]
            with act.Fori(0, TURNS["att"]) as i:
                for g in range(2):
                    gg = i * 2 + g
                    for c in range(3):
                        blk = Block("att", 3 * g + c, i)
                        tile = at_["kvt"] if c == 0 else aq[:, c - 1, :]
                        act.wait_ge(s_dense, upto(blk.before + 1))
                        fn(halves(tile), pair_of(blk.slot), ACT.Copy).then_inc(t_cp, 1)
                        act.wait_ge(t_cp, upto(gg * 3 + c + 1))
                        if c > 0:
                            act.wait_ge(t_ns, upto(gg * 3 + c))
                            fn(halves(t2), ps[:, 4:6, :], ACT.Sqrt, scale=1.0 / HEAD, bias=eps_qk).then_inc(t_rt, 1)
                            if c == 1:
                                act.wait_ge(t_vt, upto(gg + 1))
                                fn(av[:, g, 1:9, :], ps[:, 6:8, :].rearrange("p b (n e) -> p (b n) e", e=P)[:, :, 64:128], ACT.Copy).then_inc(t_v, 1)
                            act.wait_ge(t_n, upto(gg * 3 + c))
                            if c == 1:
                                fn(ak[64:128, g, P:T + P], ak[0:64, g, P:T + P], ACT.Copy).then_inc(t_k2, 1)
                        fn(t1, tile, ACT.Square).then_inc(t_sq, 1)
                    act.wait_ge(t_ns, upto(gg * 3 + 3))
                    fn(halves(t2), ps[:, 4:6, :], ACT.Sqrt, scale=1.0 / HEAD, bias=eps_qk).then_inc(t_rt, 1)
                    for tick in range(16 + 3):
                        if tick < 16:
                            u = tick
                            act.wait_ge(t_d, upto((gg * 16 + u) * 4 + 4))
                            sm = asm[:, u % 4, :]
                            for h in range(2):
                                fn(asc[:, u % 4, h, :], asc[:, u % 4, h, :], ACT.Exp, bias=sm[:, 2 + h:3 + h], accum_out=sm[:, 4 + h:5 + h]).then_inc(t_e, 1)
                            fn(sm[:, 6:8], sm[:, 6:8], ACT.Exp).then_inc(t_e, 1)
                        if 0 <= tick - 2 < 16:
                            u = tick - 2
                            act.wait_ge(t_pt, upto(gg * 16 + u + 1))
                            fn(apt[:, u % 4, :], ps[:, 6 + u % 2, :], ACT.Copy).then_inc(t_ptc, 1)
                        if 0 <= tick - 3 < 16:
                            u, t, n = tick - 3, (tick - 3) // 8, (tick - 3) % 8
                            act.wait_ge(t_o, upto(gg * 16 + u + 1))
                            if n == 0:
                                act.wait_ge(s_yc, upto((gg * 2 + t) * 16))
                            fn(ayc[:, t, n * P:(n + 1) * P], ps[:, u % 2, 0:P], ACT.Copy).then_inc(t_oc, 1)
                            if n == 7:
                                act.wait_ge(t_oc, upto(gg * 16 + u + 1))
                                act.dma_start(y_c[bass.ds((gg * 2 + t) * P, P), :], ayc[:, t, :]).then_inc(s_yc, 16)

            yn, done = 0, 0
            for nm, kts, *_ in BR:
                act.wait_ge(s_dense, upto(Block(nm, 0).before))
                for k in range(kts):
                    act.wait_ge(s_y[yn % 2], 16 * (yn // 2 + 1))
                    fn(x_hi[:, k, :], yraw[:, yn % 2, :], ACT.Copy).then_inc(m_hi, 1)
                    yn += 1
                if nm == "oa1":
                    with act.Fori(0, 4) as i:
                        for c in range(2):
                            blk = Block(nm, c, i)
                            act.wait_ge(s_dense, upto(blk.before + 1))
                            fn(halves2(x2[:, bass.ds(i * 2 + c, 1), :]), pair_of(blk.slot), ACT.Copy).then_inc(m_cp, 1)
            act.wait_ge(s_dense, upto(Block("wout", 0).before))
            act.wait_ge(m_ev, upto(48))
            for k in range(KT):
                fn(x_hi[:, k, :], mix[:, k, :], ACT.Copy).then_inc(m_hi, 1)
            act.wait_ge(m_res, upto(KT))
            for k in range(KT):
                if k >= 2:
                    act.wait_ge(m_ss, upto(k - 1))
                fn(mt[:, k % 2, :], x2[:, k, :], ACT.Square).then_inc(m_sq, 1)
            act.wait_ge(m_ss, upto(KT))
            fn(halves(yraw[:, 0, :]), ps[:, 4:6, :], ACT.Sqrt, scale=1.0 / D, bias=eps_rms).then_inc(m_rt, 1)
            for k in range(KT):
                act.wait_ge(m_nh, upto(3 * k + 2))
                fn(x_hi[:, k, :], mt[:, k % 2, :], ACT.Copy).then_inc(m_hi, 1)
            with act.Fori(0, TURNS["ffn"]) as i:
                for t in range(2):
                    act.wait_ge(s_dense, upto(Block("ffn", 2 * t, i).before + 1))
                    act.wait_ge(m_act, upto(i * 2 + t))
                    fn(halves(gtl[:, 0, :]), pair_of(Block("ffn", 2 * t, i).slot), ACT.Silu).then_inc(m_sil, 1)
                    act.wait_ge(m_act, upto(i * 2 + t + 1))
                    if t == 0:
                        act.wait_ge(m_dn, upto(i * 8))
                    fn(hid_hi[:, t, :], mt[:, t, :], ACT.Copy).then_inc(m_hh, 1)
            for t in range(8):
                act.wait_ge(m_op, upto(t + 1))
                fn(halves(mix[:, t, :]), ps[:, 4 + 2 * (t % 2):6 + 2 * (t % 2), :], ACT.Copy).then_inc(m_o, 1)

        @blockctx.vector
        def _(dve):
            v = nc.vector
            seed(dve, "dve")
            steps = [0]

            def step(ins):
                steps[0] += 1
                ins.then_inc(p0_dve, 1)
                dve.wait_ge(p0_dve, upto(steps[0]))

            for row in (row_rw, row_lru, row_mod):
                step(v.memset(row, 0.0))
            for k, dst in enumerate((rw_par, lru_par)):
                dve.wait_ge(p0_pe, upto(k + 1))
                step(v.tensor_copy(dst[:, :], ps[:, 4 + k, 0:P]))
            dve.wait_ge(p0_pe, upto(3))
            lam = lru_par[0:80, LP_LAM:LP_LAM + 16]
            v.tensor_scalar(rate[0:80, :], lam, -1.0, None, ALU.mult).then_inc(lam_s, 1)
            dve.wait_ge(lam_s, upto(1))
            v.tensor_tensor(rate[0:80, :], rate[0:80, :], lam, ALU.max).then_inc(lam_s, 1)
            dve.wait_ge(lam_s, upto(2))
            step(v.tensor_copy(mod[:, :], ps[:, 6, 0:56]))
            dve.wait_ge(p0_act, upto(9))
            cs = mod[:, 48:56].unsqueeze(2).broadcast_to([P, 8, 2])
            step(v.tensor_copy(c_hi[:, :, :], cs))
            step(v.tensor_tensor(c_lo[:, :, :], cs, c_hi[:, :, :].bitcast(F32), ALU.subtract))
            step(v.tensor_scalar(rstd, sumsq, 1.0 / D, 1e-6, ALU.mult, ALU.add))
            dve.wait_ge(p0_act, upto(11))
            step(v.reciprocal(rstd, rstd))
            for t in range(8):
                step(v.tensor_scalar(xs[:, t, :], xs[:, t, :], rstd[:, t:t + 1], None, ALU.mult))
            e, z, z2, acc = rate2[0:80, :], small[0:80, 66:82], small[0:80, 82:96], None
            z2 = lsc[0:80, 0:16]
            acc = lsc[0:80, 16:32]
            step(v.tensor_scalar(z, e, 2.0, None, ALU.add))
            step(v.reciprocal(z, z))
            step(v.tensor_tensor(z, z, e, ALU.mult))
            step(v.tensor_tensor(z2, z, z, ALU.mult))
            step(v.tensor_scalar(acc, z2, 2.0 / 19, 2.0 / 17, ALU.mult, ALU.add))
            for m in (15, 13, 11, 9, 7, 5, 3, 1):
                step(v.tensor_tensor(acc, acc, z2, ALU.mult))
                step(v.tensor_scalar(acc, acc, 2.0 / m, None, ALU.add))
            step(v.tensor_tensor(acc, acc, z, ALU.mult))
            step(v.tensor_scalar(z, lam, -1.0, 0.0, ALU.mult, ALU.max))
            step(v.tensor_tensor(acc, acc, z, ALU.add))
            step(v.tensor_scalar(rate[0:80, :], acc, -8.0, None, ALU.mult))
            step(v.tensor_scalar(rate2[0:80, :], acc, -16.0, None, ALU.mult))
            for k, val in enumerate((1e-6, 64e-5, 1.0)):
                step(v.memset(bias_t[:, k:k + 1], val))
            assert steps[0] == 8 + 1 + 1 + 8 + SOFT, steps[0]

            def ada(name, first, fix):
                with dve.Fori(0, TURNS[name]) as i:
                    for c in range(2):
                        col = mod[:, bass.ds(i * 2 + first + c, 1)]
                        dve.wait_ge(s_dense, upto(Block(name, c, i).before + 1))
                        v.tensor_tensor(col, ps[:, 6 + c, 0:1], col, ALU.add).then_inc(ada_out, 1)
                dve.wait_ge(ada_out, upto(first + 2 * TURNS[name]))
                v.tensor_scalar(mod[:, fix:fix + 8], mod[:, fix:fix + 8], 1.0, None, ALU.add).then_inc(ada_fix, 1)
            ada("ada1", 0, MOD_SC1)
            dve.wait_ge(ada_fix, upto(1))
            for k in range(KT):
                dve.wait_ge(h_pe, upto(k + 1))
                tmp = h_tmpb[:, k % 2, :]
                if k >= 2:
                    dve.wait_ge(h_lo, upto(k - 1))
                v.tensor_scalar(halves(tmp), pair_of(k % 2), mod[:, MOD_SC1 + k:MOD_SC1 + k + 1], mod[:, MOD_SH1 + k:MOD_SH1 + k + 1], ALU.mult, ALU.add).then_inc(h_tmp, 1)
                dve.wait_ge(h_hi, upto(k + 1))
                v.tensor_tensor(x_lo[:, k, :], tmp, x_hi[:, k, :].bitcast(F32), ALU.subtract).then_inc(h_lo, 1)

            dve.wait_ge(h_lo, upto(KT))
            v.memset(rw["xp"][:, 0:1], 0.0).then_inc(v_zero, 1)
            v.memset(rw["q"], 0.0).then_inc(v_zero, 1)
            dve.wait_ge(s_mask, 32)
            v.tensor_copy(hid_lo[:, :, :].rearrange("p a n -> p (a n)")[:, 0:2 * LEVELS * P], rw["ar"][:, 0:2 * LEVELS * P]).then_inc(mask_ready, 1)
            v.tensor_copy(masks[:, 0:256], rw["bn"][:, 0:256]).then_inc(mask_ready, 1)
            dve.wait_ge(mask_ready, upto(2))
            level_mask = lambda lv, o: lv_mask[:, (2 * lv + o) * P:(2 * lv + o + 1) * P].bitcast(I32).unsqueeze(1).broadcast_to([P, 2, P])
            xp = rw["xp"]

            def mix_stream(copied, mixed, dst, mu, width=P, view=None):
                dve.wait_ge(a_xp, upto(copied))
                x0, x1, t = xp[0:width, 0:T], xp[0:width, 1:T + 1], rw["t1"][0:width, :]
                v.tensor_tensor(t, x0, x1, ALU.subtract).then_inc(v_mix, 1)
                dve.wait_ge(v_mix, upto(mixed + 1))
                if view is not None:
                    t, x1 = view(t), view(x1)
                v.scalar_tensor_tensor(dst, t, mu, x1, ALU.mult, ALU.add).then_inc(v_mix, 1)
                dve.wait_ge(v_mix, upto(mixed + 2))
            for c, (dst, width) in enumerate(((rw["wa"], P), (rw["g0"], P), (rw["g1"][0:32, :], 32))):
                mix_stream(c + 1, 2 * c, dst, rw_par[0:width, PR_MU_WA + c:PR_MU_WA + c + 1], width)

            with dve.Fori(0, PAIRS) as i:
                par = lambda c: rw_par[:, bass.ds(i + c, 1)]
                count = [0]

                def prep(ins, wait=True):
                    count[0] += 1
                    ins.then_inc(v_c, 1)
                    if wait:
                        dve.wait_ge(v_c, upto(i * VC + count[0]))

                for s, (dst, view) in enumerate(((rt_v, chunked), (rw["kt"], None), (rw["v"], None))):
                    mix_stream(XP0 + i * 3 + s + 1, XM0 + i * 6 + 2 * s, dst, par(PR_MU + 8 * s), view=view)
                t1, t2, A, L, sig, bn, kt = (rw[n] for n in ("t1", "t2", "A", "L", "sig", "bn", "kt"))
                v.tensor_scalar(t1, kt, par(PR_KK), None, ALU.mult).then_inc(v_kk, 1)
                v.memset(SS[:, 0, :], 0.0).then_inc(v_zero, 1)
                dve.wait_ge(a_sa, upto(i * 2 + 2))
                prep(v.tensor_scalar(bn, A, -1.0, par(PR_KA), ALU.add, ALU.mult))
                dve.wait_ge(a_rk, upto(i + 1))
                prep(v.tensor_scalar(t2, t2, 1e-12, None, ALU.max))
                prep(v.reciprocal(t2, t2))
                prep(v.tensor_tensor(al_v, chunked(t1), chunked(t2), ALU.mult))
                prep(v.scalar_tensor_tensor(kt, bn, 1.0, kt, ALU.add, ALU.mult))
                prep(v.scalar_tensor_tensor(chunked(bn), al_v, -1.0, chunked(A), ALU.mult, ALU.mult))
                prep(v.scalar_tensor_tensor(chunked(t1), rt_v, par(PR_RK), chunked(kt), ALU.mult, ALU.mult))
                for c in range(CHUNKS):
                    tok = slice(c * P, (c + 1) * P)
                    prep(v.tensor_tensor_scan(L[:, tok], sig[:, tok], sig[:, tok], 0.0, ALU.add, ALU.max), wait=c == CHUNKS - 1)
                Lc, df, mid = chunked(L), rw["df"][:, 0:8], rw["df"][:, 8:16]
                prep(v.tensor_copy(mid.unsqueeze(2), Lc[:, :, 63:64]))
                prep(v.tensor_tensor(df.unsqueeze(2), Lc[:, :, 127:128], mid.unsqueeze(2), ALU.subtract))
                prep(v.tensor_tensor(df[:, 0:7], df[:, 0:7], mid[:, 1:8], ALU.add))
                prep(v.tensor_tensor(Lc, Lc, mid.unsqueeze(2).broadcast_to([P, CHUNKS, P]), ALU.subtract))
                prep(v.tensor_tensor(sig, L, sig, ALU.subtract))
                dve.wait_ge(a_exp, upto(i * 3 + 1))
                prep(v.tensor_tensor(al_v, al_v, chunked(sig), ALU.mult), wait=False)
                dve.wait_ge(a_exp, upto(i * 3 + 2))
                prep(v.tensor_tensor(rt_v, rt_v, chunked(t2), ALU.mult), wait=False)
                dve.wait_ge(a_exp, upto(i * 3 + 3))
                prep(v.tensor_tensor(bn, bn, L, ALU.mult), wait=False)
                prep(v.tensor_tensor(kt, kt, L, ALU.mult), wait=False)
                assert count[0] == VC
                dve.wait_ge(r_bon, upto(i + 1))
                v.tensor_tensor(halves(rw["bv"]), ps[:, 4:6, :], halves(rw["v"]), ALU.mult).then_inc(v_fin, 1)
                dve.wait_ge(a_f, upto(i + 1))
                for cc in range(CHUNKS // 2):
                    two = [(2 * cc + s, s, 4 * (1 - s)) for s in range(2)]
                    for c, s, b0 in two:
                        n = i * 8 + c
                        dve.wait_ge(r_am, upto(n + 1))
                        for h in range(2):
                            v.tensor_tensor(am[:, s, h, :, :].rearrange("p (q o) n -> p q (o n)", q=2), ps[:, b0 + h, :].rearrange("p (q n) -> p q n", q=2),
                                            am_mask.bitcast(F32).unsqueeze(1).broadcast_to([P, 2, 256]), ALU.mult).then_inc(v_am, 1)
                        dve.wait_ge(a_xi, upto(n + 1))
                        wait_alone(dve)
                        v.copy_predicated(xx[:, s, 0, :, :], level_mask(0, 0), ps[:, b0 + 2:b0 + 4, 0:P]).then_inc(v_x0, 1)
                        dve.wait_ge(v_am, upto(n * 2 + 2))
                        wait_alone(dve)
                        v.copy_predicated(xx[:, s, 1, :, :], level_mask(0, 1), am[:, s, :, 0, :]).then_inc(v_x0, 1)
                    for lv in range(1, LEVELS):
                        for c, s, b0 in two:
                            dve.wait_ge(r_xu, upto(lv_count(i, cc, lv, s) + 1))
                            if lv < LEVELS - 1:
                                wait_alone(dve)
                                v.copy_predicated(xx[:, s, 0, :, :], level_mask(lv, 0), ps[:, b0, 0:256].rearrange("p (h n) -> p h n", h=2)).then_inc(v_xu, 1)
                            wait_alone(dve)
                            v.copy_predicated(xx[:, s, 1, :, :], level_mask(lv, 1), ps[:, b0 + 1, 0:256].rearrange("p (h n) -> p h n", h=2)).then_inc(v_xu, 1)
                    for c, s, b0 in two:
                        n = i * 8 + c
                        dve.wait_ge(r_gq, upto(n + 1))
                        v.tensor_tensor(gt[:, s, :], ps[:, b0, 0:P], rt_v[:, c, :], ALU.add).then_inc(v_gt, 1)
                        for h in range(2):
                            hp = slice(64 * h, 64 * h + 64)
                            v.tensor_tensor(qq[hp, s, hp], ps[hp, b0 + 1, hp], ident[hp, hp], ALU.add).then_inc(v_q, 1)
                    for c, s, b0 in two:
                        n = i * 8 + c
                        dve.wait_ge(r_s, upto(n + 1))
                        v.tensor_scalar(SS[:, (c + 1) % 2, :], ps[:, b0 + 3, 0:P], rw["ff"][:, c:c + 1], None, ALU.mult).then_inc(v_s, 1)
                post = [0]

                def after(ins):
                    post[0] += 1
                    ins.then_inc(v_post, 1)
                    dve.wait_ge(v_post, upto(i * 6 + post[0]))
                dve.wait_ge(r_mean, upto(i + 1))
                after(v.scalar_tensor_tensor(halves(t2), ps[:, 4:6, :], -1.0 / RW_H, halves(A), ALU.mult, ALU.add))
                dve.wait_ge(a_yr, upto(i + 1))
                after(v.reciprocal(t1, t1))
                after(v.tensor_tensor(t2, t2, t1, ALU.mult))
                after(v.tensor_scalar(t2, t2, par(PR_LNW), par(PR_LNB), ALU.mult, ALU.add))
                after(v.tensor_tensor(t2, t2, rw["bv"], ALU.add))
                after(v.tensor_tensor(t2, t2, rw["g"], ALU.mult))

            dve.wait_ge(s_yb, upto(PAIRS * 16))
            dve.wait_ge(s_gst, upto(PAIRS * 48))
            v.memset(lr["xp"][:, 0:3], 0.0).then_inc(l_z, 1)
            with dve.Fori(0, TURNS["lru"]) as i:
                for u in range(2):
                    n = i * 2 + u
                    lp = lambda c: lru_par[0:80, bass.ds(n + c, 1)]
                    xpv, xa, gx, a2, aa, hh, ya, gy = (lr[k][0:80] for k in ("xp", "xa", "gx", "a2", "aa", "h", "ya", "gy"))
                    dve.wait_ge(l_x, upto(n + 1))
                    v.tensor_scalar(xa, xpv[:, 3:3 + T], lp(LP_CW + 48), lp(LP_CB), ALU.mult, ALU.add).then_inc(l_cv, 1)
                    for j in range(3):
                        dve.wait_ge(l_cv, upto(n * 4 + j + 1))
                        v.scalar_tensor_tensor(xa, xpv[:, j:j + T], lp(LP_CW + 16 * j), xa, ALU.mult, ALU.add).then_inc(l_cv, 1)
                    dve.wait_ge(l_cv, upto(n * 4 + 4))
                    dve.wait_ge(l_exp, upto(n * 2 + 1))
                    v.tensor_scalar(a2, a2, 1.0, None, ALU.min).then_inc(l_sq, 1)
                    dve.wait_ge(l_sa, upto(n * 2 + 2))
                    v.tensor_tensor(gx, gx, xa, ALU.mult).then_inc(l_u, 1)
                    dve.wait_ge(l_u, upto(n * 3 + 1))
                    dve.wait_ge(l_rt, upto(n + 1))
                    v.tensor_tensor(gx, gx, a2, ALU.mult).then_inc(l_u, 1)
                    dve.wait_ge(l_u, upto(n * 3 + 2))
                    dve.wait_ge(l_exp, upto(n * 2 + 2))
                    v.tensor_tensor_scan(hh, aa, gx, 0.0, ALU.mult, ALU.add).then_inc(l_u, 1)
                    dve.wait_ge(l_u, upto(n * 3 + 3))
                    dve.wait_ge(l_gy, upto(n + 1))
                    dve.wait_ge(s_ya, upto(n * 16))
                    v.tensor_tensor(ya, hh, gy, ALU.mult).then_inc(l_out, 1)

            dve.wait_ge(l_out, upto(LRU_N))
            dve.wait_ge(s_ya, upto(LRU_N * 16))
            for g in range(2):
                v.memset(ak[:, g, 0:P], 0.0).then_inc(t_z, 1)
                v.memset(av[:, g, 0, :], 0.0).then_inc(t_z, 1)
            dve.wait_ge(s_am, 16)
            dve.wait_ge(gain_sem, 64)
            v.tensor_scalar(nsinks[:, :], sinks_b, -1.0, None, ALU.mult).then_inc(t_z, 1)
            dve.wait_ge(t_z, upto(5))
            t2 = at_["t2"]
            amask = at_["mask"].rearrange("p (o m) -> p o m", o=2)
            with dve.Fori(0, TURNS["att"]) as i:
                for g in range(2):
                    gg = i * 2 + g
                    for c in range(3):
                        dve.wait_ge(t_rt, upto(gg * 3 + c + 1))
                        v.reciprocal(t2, t2).then_inc(t_rc, 1)
                        dve.wait_ge(t_rc, upto(gg * 3 + c + 1))
                        if c == 0:
                            v.scalar_tensor_tensor(ak[0:64, g, P:T + P], at_["kvt"][0:64, :], gains[0:64, 1:2], t2[0:64, :], ALU.mult, ALU.mult).then_inc(t_n, 1)
                        else:
                            q = aq[:, c - 1, :]
                            v.scalar_tensor_tensor(q, q, gains[:, 0:1], t2, ALU.mult, ALU.mult).then_inc(t_n, 1)
                    for tick in range(17):
                        if tick < 16:
                            u, t, n = tick, tick // 8, tick % 8
                            U = gg * 16 + u
                            sm, sc = asm[:, u % 4, :], asc[:, u % 4, :, :]
                            sk = sinks_b[:, bass.ds(gg * 4 + 2 * t, 2)]
                            dve.wait_ge(t_sc, upto(U + 1))
                            if u >= 4:
                                dve.wait_ge(t_pt, upto(U - 3))
                            v.scalar_tensor_tensor(sc, ps[:, 4 - 2 * (u % 2):6 - 2 * (u % 2), 0:256], HEAD ** -0.5,
                                                   amask[:, min(n, 1), :].unsqueeze(1).broadcast_to([P, 2, 256]), ALU.mult, ALU.add).then_inc(t_d, 1)
                            dve.wait_ge(t_d, upto(U * 4 + 1))
                            v.tensor_reduce(sm[:, 0:2], sc, AX.X, ALU.max).then_inc(t_d, 1)
                            dve.wait_ge(t_d, upto(U * 4 + 2))
                            v.scalar_tensor_tensor(sm[:, 2:4], sm[:, 0:2], -1.0, nsink(gg, t), ALU.mult, ALU.min).then_inc(t_d, 1)
                            dve.wait_ge(t_d, upto(U * 4 + 3))
                            v.tensor_tensor(sm[:, 6:8], sk, sm[:, 2:4], ALU.add).then_inc(t_d, 1)
                        if tick >= 1:
                            u = tick - 1
                            U = gg * 16 + u
                            sm, sc = asm[:, u % 4, :], asc[:, u % 4, :, :]
                            dve.wait_ge(t_e, upto(U * 3 + 3))
                            v.tensor_tensor(sm[:, 8:10], sm[:, 4:6], sm[:, 6:8], ALU.add).then_inc(t_dc, 1)
                            dve.wait_ge(t_dc, upto(U * 2 + 1))
                            v.reciprocal(sm[:, 10:12], sm[:, 8:10]).then_inc(t_dc, 1)
                            dve.wait_ge(t_dc, upto(U * 2 + 2))
                            for h in range(2):
                                v.tensor_scalar(sc[:, h, :], sc[:, h, :], sm[:, 10 + h:11 + h], None, ALU.mult).then_inc(t_p, 1)

            ada("ada2", 16, MOD_SC2)

            dve.wait_ge(s_yc, upto(8 * 16))
            yn, merged = 0, 0

            for nm, kts, *_ in BR:
                for k in range(kts):
                    dve.wait_ge(m_hi, upto(yn + 1))
                    v.tensor_tensor(x_lo[:, k, :], yraw[:, yn % 2, :], x_hi[:, k, :].bitcast(F32), ALU.subtract).then_inc(m_lo, 1)
                    yn += 1
                if nm == "oa1":
                    continue
                with dve.Fori(0, 4) as i:
                    for c in range(2):
                        blk = Block(nm, c, i)
                        m0 = merged * 2 + (i * 2 + c) * 2
                        acc, t = mix[:, bass.ds(i * 2 + c, 1), :], mt[:, c, :]
                        dve.wait_ge(s_dense, upto(blk.before + 1))
                        gate_n = merged // 2 + c // 2
                        if nm == "oa2":
                            dve.wait_ge(m_cp, upto(8))
                            v.tensor_tensor(halves(t), pair_of(blk.slot), halves2(x2[:, bass.ds(i * 2 + c, 1), :]), ALU.add).then_inc(m_ev, 1)
                            dve.wait_ge(m_ev, upto(m0 + 1))
                            dve.wait_ge(s_g[c], (merged // 2) * 16 + i * 16 + 16)
                            v.tensor_tensor(acc.rearrange("p o n -> p (o n)"), t, gtl[:, c, :], ALU.mult).then_inc(m_ev, 1)
                        else:
                            dve.wait_ge(s_g[c], (merged // 2) * 16 + i * 16 + 16)
                            v.tensor_tensor(halves(t), pair_of(blk.slot), halves(gtl[:, c, :]), ALU.mult).then_inc(m_ev, 1)
                            dve.wait_ge(m_ev, upto(m0 + 1))
                            flat = acc.rearrange("p o n -> p (o n)")
                            v.tensor_tensor(flat, flat, t, ALU.add).then_inc(m_ev, 1)
                merged += 8
            for k in range(KT):
                dve.wait_ge(m_hi, upto(NY + k + 1))
                v.tensor_tensor(x_lo[:, k, :], mix[:, k, :], x_hi[:, k, :].bitcast(F32), ALU.subtract).then_inc(m_lo, 1)
            for k in range(KT):
                dve.wait_ge(m_pe, upto(k + 1))
                v.tensor_copy(halves(x2[:, k, :]), ps[:, 4 + 2 * (k % 2):6 + 2 * (k % 2), :]).then_inc(m_xt, 1)
            dve.wait_ge(m_xt, upto(KT))
            with dve.Fori(0, TURNS["wout"]) as i:
                for c in range(2):
                    blk = Block("wout", c, i)
                    dve.wait_ge(s_dense, upto(blk.before + 1))
                    r = halves2(x2[:, bass.ds(i * 2 + c, 1), :])
                    v.scalar_tensor_tensor(r, pair_of(blk.slot), mod[:, bass.ds(i * 2 + (MOD_G1 + c), 1)], r, ALU.mult, ALU.add).then_inc(m_res, 1)
            rs = yraw[:, 0, :]
            dve.wait_ge(m_rt, upto(1))
            v.reciprocal(rs, rs).then_inc(m_n, 1)
            dve.wait_ge(m_n, upto(1))
            for k in range(KT):
                t = mt[:, k % 2, :]
                v.tensor_tensor(t, x2[:, k, :], rs, ALU.mult).then_inc(m_nh, 1)
                dve.wait_ge(m_nh, upto(3 * k + 1))
                v.tensor_scalar(t, t, mod[:, MOD_SC2 + k:MOD_SC2 + k + 1], mod[:, MOD_SH2 + k:MOD_SH2 + k + 1], ALU.mult, ALU.add).then_inc(m_nh, 1)
                dve.wait_ge(m_nh, upto(3 * k + 2))
                dve.wait_ge(m_hi, upto(NY + KT + k + 1))
                v.tensor_tensor(x_lo[:, k, :], t, x_hi[:, k, :].bitcast(F32), ALU.subtract).then_inc(m_nh, 1)
                dve.wait_ge(m_nh, upto(3 * k + 3))
            with dve.Fori(0, TURNS["ffn"]) as i:
                for t in range(2):
                    dve.wait_ge(s_dense, upto(Block("ffn", 2 * t + 1, i).before + 1))
                    dve.wait_ge(m_sil, upto(i * 2 + t + 1))
                    v.tensor_tensor(halves(mt[:, t, :]), pair_of(Block("ffn", 2 * t + 1, i).slot), halves(gtl[:, 0, :]), ALU.mult).then_inc(m_act, 1)
                    dve.wait_ge(m_act, upto(i * 2 + t + 1))
                    dve.wait_ge(m_hh, upto(i * 2 + t + 1))
                    v.tensor_tensor(hid_lo[:, t, :], mt[:, t, :], hid_hi[:, t, :].bitcast(F32), ALU.subtract).then_inc(m_hl, 1)
                for m in range(8):
                    if m % 4 == 3:
                        dve.wait_ge(s_dense, upto(Block("ffn", 4 + m // 4, i).before + 1))
                    else:
                        dve.wait_ge(m_dd, upto(i * 6 + m - m // 4 + 1))
                    r = halves(x2[:, m, :])
                    v.scalar_tensor_tensor(r, ps[:, 2 * (m % 2):2 * (m % 2) + 2, :], mod[:, MOD_G2 + m:MOD_G2 + m + 1], r, ALU.mult, ALU.add).then_inc(m_dn, 1)
                dve.wait_ge(m_dn, upto(i * 8 + 8))


INPUTS = ["x", "c", "w_ada", "b_ada", "w_in", "conv_w", "conv_b", "lru_wa", "lru_ba", "lru_wx", "lru_bx", "lru_lambda",
          "w_lru_o", "rw_mu", "rw_w0", "rw_w2", "rw_a0", "rw_a2", "rw_g2", "rw_kk", "rw_ka", "rw_rk", "rw_ln_w", "rw_ln_b",
          "w_rw_o", "q_gain", "k_gain", "sinks", "w_att_o", "w_out", "w_ffn_in", "w_ffn_out"]


def kernel(**inputs):
    import concourse.bacc as _bacc
    from concourse.bass_utils import run_bass_kernel_spmd as _run

    nc = _bacc.Bacc("TRN2", target_bir_lowering=False, num_devices=1)
    arrays, aps = {}, {}
    for name in INPUTS:
        arr = np.ascontiguousarray(inputs[name])
        arrays[f"in_{name}"] = arr
        aps[name] = nc.dram_tensor(f"in_{name}", arr.shape, F32, kind="ExternalInput").ap()
    arrays["in_consts"] = constants()
    aps["consts"] = nc.dram_tensor("in_consts", (P, C_N), F32, kind="ExternalInput").ap()
    out = nc.dram_tensor("out", (1, T, D), F32, kind="ExternalOutput").ap()
    build(nc, aps, out)
    return _run(nc, [arrays], core_ids=[0]).results[0]["out"]
```

```python
import math
from contextlib import ExitStack

import numpy as np

import concourse.bass as bass
from concourse import mybir

F32 = mybir.dt.float32
F32R = mybir.dt.float32r
I32 = mybir.dt.int32
ALU = mybir.AluOpType
ACT = mybir.ActivationFunctionType
AX = mybir.AxisListType

P = 128
T = 1024
D = 1024
KT = D // P
LRU_W, LRU_BLK = 1280, 80
LRU_N = LRU_W // LRU_BLK
RW_W, RW_H = 1024, 64
PAIRS = RW_W // P
KV_HEADS, HEAD = 4, 64
FF = 2816
FF_GROUP = 2
CHUNK = 128
CHUNKS = T // CHUNK
LEVELS = int(math.log2(CHUNK))
DECAY = math.exp(-0.5)
NEG = -1e30

COL_LX, COL_LY = 0, LRU_W
COL_RW = 2 * LRU_W
COL_LORA = COL_RW + 3 * RW_W
COL_Q = COL_LORA + 288
COL_K = COL_Q + 1024
COL_V = COL_K + 256
COL_G = COL_V + 256

PR_W0, PR_A0, PR_KK, PR_KA, PR_RK, PR_LNW, PR_LNB, PR_MU = range(0, 64, 8)
PR_MU_WA, PR_MU_G0, PR_MU_G1, PR_ROWS = 80, 81, 82, 83
LP_CW, LP_CB, LP_BA, LP_BX, LP_LAM = 0, 64, 80, 96, 112
MOD_SH1, MOD_SC1, MOD_G1, MOD_SH2, MOD_SC2, MOD_G2, MOD_N = range(0, 56, 8)

C_ID, C_BD, C_ONE, C_ATT, C_AM, C_LV = 0, 128, 256, 384, 896, 1152
C_N = C_LV + 2 * LEVELS * P
C_KEEP = C_ATT

STREAM = [("lora", 1, 3), ("rwkv", PAIRS, 6), ("lru", LRU_N // 2, 4), ("att", 2, 6),
          ("oa0", 4, 2), ("oa1", 4, 2), ("oa2", 4, 2), ("oc0", 4, 2), ("oc1", 4, 2), ("ob0", 4, 2), ("ob1", 4, 2),
          ("wout0", 4, 2), ("wout1", 4, 2), ("ffn_first", 1, 2), ("ffn", FF // P // FF_GROUP - 1, 6), ("ffn_last", 1, 4)]
STREAM_START = 2
BASE, _at = {}, STREAM_START
for _name, _turns, _per in STREAM:
    BASE[_name] = _at
    _at += _turns * _per
TURNS = {n: t for n, t, _ in STREAM}
PER = {n: p for n, _, p in STREAM}


def constants():
    c = np.zeros((P, C_N), np.float32)
    r, k = np.arange(P)[:, None], np.arange(P)[None, :]
    c[:, C_ID:C_ID + P] = r == k
    c[:, C_BD:C_BD + P] = r // 64 == k // 64
    c[:, C_ONE:C_ONE + P] = 1
    kj = np.arange(2 * P)[None, :]
    local = (kj <= r + P) & (r + P - kj < P)
    c[:, C_ATT:C_ATT + 256] = np.where(local & (kj >= P), 0, NEG)
    c[:, C_ATT + 256:C_ATT + 512] = np.where(local, 0, NEG)
    c[:, C_AM:C_AM + P] = k > r
    c[:, C_AM + P:C_AM + 2 * P] = k >= r
    for lv in range(LEVELS):
        s = 2 ** lv
        low = (r // s % 2 == 1) & (k // s == r // s - 1)
        c[:, C_LV + 2 * lv * P:C_LV + (2 * lv + 1) * P] = low
        c[:, C_LV + (2 * lv + 1) * P:C_LV + (2 * lv + 2) * P] = low.T
    return c


class Block:

    def __init__(self, name, c, i=0):
        at = BASE[name] + c
        self.slot = at % 2
        self.before = i * PER[name] + at
        self.loads = i * (PER[name] // 2) + at // 2 - STREAM_START // 2


def build(nc, a, out):
    ctx = ExitStack()
    with ctx:
        def sb(name, shape, dt=F32):
            return ctx.enter_context(nc.sbuf_tensor(name, shape, dt))

        def sem(name):
            return ctx.enter_context(nc.semaphore(name))

        def dram(name, rows):
            return nc.dram_tensor(name, (rows, T), F32, kind="Internal").ap()

        y_a, y_b, y_c, gates = dram("y_a", LRU_W), dram("y_b", RW_W), dram("y_c", D), dram("gates_sig", 3 * D)

        x_hi = sb("x_hi", [P, KT, T], F32R)
        x_lo = sb("x_lo", [P, KT, T], F32R)
        w_raw = sb("w_raw", [P, 2, 1024])
        w_hi = sb("w_hi", [P, 2, 1024], F32R)
        w_lo = sb("w_lo", [P, 2, 1024], F32R)
        hid_hi = sb("hid_hi", [P, 2, T], F32R)
        hid_lo = sb("hid_lo", [P, 2, T], F32R)
        keep = sb("keep", [P, C_KEEP])
        rw_par = sb("rw_par", [P, P])
        lru_par = sb("lru_par", [P, P])
        mod = sb("mod", [P, 56])
        small = sb("small", [P, 96])
        ARENA = 25100
        arena = sb("arena", [P, ARENA])
        ps = ctx.enter_context(nc.psum_tensor("ps", [P, 8, 512], F32))

        ident = keep[:, C_ID:C_ID + P]
        headsum = keep[:, C_BD:C_BD + P]
        ones = keep[:, C_ONE:C_ONE + P]

        def carve(sizes):
            at, got = 0, {}
            for name, n in sizes:
                got[name] = arena[:, at:at + n]
                at += n
            assert at <= ARENA, at
            return got

        def pair_of(slot):
            return ps[:, 2 * slot:2 * slot + 2, :]

        def halves(ap):
            return ap.rearrange("p (h n) -> p h n", h=2)

        s_const = sem("constants_loaded")
        s_par = sem("parameters_loaded")
        s_w = [sem("weights_loaded_0"), sem("weights_loaded_1")]
        s_whi = sem("weights_high_part")
        s_wsplit = sem("weights_split")
        s_dense = sem("dense_done")

        s_yb, s_gst, s_ya, s_yc = (sem(n) for n in ("y_b_stored", "gate_stored", "y_a_stored", "y_c_stored"))
        stream_sems = [s_dense, s_whi, s_wsplit]
        engine_sems = {"pe": [s_dense], "act": [s_yb, s_gst, s_ya, s_yc], "dve": [], "pool": [s_whi, s_wsplit]}

        def made_by(engine, *names):
            got = [sem(n) for n in names]
            engine_sems[engine] += got
            return got if len(got) > 1 else got[0]

        s_x = sem("x_loaded")
        p0_pe, p0_act, p0_dve = made_by("pe", "start_pe"), made_by("act", "start_act"), made_by("dve", "start_dve")
        ada_out, ada_pe = made_by("dve", "mod_columns_ready"), made_by("pe", "mod_columns_done")
        s_ada = [sem(f"ada_weights_loaded_{k}") for k in range(4)]
        ADA0 = 8
        ada_fix = made_by("dve", "mod_scales_ready")
        h_pe, h_tmp, h_hi, h_lo = made_by("pe", "xnT_done"), made_by("dve", "h_ready"), made_by("act", "h_high"), made_by("dve", "h_low")

        passed = {"SP": sem("sp_waits_passed"), "Pool": sem("pool_waits_passed"), "DVE": sem("dve_waits_passed")}

        def wait_alone(eng):
            eng.sem_inc(passed[eng.engine.name], 1)

        def upto(n):
            return max(n, 0) + 1 if isinstance(n, int) else n + 1

        def seed(eng, name):
            for s in engine_sems[name]:
                eng.sem_inc(s, 1 + STREAM_START if s in stream_sems else 1)

        def load_block(sp, blk, src, width):
            n = src.shape[1] * width
            dst = w_raw[:, blk.slot, 0:n].rearrange("p (k m) -> p k m", m=width)
            sp.wait_ge(s_wsplit, upto(blk.before - 1))
            wait_alone(sp)
            sp.dma_start(dst, src).then_inc(s_w[blk.slot], 16)

        def split_block(pool, blk, n):
            raw, hi, lo = (t[:, blk.slot, 0:n] for t in (w_raw, w_hi, w_lo))
            pool.wait_ge(s_w[blk.slot], blk.loads * 16 + 16)
            pool.wait_ge(s_dense, upto(blk.before - 1))
            wait_alone(pool)
            nc.gpsimd.tensor_copy(hi, raw).then_inc(s_whi, 1)
            pool.wait_ge(s_whi, upto(blk.before + 1))
            nc.gpsimd.tensor_tensor(lo, raw, hi.bitcast(F32), ALU.subtract).then_inc(s_wsplit, 1)

        def three_passes(dst, w, x, first, last):
            (wh, wl), (xh, xl) = w, x
            n = len(dst)
            for m, (wp, xp) in enumerate(((wh, xh), (wh, xl), (wl, xh))):
                for h in range(n):
                    ins = nc.tensor.matmul(dst[h], wp, xp[h], start=first and m == 0, stop=last and m == 2)
            return ins

        def dense(pe, blk, width=P, tiles=KT, first=0):
            pe.wait_ge(s_wsplit, upto(blk.before + 1))
            dst = [ps[0:width, 2 * blk.slot + h, :] for h in range(2)]
            for k in range(tiles):
                w = [t[:, blk.slot, k * width:(k + 1) * width] for t in (w_hi, w_lo)]
                x = [[t[:, first + k, h * 512:(h + 1) * 512] for h in range(2)] for t in (x_hi, x_lo)]
                ins = three_passes(dst, w, x, k == 0, k == tiles - 1)
            ins.then_inc(s_dense, 1)

        def cols(w, c0, n):
            return w[:, bass.ds(c0, n)].rearrange("(k p) m -> p k m", p=P)

        st0 = carve([("row_rw", P), ("row_lru", P), ("row_mod", P), ("xs", 8 * D), ("tmp", 2 * T), ("sq", 2 * D),
                     ("ada", 4 * 2048)])
        ada_w0 = st0["ada"].rearrange("p (s k m) -> p s k m", s=4, k=KT)
        row_rw, row_lru, row_mod = st0["row_rw"], st0["row_lru"], st0["row_mod"]
        xs = st0["xs"].rearrange("p (t d) -> p t d", t=8)
        h_tmpb = st0["tmp"].rearrange("p (s n) -> p s n", s=2)
        sq0 = st0["sq"].rearrange("p (s n) -> p s n", s=2)
        sumsq, rstd = small[:, 0:8], small[:, 8:16]
        sinks_b = small[:, 16:32]
        gains = small[:, 32:34]
        rate, rate2 = small[:, 34:50], small[:, 50:66]

        def load_parameters(sp):
            for src, dst in (("rw_w0", PR_W0), ("rw_a0", PR_A0), ("rw_kk", PR_KK), ("rw_ka", PR_KA), ("rw_rk", PR_RK),
                             ("rw_ln_w", PR_LNW), ("rw_ln_b", PR_LNB)):
                sp.dma_start(row_rw[dst:dst + 8, :], a[src][0].rearrange("(t p) -> t p", p=P)).then_inc(s_par, 16)
            mu = a["rw_mu"][0]
            sp.dma_start(row_rw[PR_MU:PR_MU_G1, :], mu[0:26 * P].rearrange("(t p) -> t p", p=P)).then_inc(s_par, 16)
            sp.dma_start(row_rw[PR_MU_G1:PR_ROWS, 0:32], mu[26 * P:26 * P + 32].rearrange("(t p) -> t p", t=1)).then_inc(s_par, 16)
            sp.dma_start(row_lru[0:64, 0:80], a["conv_w"][0].rearrange("j (b n) -> (j b) n", n=80)).then_inc(s_par, 16)
            for src, dst in (("conv_b", LP_CB), ("lru_ba", LP_BA), ("lru_bx", LP_BX), ("lru_lambda", LP_LAM)):
                sp.dma_start(row_lru[dst:dst + 16, 0:80], a[src][0].rearrange("(b n) -> b n", n=80)).then_inc(s_par, 16)
            sp.dma_start(row_mod[0:48, :], a["b_ada"][0].rearrange("(t p) -> t p", p=P)).then_inc(s_par, 16)
            sp.dma_start(row_mod[48:56, :], a["c"][0].rearrange("(t p) -> t p", p=P)).then_inc(s_par, 16)
            sp.dma_start(sinks_b, a["sinks"].broadcast_to([P, 16])).then_inc(s_par, 16)

        gain_sem = sem("gains_loaded")

        def load_gains(sp):
            for col, name in ((0, "q_gain"), (1, "k_gain")):
                for h in range(2):
                    sp.dma_start(gains[64 * h:64 * h + 64, col:col + 1], a[name].rearrange("a (n o) -> n (a o)", o=1)).then_inc(gain_sem, 16)

        PLACES = 4
        PLACE_SIZE = 2560
        rw_at = {"t1": 5 * T + 8}
        rw = carve([("wa", T), ("g0", T), ("g1", T), ("xp", T + 8), ("A", T), ("t1", T), ("t2", T), ("sig", T), ("L", T),
                    ("ar", 2 * T), ("bn", T), ("kt", T), ("v", T), ("bv", T), ("g", T), ("gs", T),
                    ("lw", P), ("lg0", P), ("lg1", P), ("S", 2 * P), ("df", 16), ("ff", 8), ("q", PLACES * P),
                    ("place0", PLACE_SIZE), ("place1", PLACE_SIZE), ("place3", PLACE_SIZE - (4 * T - PLACE_SIZE))])
        ar = rw["ar"].rearrange("p (c s n) -> p c s n", c=CHUNKS, s=2)
        al_v, rt_v = ar[:, :, 0, :], ar[:, :, 1, :]
        chunked = lambda ap: ap.rearrange("p (c n) -> p c n", c=CHUNKS)
        scratch = arena[:, rw_at["t1"]:rw_at["t1"] + 4 * T]
        left = 4 * T - PLACE_SIZE
        parts = {"am": 1024, "xx": 512, "y1": 256, "tk": 512, "R": 256}
        places = []
        for base in (rw["place0"], rw["place1"], scratch[:, 0:PLACE_SIZE], None):
            at, got = 0, {}
            for name, n in parts.items():
                if base is not None:
                    got[name] = base[:, at:at + n]
                elif at + n <= left:
                    got[name] = scratch[:, PLACE_SIZE + at:PLACE_SIZE + at + n]
                    rest = at + n
                else:
                    got[name] = rw["place3"][:, at - rest:at - rest + n]
                at += n
            places.append(got)
        am = [g["am"].rearrange("p (h q n) -> p h q n", h=2, q=4) for g in places]
        xx = [g["xx"].rearrange("p (o h n) -> p o h n", o=2, h=2) for g in places]
        y1 = [g["y1"].rearrange("p (h n) -> p h n", h=2) for g in places]
        tk = [g["tk"].rearrange("p (q n) -> p q n", q=4) for g in places]
        RR = [g["R"].rearrange("p (h n) -> p h n", h=2) for g in places]
        uw = y1
        gt = [x[:, 0, 0, :] for x in xx]
        qq = rw["q"].rearrange("p (s n) -> p s n", s=PLACES)

        def blocks_of(ap, lv, odd):
            return ap.rearrange("p h (b two e) -> p h b two e", two=2, e=2 ** lv)[..., odd, :]

        def per_head(ap):
            return ap.rearrange("p (h n) -> p h n", h=2)
        SS = rw["S"].rearrange("p (s n) -> p s n", s=2)
        masks = hid_hi[:, :, :].rearrange("p a n -> p (a n)")
        am_mask = masks[:, 0:256]
        lv_mask = hid_lo[:, :, :].rearrange("p a n -> p (a n)")[:, 0:2 * LEVELS * P]
        s_mask, s_lw = sem("masks_loaded"), sem("lora_weights_loaded")
        mask_ready = made_by("dve", "masks_ready")
        (r_lwa, r_kks, r_g, r_bon, r_mean, r_var) = made_by("pe", "rw_lora_done", "rw_kk_sums", "rw_g_done", "rw_bonus_sums", "rw_mean_done", "rw_var_done")
        (r_tk, r_am, r_x0, r_y1, r_xu, r_ak, r_uw, r_gq, r_s, r_y) = made_by(
            "pe", "tokens_major_done", "pair_products_done", "level0_product_done", "level_product_done", "level_update_done", "ak_v_done",
            "solve_done", "g_q_done", "state_done", "y_chunk_done")
        (a_xp, a_sa, a_sqk, a_gate, a_rk, a_g, a_exp, a_f, a_wa) = made_by(
            "act", "rw_stream_copied", "rw_sigmoids_ready", "rw_kk_squared", "gate_ready", "rw_kk_root", "rw_g_ready",
            "rw_exponentials", "rw_state_scale", "rw_lora_in_ready")
        (a_tk, a_xi, a_y1, a_ak, a_uw, a_y, a_ysq, a_yr) = made_by(
            "act", "tokens_major_ready", "inverse_started", "level_product_ready", "ak_v_ready", "solve_ready", "y_chunk_ready",
            "y_squared", "y_root")
        (v_mix, v_kk, v_c, v_fin, v_am, v_x0, v_xu, v_gt, v_q, v_s, v_post, v_zero, v_lora) = made_by(
            "dve", "rw_stream_mixed", "rw_kk_ready", "rw_prep", "rw_bonus_ready", "pair_products_ready", "level0_ready",
            "level_ready", "g_ready", "q_ready", "state_ready", "rw_post", "rw_zeroed", "lora_mixed")

        lr = carve([("xp", T + 8), ("xa", T), ("ga", T), ("gx", T), ("aa", T), ("a2", T), ("h", T), ("gy", T), ("ya", T),
                    ("wa", 2 * LRU_BLK), ("wx", 2 * LRU_BLK), ("ada", 2 * 2048)])
        ada_w1 = lr["ada"].rearrange("p (s k m) -> p s k m", s=2, k=KT)
        l_x, l_sa, l_rt, l_gy, l_exp = made_by("act", "lru_x_copied", "lru_gates_ready", "lru_root_ready", "lru_gelu_ready", "lru_decay_ready")
        l_pe = made_by("pe", "lru_gates_done")
        l_cv, l_sq, l_u, l_out, l_z = made_by("dve", "conv_steps", "decay_squared", "lru_input_steps", "lru_out_steps", "lru_zeroed")
        s_lw2 = [sem("lru_gate_weights_loaded_0"), sem("lru_gate_weights_loaded_1")]

        at_ = carve([("k", 2 * (T + P)), ("v", 2 * 9 * HEAD), ("kvt", T), ("t1", T), ("t2", T), ("q", 2 * T), ("yc", 2 * T),
                     ("mask", 512), ("s", 4 * 512), ("pT", 4 * 512), ("sm", 64)])
        ak = at_["k"].rearrange("p (g n) -> p g n", g=2)
        av = at_["v"].rearrange("p (g b d) -> p g b d", g=2, b=9)
        aq = at_["q"].rearrange("p (t n) -> p t n", t=2)
        ayc = at_["yc"].rearrange("p (t n) -> p t n", t=2)
        asc = at_["s"].rearrange("p (u h n) -> p u h n", u=4, h=2)
        apt = at_["pT"].rearrange("p (u m) -> p u m", u=4)
        asm = at_["sm"].rearrange("p (u m) -> p u m", u=4)
        s_am, s_kfirst = sem("attention_masks_loaded"), sem("k_half_loaded")
        t_ns, t_vt, t_sc, t_pt, t_o = made_by("pe", "norm_sums_done", "v_transposed", "scores_done", "probs_transposed", "attention_out_done")
        t_cp, t_sq, t_rt, t_v, t_e, t_ptc, t_oc, t_k2 = made_by(
            "act", "kv_copied", "head_squares", "head_root", "v_ready", "exp_done", "probs_t_ready", "attention_out_ready", "k_second_half")
        t_rc, t_n, t_d, t_m, t_p, t_z, t_dc = made_by("dve", "head_rsqrt", "head_normed", "softmax_steps", "neg_max_ready", "probs_ready", "att_zeroed", "denominator_steps")

        mg = carve([("x2", KT * T), ("mix", KT * T), ("yraw", 2 * T), ("gt", 2 * T), ("t", 2 * T)])
        x2 = mg["x2"].rearrange("p (k n) -> p k n", k=KT)
        mix = mg["mix"].rearrange("p (k n) -> p k n", k=KT)
        yraw = mg["yraw"].rearrange("p (s n) -> p s n", s=2)
        gtl = mg["gt"].rearrange("p (s n) -> p s n", s=2)
        mt = mg["t"].rearrange("p (s n) -> p s n", s=2)
        s_y = [sem("y_tile_loaded_0"), sem("y_tile_loaded_1")]
        s_g = [sem("gate_tile_loaded_0"), sem("gate_tile_loaded_1")]
        s_x2, s_out = [sem("x_loaded_again_0"), sem("x_loaded_again_1")], sem("out_stored")
        m_hi, m_sq, m_rt, m_sil, m_hh, m_o = made_by("act", "operand_high", "x2_squared", "x2_root", "silu_ready", "hidden_high", "out_copied")
        m_lo, m_ev, m_xt, m_res, m_n, m_nh, m_act, m_hl, m_dn = made_by(
            "dve", "operand_low", "merge_steps", "xT_ready", "residual_ready", "x2_rstd", "h2_steps", "hidden_ready", "hidden_low", "down_added")
        m_pe, m_ss, m_dd, m_op = made_by("pe", "xT_done", "x2_sums_done", "down_done", "out_transposed")

        BR = [("oa0", 4, "w_lru_o", 0, y_a, None), ("oa1", 3, "w_lru_o", 512, y_a, None), ("oa2", 3, "w_lru_o", 896, y_a, 0),
              ("oc0", 4, "w_att_o", 0, y_c, None), ("oc1", 4, "w_att_o", 512, y_c, 2),
              ("ob0", 4, "w_rw_o", 0, y_b, None), ("ob1", 4, "w_rw_o", 512, y_b, 1)]
        PARTS = (slice(0, 2), slice(2, 4))
        HALF = KT // 2
        NY = sum(kts for _, kts, *_ in BR)
        Y0 = [sum(kts for _, kts, *_ in BR[:g]) for g in range(len(BR))]
        M_EV = {"oa0": 1, "oa1": 1, "oa2": 2, "oc0": 1, "oc1": 3, "ob0": 1, "ob1": 3}
        EV0, _n = {}, 0
        for nm, *_ in BR:
            EV0[nm] = _n
            _n += 8 * M_EV[nm]
        EV_ALL = _n

        lam_s = made_by("dve", "lambda_steps")
        bias_t = sb("bias_t", [P, 4])
        eps_qk, eps_rms, eps_ln, one_b = bias_t[:, 0:1], bias_t[:, 0:1], bias_t[:, 1:2], bias_t[:, 2:3]
        lsc = sb("lsc", [P, 32])
        SOFT = 5 + 16 + 5 + 3
        VC = 24
        VZ = 5
        XP0, XM0 = 3, 6
        N_PAR_DMA = 7 + 2 + 1 + 4 + 2 + 1
        nsinks = sb("nsinks", [P, 16])

        def nsink(gg, t):
            return nsinks[:, bass.ds(gg * 4 + 2 * t, 2)]

        def halves2(ap):
            return ap.rearrange("p o (h n) -> p (o h) n", h=2)

        def lv_count(i, cc, lv, s):
            return i * (CHUNKS * (LEVELS - 1)) + (cc * (LEVELS - 1) + lv - 1) * PLACES + s

        def xu_count(i, cc, lv, s):
            last = LEVELS - 1
            turn = PLACES * (2 * (LEVELS - 2) + 1)
            return i * (CHUNKS // PLACES * turn) + cc * turn + ((lv - 1) * 2 * PLACES + 2 * s if lv < last else (last - 1) * 2 * PLACES + s)

        def round_of(cc):
            return [(PLACES * cc + s, s, 2 * s) for s in range(PLACES)]

        blockctx = ctx.enter_context(nc.Block())

        @blockctx.sync
        def _(sp):
            sp.dma_start(keep[:, :], a["consts"][:, 0:C_KEEP]).then_inc(s_const, 16)
            sp.wait_ge(p0_dve, upto(3))
            load_parameters(sp)
            for t in range(8):
                sp.dma_start(xs[:, t, :], a["x"][0, t * P:(t + 1) * P, :]).then_inc(s_x, 16)
            load_gains(sp)
            w_in, w_ada = a["w_in"][0], a["w_ada"][0]

            with sp.Fori(0, ADA0 // 4) as i:
                for k in range(4):
                    sp.wait_ge(ada_pe, upto(i * 4))
                    wait_alone(sp)
                    sp.dma_start(ada_w0[:, k, :, :], cols(w_ada, k * 256 + i * 1024, 256)).then_inc(s_ada[k], 16)
            sp.wait_ge(h_lo, upto(KT))
            sp.dma_start(rw["ar"][:, 0:2 * LEVELS * P], a["consts"][:, C_LV:C_N]).then_inc(s_mask, 16)
            sp.dma_start(rw["bn"][:, 0:256], a["consts"][:, C_AM:C_AM + 256]).then_inc(s_mask, 16)
            for c, (c0, n) in enumerate(((0, P), (P, P), (2 * P, 32))):
                load_block(sp, Block("lora", c), cols(w_in, COL_LORA + c0, n), n)
            w2, a2, g2 = a["rw_w2"][0], a["rw_a2"][0], a["rw_g2"][0]
            with sp.Fori(0, PAIRS) as i:
                for c in range(3):
                    load_block(sp, Block("rwkv", c, i), cols(w_in, COL_RW + c * RW_W + i * P, P), P)
                sp.wait_ge(r_g, upto(i))
                wait_alone(sp)
                sp.dma_start(rw["lw"][0:64, :], w2[:, bass.ds(i * P, P)]).then_inc(s_lw, 16)
                sp.dma_start(rw["lw"][64:128, :], a2[:, bass.ds(i * P, P)]).then_inc(s_lw, 16)
                sp.dma_start(rw["lg0"], g2[0:P, bass.ds(i * P, P)]).then_inc(s_lw, 16)
                sp.dma_start(rw["lg1"][0:32, :], g2[P:160, bass.ds(i * P, P)]).then_inc(s_lw, 16)
                for c in range(3):
                    load_block(sp, Block("rwkv", 3 + c, i), cols(w_in, COL_G + c * D + i * P, P), P)
            sp.wait_ge(v_post, upto(PAIRS * 6))
            sp.wait_ge(s_yb, upto(PAIRS * 16))
            sp.wait_ge(s_gst, upto(PAIRS * 48))
            with sp.Fori(0, TURNS["lru"]) as i:
                for u in range(2):
                    for c, c0 in enumerate((COL_LX, COL_LY)):
                        load_block(sp, Block("lru", 2 * u + c, i), cols(w_in, c0 + u * 80 + i * 160, 80), 80)
                    sp.wait_ge(ada_pe, upto(i * 2 + (ADA0 + u - 1)))
                    wait_alone(sp)
                    sp.dma_start(ada_w1[:, u, :, :], cols(w_ada, (ADA0 + u) * 256 + i * 512, 256)).then_inc(s_ada[u], 16)
                    sp.wait_ge(l_pe, upto(i * 2))
                    wait_alone(sp)
                    for nm, dst in (("lru_wa", lr["wa"]), ("lru_wx", lr["wx"])):
                        sp.dma_start(dst[0:80, 80 * u:80 * u + 80], a[nm][0, bass.ds(i * 2 + u, 1)].rearrange("o n m -> (o n) m")).then_inc(s_lw2[u], 16)
            sp.wait_ge(l_out, upto(LRU_N))
            sp.wait_ge(s_ya, upto(LRU_N * 16))
            sp.dma_start(at_["mask"], a["consts"][:, C_ATT:C_ATT + 512]).then_inc(s_am, 16)
            with sp.Fori(0, 2) as i:
                for g in range(2):
                    b = Block("att", 3 * g, i)
                    n = KT * P
                    dst = w_raw[:, b.slot, 0:n].rearrange("p (k s m) -> p k s m", k=KT, s=2)
                    sp.wait_ge(s_wsplit, upto(b.before - 1))
                    wait_alone(sp)
                    for s in range(2):
                        src = w_in[:, bass.ds(COL_K + 256 * s + 64 * g + i * 128, 64)].rearrange("(k p) m -> p k m", p=P)
                        sp.dma_start(dst[:, :, s, :], src).then_inc(s_w[b.slot] if s else s_kfirst, 16)
                    for t in range(2):
                        load_block(sp, Block("att", 3 * g + 1 + t, i), cols(w_in, COL_Q + 256 * g + P * t + i * 512, P), P)
            sp.wait_ge(s_yc, upto(8 * 16))

            def load_y(g, part):
                if g < len(BR):
                    _, kts, _, row0, y, _ = BR[g]
                    for k in range(kts)[part]:
                        n = Y0[g] + k
                        sp.wait_ge(m_lo, upto(n - 1))
                        sp.dma_start(yraw[:, n % 2, :], y[row0 + k * P:row0 + (k + 1) * P, :]).then_inc(s_y[n % 2], 16)
            for part in PARTS:
                load_y(0, part)
            for g, (nm, kts, wname, row0, _, gi) in enumerate(BR):
                wv = a[wname][0][row0:row0 + kts * P, :]
                for part in PARTS:
                    load_y(g + 1, part)
                    with sp.Fori(part.start, part.stop) as i:
                        for c in range(2):
                            load_block(sp, Block(nm, c, i), cols(wv, c * P + i * 2 * P, P), P)
                            if gi is not None:
                                sp.wait_ge(m_ev, upto(EV0[nm] + (i * 2 + c) * M_EV[nm]))
                                wait_alone(sp)
                                sp.dma_start(gtl[:, c, :], gates[bass.ds(gi * D + c * P + i * 2 * P, P), :]).then_inc(s_g[c], 16)
            for t in range(8):
                if t < 2:
                    sp.wait_ge(m_lo, upto(NY))
                else:
                    sp.wait_ge(m_pe, upto(t - 1))
                sp.dma_start(yraw[:, t % 2, :], a["x"][0, t * P:(t + 1) * P, :]).then_inc(s_x2[t % 2], 16)
            for half in range(2):
                wv = a["w_out"][0][half * 512:(half + 1) * 512, :]
                with sp.Fori(0, 4) as i:
                    for c in range(2):
                        load_block(sp, Block(f"wout{half}", c, i), cols(wv, c * P + i * 2 * P, P), P)
            wf, wo = a["w_ffn_in"][0], a["w_ffn_out"][0]

            def load_up(blk, tile, part):
                load_block(sp, blk, cols(wf, part * FF + tile * P, P), P)

            def load_down(blk, turn, part):
                rows = wo[bass.ds(turn * (2 * P), 2 * P), part * 512:(part + 1) * 512].rearrange("(k p) m -> p k m", p=P)
                load_block(sp, blk, rows, 512)
            for part in range(2):
                load_up(Block("ffn_first", part), 0, part)
            with sp.Fori(0, TURNS["ffn"]) as i:
                for part in range(2):
                    load_up(Block("ffn", part, i), i * 2 + 1, part)
                for part in range(2):
                    load_up(Block("ffn", 2 + part, i), i * 2 + 2, part)
                for part in range(2):
                    load_down(Block("ffn", 4 + part, i), i, part)
            for part in range(2):
                load_up(Block("ffn_last", part), 2 * TURNS["ffn"] + 1, part)
            for part in range(2):
                load_down(Block("ffn_last", 2 + part), TURNS["ffn"], part)
            for t in range(8):
                sp.wait_ge(m_o, upto(t + 1))
                sp.dma_start(out[0, t * P:(t + 1) * P, :], mix[:, t, :]).then_inc(s_out, 16)
            sp.wait_ge(s_out, 8 * 16)

        @blockctx.gpsimd
        def _(pool):
            seed(pool, "pool")

            def split_turns(name, sizes):
                with pool.Fori(0, TURNS[name]) as i:
                    for c, n in enumerate(sizes):
                        split_block(pool, Block(name, c, i), n)
            for c, n in enumerate((1024, 1024, 256)):
                split_block(pool, Block("lora", c), n)
            split_turns("rwkv", [1024] * 6)
            split_turns("lru", [640] * 4)
            with pool.Fori(0, TURNS["att"]) as i:
                for c in range(6):
                    if c % 3 == 0:
                        pool.wait_ge(s_kfirst, i * 32 + (c // 3 + 1) * 16)
                    split_block(pool, Block("att", c, i), 1024)
            for nm, kts, *_ in BR:
                split_turns(nm, [kts * P] * 2)
            for half in range(2):
                split_turns(f"wout{half}", [512] * 2)
            for c in range(2):
                split_block(pool, Block("ffn_first", c), 1024)
            split_turns("ffn", [1024] * 6)
            for c in range(4):
                split_block(pool, Block("ffn_last", c), 1024)

        @blockctx.tensor
        def _(pe):
            mm = nc.tensor.matmul
            seed(pe, "pe")

            pe.wait_ge(s_const, 16)
            pe.wait_ge(p0_dve, upto(3))
            pe.wait_ge(s_par, N_PAR_DMA * 16)
            for k, row in enumerate((row_rw, row_lru, row_mod)):
                pe.transpose(ps[:, 4 + k, 0:P], row, ident).then_inc(p0_pe, 1)
            pe.wait_ge(p0_act, upto(9))

            def ada_columns(w, bank):
                for c in range(2):
                    for k in range(KT):
                        ins = mm(ps[:, bank, c:c + 1], w[:, k, c * P:(c + 1) * P], mod[:, 48 + k:49 + k], start=k == 0, stop=k == KT - 1)
                ins.then_inc(ada_pe, 1)

            with pe.Fori(0, ADA0 // 4) as i:
                for k in range(4):
                    pe.wait_ge(s_ada[k], i * 16 + 16)
                    pe.wait_ge(ada_out, upto(i * 4 + max(k - 1, 0)))
                    ada_columns(ada_w0[:, k, :, :], 6 + k % 2)
            for k in range(KT):
                if k == 0:
                    pe.wait_ge(p0_dve, upto(16))
                if k >= 2:
                    pe.wait_ge(h_tmp, upto(k - 1))
                for t in range(8):
                    ins = pe.transpose(ps[:, 2 * (k % 2) + t // 4, (t % 4) * P:(t % 4 + 1) * P], xs[:, t, k * P:(k + 1) * P], ident)
                ins.then_inc(h_pe, 1)

            pe.wait_ge(h_lo, upto(KT))
            dense(pe, Block("lora", 0))
            dense(pe, Block("lora", 1))
            pe.wait_ge(a_xp, upto(1))
            dense(pe, Block("lora", 2), width=32)
            pe.wait_ge(a_wa, upto(3))

            def sums(dst_bank, lhs, x):
                for h in range(2):
                    ins = mm(ps[:, dst_bank + h, :], lhs, x[:, h * 512:(h + 1) * 512], start=True, stop=True)
                return ins

            with pe.Fori(0, PAIRS) as i:
                pe.wait_ge(a_y, upto(i * 8))
                pe.wait_ge(v_s, upto(i * 8))
                dense(pe, Block("rwkv", 0, i))
                dense(pe, Block("rwkv", 1, i))
                pe.wait_ge(a_xp, upto(XP0 + i * 3 + 1))
                dense(pe, Block("rwkv", 2, i))
                pe.wait_ge(s_lw, i * 64 + 64)
                pe.wait_ge(v_post, upto(i * 6))
                for h in range(2):
                    hs = slice(h * 512, (h + 1) * 512)
                    mm(ps[:, 4 + h, :], rw["lw"][0:64, :], rw["wa"][0:64, hs], start=True, stop=True)
                    ins = mm(ps[:, 6 + h, :], rw["lw"][64:128, :], rw["wa"][64:128, hs], start=True, stop=True)
                ins.then_inc(r_lwa, 1)
                pe.wait_ge(a_xp, upto(XP0 + i * 3 + 2))
                dense(pe, Block("rwkv", 3, i))
                pe.wait_ge(a_sa, upto(i * 2 + 1))
                pe.wait_ge(a_sqk, upto(i + 1))
                sums(4, headsum, rw["t2"]).then_inc(r_kks, 1)
                pe.wait_ge(a_xp, upto(XP0 + i * 3 + 3))
                dense(pe, Block("rwkv", 4, i))
                pe.wait_ge(a_sa, upto(i * 2 + 2))
                for h in range(2):
                    hs = slice(h * 512, (h + 1) * 512)
                    mm(ps[:, 6 + h, :], rw["lg0"], rw["g0"][:, hs], start=True, stop=False)
                    ins = mm(ps[:, 6 + h, :], rw["lg1"][0:32, :], rw["g1"][0:32, hs], start=False, stop=True)
                ins.then_inc(r_g, 1)
                pe.wait_ge(a_gate, upto(i * 3 + 1))
                dense(pe, Block("rwkv", 5, i))
                pe.wait_ge(a_rk, upto(i + 1))
                pe.wait_ge(v_c, upto(i * VC + 7))
                sums(4, headsum, rw["t1"]).then_inc(r_bon, 1)
                pe.wait_ge(v_c, upto(i * VC + VC))
                pe.wait_ge(v_fin, upto(i + 1))
                pe.wait_ge(a_g, upto(i + 1))
                pe.wait_ge(a_gate, upto(i * 3 + 3))
                for cc in range(CHUNKS // PLACES):
                    chunks = round_of(cc)
                    for c, s, b0 in chunks:
                        if c >= PLACES:
                            pe.wait_ge(a_y, upto(i * 8 + (c - PLACES + 1)))
                            pe.wait_ge(v_s, upto(i * 8 + (c - PLACES + 1)))
                        tok = slice(c * P, (c + 1) * P)
                        for q, src in enumerate((rw["v"][:, tok], al_v[:, c, :], rw["bn"][:, tok], rw["kt"][:, tok])):
                            ins = pe.transpose(ps[:, b0 + 1, q * P:(q + 1) * P], src, ident)
                        ins.then_inc(r_tk, 1)
                    for c, s, b0 in chunks:
                        tok = slice(c * P, (c + 1) * P)
                        for h in range(2):
                            hp = slice(64 * h, 64 * h + 64)
                            if h == 1:
                                pe.wait_ge(a_tk, upto((i * 8 + c) * 2 + 2))
                            mm(ps[:, b0 + h, 0:256], rw["bn"][hp, tok], ar[hp, c, :, :], start=True, stop=True)
                            ins = mm(ps[:, b0 + h, 256:512], rw["kt"][hp, tok], ar[hp, c, :, :], start=True, stop=True)
                        ins.then_inc(r_am, 1)
                    for c, s, b0 in chunks:
                        pe.wait_ge(v_am, upto((i * 8 + c) * 2 + 2))
                        for h in range(2):
                            hp = slice(64 * h, 64 * h + 64)
                            ins = mm(ps[:, b0 + h, 0:P], al_v[hp, c, :], rw["bn"][hp, c * P:(c + 1) * P], start=True, stop=True)
                        ins.then_inc(r_x0, 1)
                    for c, s, b0 in chunks:
                        pe.wait_ge(v_x0, upto((i * 8 + c) * 2 + 2))
                        for h in range(2):
                            ins = mm(ps[:, b0 + 1, h * 64:(h + 1) * 64], am[s][:, h, 2, :], tk[s][:, 0, 64 * h:64 * h + 64], start=True, stop=True)
                        ins.then_inc(r_ak, 1)
                    for lv in range(1, LEVELS):
                        for c, s, b0 in chunks:
                            if lv > 1:
                                pe.wait_ge(v_xu, upto(xu_count(i, cc, lv - 1, s) + 2))
                            for h in range(2):
                                ins = mm(ps[:, b0, h * P:(h + 1) * P], am[s][:, h, 0, :], xx[s][:, 0, h, :], start=True, stop=True)
                            ins.then_inc(r_y1, 1)
                        for c, s, b0 in chunks:
                            if lv == 1:
                                pe.wait_ge(a_ak, upto(i * 8 + c + 1))
                            pe.wait_ge(a_y1, upto(lv_count(i, cc, lv, s) + 1))
                            for h in range(2):
                                if lv < LEVELS - 1:
                                    mm(ps[:, b0 + 1, h * P:(h + 1) * P], xx[s][:, 1, h, :], y1[s][:, h, :], start=True, stop=True)
                            for h in range(2):
                                ins = mm(ps[:, b0 + 1, (2 + h) * P:(3 + h) * P], y1[s][:, h, :], xx[s][:, 1, h, :], start=True, stop=True)
                            ins.then_inc(r_xu, 1)
                    for c, s, b0 in chunks:
                        pe.wait_ge(v_xu, upto(xu_count(i, cc, LEVELS - 1, s) + 1))
                        for h in range(2):
                            ins = mm(ps[:, b0, h * P:(h + 1) * P], xx[s][:, 1, h, :], RR[s][:, h, :], start=True, stop=True)
                        ins.then_inc(r_uw, 1)
                    for c, s, b0 in chunks:
                        pe.wait_ge(a_uw, upto(i * 8 + c + 1))
                        for h in range(2):
                            hp = slice(64 * h, 64 * h + 64)
                            mm(ps[hp, b0 + 1, 0:P], uw[s][:, h, 64:128], am[s][:, h, 1, :], start=True, stop=True)
                        for h in range(2):
                            hp = slice(64 * h, 64 * h + 64)
                            ins = mm(ps[hp, b0 + 1, P + 64 * h:P + 64 * h + 64], uw[s][:, h, 64:128], tk[s][:, 2, hp], start=True, stop=True)
                        ins.then_inc(r_gq, 1)
                    for c, s, b0 in chunks:
                        pe.wait_ge(v_q, upto((i * 8 + c) * 2 + 2))
                        if c == 0:
                            pe.wait_ge(v_zero, upto(VZ + i + 1))
                        else:
                            pe.wait_ge(v_s, upto(i * 8 + c))
                        mm(ps[:, b0, 0:P], qq[:, s, :], SS[:, c % 2, :], start=True, stop=False)
                        for h in range(2):
                            hp = slice(64 * h, 64 * h + 64)
                            mm(ps[hp, b0, hp], tk[s][:, 2, hp], uw[s][:, h, 0:64], start=False, stop=False)
                            ins = mm(ps[hp, b0, hp], tk[s][:, 3, hp], tk[s][:, 0, hp], start=False, stop=True)
                        ins.then_inc(r_s, 1)
                        mm(ps[:, b0 + 1, 0:P], SS[:, c % 2, :], gt[s], start=True, stop=False)
                        for h in range(2):
                            hp = slice(64 * h, 64 * h + 64)
                            mm(ps[hp, b0 + 1, 0:P], uw[s][:, h, 0:64], am[s][:, h, 1, :], start=False, stop=False)
                            ins = mm(ps[hp, b0 + 1, 0:P], tk[s][:, 0, hp], am[s][:, h, 3, :], start=False, stop=True)
                        ins.then_inc(r_y, 1)
                pe.wait_ge(a_y, upto(i * 8 + 8))
                pe.wait_ge(v_s, upto(i * 8 + 8))
                sums(4, headsum, rw["A"]).then_inc(r_mean, 1)
                pe.wait_ge(a_ysq, upto(i + 1))
                sums(6, headsum, rw["t1"]).then_inc(r_var, 1)

            pe.wait_ge(v_post, upto(PAIRS * 6))
            with pe.Fori(0, TURNS["lru"]) as i:
                for u in range(2):
                    n = i * 2 + u
                    pe.wait_ge(l_x, upto(n))
                    dense(pe, Block("lru", 2 * u, i), width=80)
                    pe.wait_ge(s_ada[u], i * 16 + (ADA0 // 4 * 16 + 16))
                    pe.wait_ge(l_sa, upto(n * 2))
                    ada_columns(ada_w1[:, u, :, :], 4)
                    pe.wait_ge(l_gy, upto(n))
                    dense(pe, Block("lru", 2 * u + 1, i), width=80)
                    pe.wait_ge(l_cv, upto(n * 4 + 4))
                    pe.wait_ge(ada_out, upto(n + (ADA0 + 1)))
                    pe.wait_ge(s_lw2[u], i * 32 + 32)
                    for q, w in enumerate(("wa", "wx")):
                        for h in range(2):
                            ins = mm(ps[0:80, 4 + 2 * q + h, :], lr[w][0:80, 80 * u:80 * u + 80], lr["xa"][0:80, h * 512:(h + 1) * 512], start=True, stop=True)
                    ins.then_inc(l_pe, 1)

            pe.wait_ge(l_out, upto(LRU_N))
            with pe.Fori(0, TURNS["att"]) as i:
                for g in range(2):
                    gg = i * 2 + g
                    for c in range(3):
                        pe.wait_ge(t_cp, upto(gg * 3 + c))
                        if c == 0:
                            pe.wait_ge(t_oc, upto(gg * 16))
                        dense(pe, Block("att", 3 * g + c, i))
                        if c == 0:
                            pe.wait_ge(t_cp, upto(gg * 3 + 1))
                            for n in range(8):
                                ins = pe.transpose(ps[:, 6 + n // 4, (n % 4) * P:(n % 4 + 1) * P], at_["kvt"][:, n * P:(n + 1) * P], ident)
                            ins.then_inc(t_vt, 1)
                        if c > 0:
                            pe.wait_ge(t_sq, upto(gg * 3 + c))
                            pe.wait_ge(t_rt, upto(gg * 3 + c - 1))
                            sums(4, headsum, at_["t1"]).then_inc(t_ns, 1)
                    pe.wait_ge(t_sq, upto(gg * 3 + 3))
                    pe.wait_ge(t_rt, upto(gg * 3 + 2))
                    sums(4, headsum, at_["t1"]).then_inc(t_ns, 1)
                    pe.wait_ge(t_rt, upto(gg * 3 + 3))
                    pe.wait_ge(t_n, upto(gg * 3 + 3))
                    pe.wait_ge(t_k2, upto(gg + 1))
                    pe.wait_ge(t_v, upto(gg + 1))
                    for tick in range(16 + 3):
                        if tick < 16:
                            u, t, n = tick, tick // 8, tick % 8
                            if u >= 2:
                                pe.wait_ge(t_d, upto((gg * 16 + u - 2) * 4 + 1))
                            for h in range(2):
                                hp = slice(64 * h, 64 * h + 64)
                                ins = mm(ps[:, 4 - 2 * (u % 2) + h, 0:256], aq[hp, t, n * P:(n + 1) * P], ak[hp, g, n * P:n * P + 256], start=True, stop=True)
                            ins.then_inc(t_sc, 1)
                        if 0 <= tick - 2 < 16:
                            u = tick - 2
                            pe.wait_ge(t_p, upto((gg * 16 + u) * 2 + 2))
                            if u >= 2:
                                pe.wait_ge(t_ptc, upto(gg * 16 + u - 1))
                            for h in range(2):
                                for kb in range(2):
                                    ins = pe.transpose(ps[:, 6 + u % 2, (2 * h + kb) * P:(2 * h + kb + 1) * P], asc[:, u % 4, h, kb * P:(kb + 1) * P], ident)
                            ins.then_inc(t_pt, 1)
                        if 0 <= tick - 3 < 16:
                            u, t, n = tick - 3, (tick - 3) // 8, (tick - 3) % 8
                            pe.wait_ge(t_ptc, upto(gg * 16 + u + 1))
                            if u >= 2:
                                pe.wait_ge(t_oc, upto(gg * 16 + u - 1))
                            for h in range(2):
                                hp = slice(64 * h, 64 * h + 64)
                                for kb in range(2):
                                    ins = mm(ps[hp, u % 2, 0:P], av[:, g, n + kb, :], apt[:, u % 4, (2 * h + kb) * P:(2 * h + kb + 1) * P], start=kb == 0, stop=kb == 1)
                            ins.then_inc(t_o, 1)

            pe.wait_ge(t_oc, upto(64))
            pe.wait_ge(t_ptc, upto(64))
            yn = 0
            for g, (nm, kts, *_) in enumerate(BR):
                yn += kts
                pe.wait_ge(m_lo, upto(yn))
                per = M_EV[nm]
                with pe.Fori(0, 4) as i:
                    for c in range(2):
                        pe.wait_ge(m_ev, upto(i * (2 * per) + EV0[nm]))
                        dense(pe, Block(nm, c, i), tiles=kts, first=HALF * (g % 2))
            for t in range(8):
                pe.wait_ge(s_x2[t % 2], 16 * (t // 2 + 1))
                if t >= 2:
                    pe.wait_ge(m_xt, upto(t - 1))
                for k in range(KT):
                    ins = pe.transpose(ps[:, 4 + 2 * (t % 2) + k // 4, (k % 4) * P:(k % 4 + 1) * P], yraw[:, t % 2, k * P:(k + 1) * P], ident)
                ins.then_inc(m_pe, 1)
            for half in range(2):
                pe.wait_ge(m_lo, upto(NY + HALF * (half + 1)))
                first = (HALF * (len(BR) % 2) + HALF * half) % KT
                with pe.Fori(0, 4) as i:
                    for c in range(2):
                        if half == 0:
                            pe.wait_ge(m_ev, upto(EV_ALL))
                        pe.wait_ge(m_res, upto(half * 8 + i * 2))
                        dense(pe, Block(f"wout{half}", c, i), tiles=HALF, first=first)
            for k in range(KT):
                pe.wait_ge(m_sq, upto(k + 1))
                for h in range(2):
                    ins = mm(ps[:, 4 + h, :], ones, mt[:, k % 2, h * 512:(h + 1) * 512], start=k == 0, stop=k == KT - 1)
                ins.then_inc(m_ss, 1)
            pe.wait_ge(m_nh, upto(KT * 2))

            def up(blk_gate, blk_up, tile):
                pe.wait_ge(m_sil, upto(tile))
                dense(pe, blk_gate)
                pe.wait_ge(m_act, upto(tile))
                dense(pe, blk_up)

            def down(name, c0, i, turn):
                pe.wait_ge(m_hl, upto(turn * 2 + 2))
                for m in range(8):
                    blk = Block(name, c0 + m // 4, i)
                    if m % 4 == 0:
                        pe.wait_ge(s_wsplit, upto(blk.before + 1))
                    if m < 2:
                        pe.wait_ge(m_dn, upto(turn * 8))
                    else:
                        pe.wait_ge(m_dn, upto(turn * 8 + m - 1))
                    dst = [ps[:, 4 + 2 * (m % 2) + h, :] for h in range(2)]
                    for k in range(FF_GROUP):
                        at = k * 512 + (m % 4) * P
                        w = [t[:, blk.slot, at:at + P] for t in (w_hi, w_lo)]
                        x = [[t[:, k, h * 512:(h + 1) * 512] for h in range(2)] for t in (hid_hi, hid_lo)]
                        ins = three_passes(dst, w, x, k == 0, k == FF_GROUP - 1)
                    ins.then_inc(s_dense if m % 4 == 3 else m_dd, 1)
            up(Block("ffn_first", 0), Block("ffn_first", 1), 0)
            with pe.Fori(0, TURNS["ffn"]) as i:
                up(Block("ffn", 0, i), Block("ffn", 1, i), i * 2 + 1)
                up(Block("ffn", 2, i), Block("ffn", 3, i), i * 2 + 2)
                down("ffn", 4, i, i)
            up(Block("ffn_last", 0), Block("ffn_last", 1), 2 * TURNS["ffn"] + 1)
            down("ffn_last", 2, 0, TURNS["ffn"])
            pe.wait_ge(m_dn, upto((TURNS["ffn"] + 1) * 8))
            for t in range(8):
                if t >= 2:
                    pe.wait_ge(m_o, upto(t - 1))
                for k in range(KT):
                    ins = pe.transpose(ps[:, 4 + 2 * (t % 2) + k // 4, (k % 4) * P:(k % 4 + 1) * P], x2[:, k, t * P:(t + 1) * P], ident)
                ins.then_inc(m_op, 1)

        @blockctx.scalar
        def _(act):
            fn = nc.scalar.activation
            seed(act, "act")
            for t in range(8):
                act.wait_ge(s_x, 16 * 8)
                if t >= 2:
                    act.wait_ge(p0_act, upto(t - 1))
                fn(sq0[:, t % 2, :], xs[:, t, :], ACT.Square, accum_out=sumsq[:, t:t + 1]).then_inc(p0_act, 1)
            act.wait_ge(p0_dve, upto(6))
            fn(mod[:, 48:56], mod[:, 48:56], ACT.Silu).then_inc(p0_act, 1)
            fn(rate2[0:80, :], rate[0:80, :], ACT.Exp, scale=-1.0).then_inc(p0_act, 1)
            act.wait_ge(p0_dve, upto(7))
            fn(rstd, rstd, ACT.Sqrt).then_inc(p0_act, 1)
            for k in range(KT):
                act.wait_ge(h_tmp, upto(k + 1))
                fn(x_hi[:, k, :], h_tmpb[:, k % 2, :], ACT.Copy).then_inc(h_hi, 1)

            xp = rw["xp"]

            def copy_stream(blk, count, mixed, width=P):
                act.wait_ge(s_dense, upto(blk.before + 1))
                act.wait_ge(v_mix, upto(mixed))
                fn(halves(xp[0:width, 1:T + 1]), ps[0:width, 2 * blk.slot:2 * blk.slot + 2, :], ACT.Copy).then_inc(a_xp, 1)

            act.wait_ge(v_zero, upto(VZ))
            for c, width in enumerate((P, P, 32)):
                copy_stream(Block("lora", c), c, 2 * c, width)
                act.wait_ge(v_mix, upto(2 * c + 2))
                if c == 0:
                    fn(rw["wa"][0:64, :], rw["wa"][0:64, :], ACT.Tanh).then_inc(a_wa, 1)
                else:
                    t = rw["g0"] if c == 1 else rw["g1"][0:32, :]
                    fn(t, t, ACT.Sigmoid).then_inc(a_wa, 1)

            with act.Fori(0, PAIRS) as i:
                par = lambda c: rw_par[:, bass.ds(i + c, 1)]
                for s in range(3):
                    copy_stream(Block("rwkv", s, i), None, XM0 + i * 6 + 2 * s)

                def gate(c):
                    blk = Block("rwkv", 3 + c, i)
                    act.wait_ge(s_dense, upto(blk.before + 1))
                    act.wait_ge(s_gst, upto(i * 48 + c * 16))
                    fn(halves(rw["gs"]), pair_of(blk.slot), ACT.Sigmoid).then_inc(a_gate, 1)
                    act.wait_ge(a_gate, upto(i * 3 + c + 1))
                    act.dma_start(gates[bass.ds(c * D + i * P, P), :], rw["gs"]).then_inc(s_gst, 16)

                act.wait_ge(r_lwa, upto(i + 1))
                fn(halves(rw["sig"]), ps[:, 4:6, :], ACT.Sigmoid, bias=par(PR_W0)).then_inc(a_sa, 1)
                fn(halves(rw["A"]), ps[:, 6:8, :], ACT.Sigmoid, bias=par(PR_A0)).then_inc(a_sa, 1)
                act.wait_ge(v_kk, upto(i + 1))
                act.wait_ge(s_yb, upto(i * 16))
                fn(rw["t2"], rw["t1"], ACT.Square).then_inc(a_sqk, 1)
                gate(0)
                act.wait_ge(r_kks, upto(i + 1))
                fn(halves(rw["t2"]), ps[:, 4:6, :], ACT.Sqrt).then_inc(a_rk, 1)
                gate(1)
                act.wait_ge(r_g, upto(i + 1))
                fn(halves(rw["g"]), ps[:, 6:8, :], ACT.Copy).then_inc(a_g, 1)
                act.wait_ge(v_c, upto(i * VC + 18))
                fn(rw["ff"], rw["df"][:, 0:8], ACT.Exp, scale=-DECAY).then_inc(a_f, 1)
                act.wait_ge(v_c, upto(i * VC + 20))
                fn(rw["sig"], rw["sig"], ACT.Exp, scale=-DECAY).then_inc(a_exp, 1)
                fn(rw["t2"], rw["L"], ACT.Exp, scale=-DECAY).then_inc(a_exp, 1)
                act.wait_ge(a_exp, upto(i * 3 + 2))
                fn(rw["L"], rw["L"], ACT.Exp, scale=DECAY).then_inc(a_exp, 1)
                gate(2)
                for cc in range(CHUNKS // PLACES):
                    chunks = round_of(cc)
                    for c, s, b0 in chunks:
                        act.wait_ge(r_tk, upto(i * 8 + c + 1))
                        fn(tk[s], ps[:, b0 + 1, :].rearrange("p (q n) -> p q n", q=4), ACT.Copy).then_inc(a_tk, 1)
                        fn(RR[s][:, :, 64:128], ps[:, b0 + 1, P:2 * P].rearrange("p (h n) -> p h n", h=2), ACT.Copy).then_inc(a_tk, 1)
                        fn(xx[s].rearrange("p o h n -> p (o h) n"), ident.unsqueeze(1).broadcast_to([P, 4, P]), ACT.Copy).then_inc(a_xi, 1)
                    for c, s, b0 in chunks:
                        act.wait_ge(r_ak, upto(i * 8 + c + 1))
                        fn(RR[s][:, :, 0:64], ps[:, b0 + 1, 0:P].rearrange("p (h n) -> p h n", h=2), ACT.Copy).then_inc(a_ak, 1)
                    for lv in range(1, LEVELS):
                        for c, s, b0 in chunks:
                            act.wait_ge(r_y1, upto(lv_count(i, cc, lv, s) + 1))
                            fn(blocks_of(y1[s], lv, 0), blocks_of(per_head(ps[:, b0, 0:256]), lv, 0), ACT.Copy).then_inc(a_y1, 1)
                    for c, s, b0 in chunks:
                        act.wait_ge(r_uw, upto(i * 8 + c + 1))
                        fn(uw[s], ps[:, b0, 0:256].rearrange("p (h n) -> p h n", h=2), ACT.Copy).then_inc(a_uw, 1)
                    for c, s, b0 in chunks:
                        act.wait_ge(r_y, upto(i * 8 + c + 1))
                        fn(rw["A"][:, c * P:(c + 1) * P], ps[:, b0 + 1, 0:P], ACT.Copy).then_inc(a_y, 1)
                act.wait_ge(v_post, upto(i * 6 + 1))
                fn(rw["t1"], rw["t2"], ACT.Square).then_inc(a_ysq, 1)
                act.wait_ge(r_var, upto(i + 1))
                fn(halves(rw["t1"]), ps[:, 6:8, :], ACT.Sqrt, scale=1.0 / RW_H, bias=eps_ln).then_inc(a_yr, 1)
                act.wait_ge(v_post, upto(i * 6 + 6))
                act.dma_start(y_b[bass.ds(i * P, P), :], rw["t2"]).then_inc(s_yb, 16)

            with act.Fori(0, TURNS["lru"]) as i:
                for u in range(2):
                    n = i * 2 + u
                    lp = lambda c: lru_par[0:80, bass.ds(n + c, 1)]
                    act.wait_ge(s_dense, upto(Block("lru", 2 * u, i).before + 1))
                    act.wait_ge(l_cv, upto(n * 4))
                    act.wait_ge(l_z, upto(1))
                    fn(halves(lr["xp"][0:80, 3:T + 3]), pair_of(Block("lru", 2 * u, i).slot)[0:80], ACT.Copy).then_inc(l_x, 1)
                    act.wait_ge(l_pe, upto(n + 1))
                    act.wait_ge(l_u, upto(n * 3))
                    fn(halves(lr["ga"][0:80]), ps[0:80, 4:6, :], ACT.Sigmoid, bias=lp(LP_BA)).then_inc(l_sa, 1)
                    fn(halves(lr["gx"][0:80]), ps[0:80, 6:8, :], ACT.Sigmoid, bias=lp(LP_BX)).then_inc(l_sa, 1)
                    act.wait_ge(l_sa, upto(n * 2 + 2))
                    fn(lr["a2"][0:80], lr["ga"][0:80], ACT.Exp, scale=rate2[0:80, bass.ds(n, 1)]).then_inc(l_exp, 1)
                    fn(lr["aa"][0:80], lr["ga"][0:80], ACT.Exp, scale=rate[0:80, bass.ds(n, 1)]).then_inc(l_exp, 1)
                    act.wait_ge(l_sq, upto(n + 1))
                    fn(lr["a2"][0:80], lr["a2"][0:80], ACT.Sqrt, scale=-1.0, bias=one_b[0:80, :]).then_inc(l_rt, 1)
                    act.wait_ge(l_out, upto(n))
                    fn(halves(lr["gy"][0:80]), pair_of(Block("lru", 2 * u + 1, i).slot)[0:80], ACT.Gelu_apprx_tanh).then_inc(l_gy, 1)
                    act.wait_ge(l_out, upto(n + 1))
                    act.dma_start(y_a[bass.ds(n * 80, 80), :], lr["ya"][0:80]).then_inc(s_ya, 16)

            act.wait_ge(t_z, upto(4))
            t1, t2 = at_["t1"], at_["t2"]
            with act.Fori(0, TURNS["att"]) as i:
                for g in range(2):
                    gg = i * 2 + g
                    for c in range(3):
                        blk = Block("att", 3 * g + c, i)
                        tile = at_["kvt"] if c == 0 else aq[:, c - 1, :]
                        act.wait_ge(s_dense, upto(blk.before + 1))
                        fn(halves(tile), pair_of(blk.slot), ACT.Copy).then_inc(t_cp, 1)
                        act.wait_ge(t_cp, upto(gg * 3 + c + 1))
                        if c > 0:
                            act.wait_ge(t_ns, upto(gg * 3 + c))
                            fn(halves(t2), ps[:, 4:6, :], ACT.Sqrt, scale=1.0 / HEAD, bias=eps_qk).then_inc(t_rt, 1)
                            if c == 1:
                                act.wait_ge(t_vt, upto(gg + 1))
                                fn(av[:, g, 1:9, :], ps[:, 6:8, :].rearrange("p b (n e) -> p (b n) e", e=P)[:, :, 64:128], ACT.Copy).then_inc(t_v, 1)
                            act.wait_ge(t_n, upto(gg * 3 + c))
                            if c == 1:
                                fn(ak[64:128, g, P:T + P], ak[0:64, g, P:T + P], ACT.Copy).then_inc(t_k2, 1)
                        fn(t1, tile, ACT.Square).then_inc(t_sq, 1)
                    act.wait_ge(t_ns, upto(gg * 3 + 3))
                    fn(halves(t2), ps[:, 4:6, :], ACT.Sqrt, scale=1.0 / HEAD, bias=eps_qk).then_inc(t_rt, 1)
                    for tick in range(16 + 3):
                        if tick < 16:
                            u = tick
                            act.wait_ge(t_d, upto((gg * 16 + u) * 4 + 4))
                            sm = asm[:, u % 4, :]
                            for h in range(2):
                                fn(asc[:, u % 4, h, :], asc[:, u % 4, h, :], ACT.Exp, bias=sm[:, 2 + h:3 + h], accum_out=sm[:, 4 + h:5 + h]).then_inc(t_e, 1)
                            fn(sm[:, 6:8], sm[:, 6:8], ACT.Exp).then_inc(t_e, 1)
                        if 0 <= tick - 2 < 16:
                            u = tick - 2
                            act.wait_ge(t_pt, upto(gg * 16 + u + 1))
                            fn(apt[:, u % 4, :], ps[:, 6 + u % 2, :], ACT.Copy).then_inc(t_ptc, 1)
                        if 0 <= tick - 3 < 16:
                            u, t, n = tick - 3, (tick - 3) // 8, (tick - 3) % 8
                            act.wait_ge(t_o, upto(gg * 16 + u + 1))
                            if n == 0:
                                act.wait_ge(s_yc, upto((gg * 2 + t) * 16))
                            fn(ayc[:, t, n * P:(n + 1) * P], ps[:, u % 2, 0:P], ACT.Copy).then_inc(t_oc, 1)
                            if n == 7:
                                act.wait_ge(t_oc, upto(gg * 16 + u + 1))
                                act.dma_start(y_c[bass.ds((gg * 2 + t) * P, P), :], ayc[:, t, :]).then_inc(s_yc, 16)

            yn = 0
            for g, (nm, kts, *_) in enumerate(BR):
                act.wait_ge(s_dense, upto(Block(BR[max(g - 1, 0)][0], 0).before))
                for k in range(kts):
                    act.wait_ge(s_y[yn % 2], 16 * (yn // 2 + 1))
                    fn(x_hi[:, HALF * (g % 2) + k, :], yraw[:, yn % 2, :], ACT.Copy).then_inc(m_hi, 1)
                    yn += 1
            for m in range(KT):
                at = (HALF * (len(BR) % 2) + m) % KT
                if m == 0:
                    act.wait_ge(s_dense, upto(Block("ob1", 0).before))
                if m == HALF:
                    act.wait_ge(s_dense, upto(Block("wout0", 0).before))
                act.wait_ge(m_ev, upto(EV0["ob1"] + 3 * (m + 1)))
                fn(x_hi[:, at, :], mix[:, m, :], ACT.Copy).then_inc(m_hi, 1)
            act.wait_ge(m_ev, upto(EV_ALL))
            for t in range(8):
                act.wait_ge(m_pe, upto(t + 1))
                fn(x2[:, :, t * P:(t + 1) * P], ps[:, 4 + 2 * (t % 2):6 + 2 * (t % 2), :].rearrange("p b (k n) -> p (b k) n", n=P), ACT.Copy).then_inc(m_xt, 1)
            for k in range(KT):
                act.wait_ge(m_res, upto(KT + k + 1))
                if k >= 2:
                    act.wait_ge(m_ss, upto(k - 1))
                fn(mt[:, k % 2, :], x2[:, k, :], ACT.Square).then_inc(m_sq, 1)
            act.wait_ge(m_ss, upto(KT))
            fn(halves(yraw[:, 0, :]), ps[:, 4:6, :], ACT.Sqrt, scale=1.0 / D, bias=eps_rms).then_inc(m_rt, 1)
            for k in range(KT):
                act.wait_ge(m_nh, upto(2 * k + 1))
                fn(x_hi[:, k, :], mt[:, k % 2, :], ACT.Identity, bias=mod[:, MOD_SH2 + k:MOD_SH2 + k + 1]).then_inc(m_hi, 1)

            def hidden(blk, tile, t):
                act.wait_ge(s_dense, upto(blk.before + 1))
                act.wait_ge(m_act, upto(tile))
                fn(halves(gtl[:, 0, :]), pair_of(blk.slot), ACT.Silu).then_inc(m_sil, 1)

            def hidden_high(tile, t):
                act.wait_ge(m_act, upto(tile + 1))
                fn(hid_hi[:, t, :], mt[:, t, :], ACT.Copy).then_inc(m_hh, 1)
            hidden(Block("ffn_first", 0), 0, 0)
            hidden_high(0, 0)
            with act.Fori(0, TURNS["ffn"]) as i:
                hidden(Block("ffn", 0, i), i * 2 + 1, 1)
                hidden_high(i * 2 + 1, 1)
                hidden(Block("ffn", 2, i), i * 2 + 2, 0)
                act.wait_ge(s_dense, upto(Block("ffn", 5, i).before + 1))
                hidden_high(i * 2 + 2, 0)
            hidden(Block("ffn_last", 0), 2 * TURNS["ffn"] + 1, 1)
            hidden_high(2 * TURNS["ffn"] + 1, 1)
            for t in range(8):
                act.wait_ge(m_op, upto(t + 1))
                fn(halves(mix[:, t, :]), ps[:, 4 + 2 * (t % 2):6 + 2 * (t % 2), :], ACT.Copy).then_inc(m_o, 1)

        @blockctx.vector
        def _(dve):
            v = nc.vector
            seed(dve, "dve")
            steps = [0]

            def step(ins):
                steps[0] += 1
                ins.then_inc(p0_dve, 1)
                dve.wait_ge(p0_dve, upto(steps[0]))

            for row in (row_rw, row_lru, row_mod):
                step(v.memset(row, 0.0))
            for k, dst in enumerate((rw_par, lru_par)):
                dve.wait_ge(p0_pe, upto(k + 1))
                step(v.tensor_copy(dst[:, :], ps[:, 4 + k, 0:P]))
            dve.wait_ge(p0_pe, upto(3))
            lam = lru_par[0:80, LP_LAM:LP_LAM + 16]
            v.tensor_scalar(rate[0:80, :], lam, -1.0, None, ALU.mult).then_inc(lam_s, 1)
            dve.wait_ge(lam_s, upto(1))
            v.tensor_tensor(rate[0:80, :], rate[0:80, :], lam, ALU.max).then_inc(lam_s, 1)
            dve.wait_ge(lam_s, upto(2))
            step(v.tensor_copy(mod[:, :], ps[:, 6, 0:56]))
            dve.wait_ge(p0_act, upto(9))
            step(v.tensor_scalar(rstd, sumsq, 1.0 / D, 1e-6, ALU.mult, ALU.add))
            dve.wait_ge(p0_act, upto(11))
            step(v.reciprocal(rstd, rstd))
            for t in range(8):
                step(v.tensor_scalar(xs[:, t, :], xs[:, t, :], rstd[:, t:t + 1], None, ALU.mult))
            e, z, z2, acc = rate2[0:80, :], small[0:80, 66:82], small[0:80, 82:96], None
            z2 = lsc[0:80, 0:16]
            acc = lsc[0:80, 16:32]
            step(v.tensor_scalar(z, e, 2.0, None, ALU.add))
            step(v.reciprocal(z, z))
            step(v.tensor_tensor(z, z, e, ALU.mult))
            step(v.tensor_tensor(z2, z, z, ALU.mult))
            step(v.tensor_scalar(acc, z2, 2.0 / 19, 2.0 / 17, ALU.mult, ALU.add))
            for m in (15, 13, 11, 9, 7, 5, 3, 1):
                step(v.tensor_tensor(acc, acc, z2, ALU.mult))
                step(v.tensor_scalar(acc, acc, 2.0 / m, None, ALU.add))
            step(v.tensor_tensor(acc, acc, z, ALU.mult))
            step(v.tensor_scalar(z, lam, -1.0, 0.0, ALU.mult, ALU.max))
            step(v.tensor_tensor(acc, acc, z, ALU.add))
            step(v.tensor_scalar(rate[0:80, :], acc, -8.0, None, ALU.mult))
            step(v.tensor_scalar(rate2[0:80, :], acc, -16.0, None, ALU.mult))
            for k, val in enumerate((1e-6, 64e-5, 1.0)):
                step(v.memset(bias_t[:, k:k + 1], val))
            assert steps[0] == 6 + 1 + 1 + 8 + SOFT, steps[0]

            def ada_pair(bank, n):
                dve.wait_ge(ada_pe, upto(n + 1))
                cols2 = mod[:, bass.ds(n * 2, 2)]
                v.tensor_tensor(cols2, ps[:, bank, 0:2], cols2, ALU.add).then_inc(ada_out, 1)

            with dve.Fori(0, ADA0 // 4) as i:
                for k in range(4):
                    ada_pair(6 + k % 2, i * 4 + k)
            dve.wait_ge(ada_out, upto(ADA0))
            v.tensor_scalar(mod[:, MOD_SC1:MOD_SC1 + 8], mod[:, MOD_SC1:MOD_SC1 + 8], 1.0, None, ALU.add).then_inc(ada_fix, 1)
            dve.wait_ge(ada_fix, upto(1))
            for k in range(KT):
                dve.wait_ge(h_pe, upto(k + 1))
                tmp = h_tmpb[:, k % 2, :]
                if k >= 2:
                    dve.wait_ge(h_lo, upto(k - 1))
                v.tensor_scalar(halves(tmp), pair_of(k % 2), mod[:, MOD_SC1 + k:MOD_SC1 + k + 1], mod[:, MOD_SH1 + k:MOD_SH1 + k + 1], ALU.mult, ALU.add).then_inc(h_tmp, 1)
                dve.wait_ge(h_hi, upto(k + 1))
                v.tensor_tensor(x_lo[:, k, :], tmp, x_hi[:, k, :].bitcast(F32), ALU.subtract).then_inc(h_lo, 1)

            dve.wait_ge(h_lo, upto(KT))
            v.memset(rw["xp"][:, 0:1], 0.0).then_inc(v_zero, 1)
            v.memset(rw["q"], 0.0).then_inc(v_zero, 1)
            for s in (0, 1, 3):
                v.memset(places[s]["y1"], 0.0).then_inc(v_zero, 1)
            dve.wait_ge(s_mask, 32)
            v.tensor_copy(hid_lo[:, :, :].rearrange("p a n -> p (a n)")[:, 0:2 * LEVELS * P], rw["ar"][:, 0:2 * LEVELS * P]).then_inc(mask_ready, 1)
            v.tensor_copy(masks[:, 0:256], rw["bn"][:, 0:256]).then_inc(mask_ready, 1)
            dve.wait_ge(mask_ready, upto(2))

            def level_mask(lv, o):
                m = lv_mask[:, (2 * lv + o) * P:(2 * lv + o + 1) * P].bitcast(I32).unsqueeze(1).broadcast_to([P, 2, P])
                return blocks_of(m, lv, o)
            xp = rw["xp"]

            def mix_stream(copied, mixed, dst, mu, width=P, view=None):
                dve.wait_ge(a_xp, upto(copied))
                x0, x1, t = xp[0:width, 0:T], xp[0:width, 1:T + 1], rw["t1"][0:width, :]
                v.tensor_tensor(t, x0, x1, ALU.subtract).then_inc(v_mix, 1)
                dve.wait_ge(v_mix, upto(mixed + 1))
                if view is not None:
                    t, x1 = view(t), view(x1)
                v.scalar_tensor_tensor(dst, t, mu, x1, ALU.mult, ALU.add).then_inc(v_mix, 1)
                dve.wait_ge(v_mix, upto(mixed + 2))
            for c, (dst, width) in enumerate(((rw["wa"], P), (rw["g0"], P), (rw["g1"][0:32, :], 32))):
                mix_stream(c + 1, 2 * c, dst, rw_par[0:width, PR_MU_WA + c:PR_MU_WA + c + 1], width)

            with dve.Fori(0, PAIRS) as i:
                par = lambda c: rw_par[:, bass.ds(i + c, 1)]
                count = [0]

                def prep(ins, wait=True):
                    count[0] += 1
                    ins.then_inc(v_c, 1)
                    if wait:
                        dve.wait_ge(v_c, upto(i * VC + count[0]))

                for s, (dst, view) in enumerate(((rt_v, chunked), (rw["kt"], None), (rw["v"], None))):
                    mix_stream(XP0 + i * 3 + s + 1, XM0 + i * 6 + 2 * s, dst, par(PR_MU + 8 * s), view=view)
                t1, t2, A, L, sig, bn, kt = (rw[n] for n in ("t1", "t2", "A", "L", "sig", "bn", "kt"))
                v.tensor_scalar(t1, kt, par(PR_KK), None, ALU.mult).then_inc(v_kk, 1)
                v.memset(SS[:, 0, :], 0.0).then_inc(v_zero, 1)
                dve.wait_ge(a_sa, upto(i * 2 + 2))
                prep(v.tensor_scalar(bn, A, -1.0, par(PR_KA), ALU.add, ALU.mult))
                dve.wait_ge(a_rk, upto(i + 1))
                prep(v.tensor_scalar(t2, t2, 1e-12, None, ALU.max))
                prep(v.reciprocal(t2, t2))
                prep(v.tensor_tensor(al_v, chunked(t1), chunked(t2), ALU.mult))
                prep(v.scalar_tensor_tensor(kt, bn, 1.0, kt, ALU.add, ALU.mult))
                prep(v.scalar_tensor_tensor(chunked(bn), al_v, -1.0, chunked(A), ALU.mult, ALU.mult))
                prep(v.scalar_tensor_tensor(chunked(t1), rt_v, par(PR_RK), chunked(kt), ALU.mult, ALU.mult))
                for c in range(CHUNKS):
                    tok = slice(c * P, (c + 1) * P)
                    prep(v.tensor_tensor_scan(L[:, tok], sig[:, tok], sig[:, tok], 0.0, ALU.add, ALU.max), wait=c == CHUNKS - 1)
                Lc, df, mid = chunked(L), rw["df"][:, 0:8], rw["df"][:, 8:16]
                prep(v.tensor_copy(mid.unsqueeze(2), Lc[:, :, 63:64]))
                prep(v.tensor_tensor(df.unsqueeze(2), Lc[:, :, 127:128], mid.unsqueeze(2), ALU.subtract))
                prep(v.tensor_tensor(df[:, 0:7], df[:, 0:7], mid[:, 1:8], ALU.add))
                prep(v.tensor_tensor(Lc, Lc, mid.unsqueeze(2).broadcast_to([P, CHUNKS, P]), ALU.subtract))
                prep(v.tensor_tensor(sig, L, sig, ALU.subtract))
                dve.wait_ge(a_exp, upto(i * 3 + 1))
                prep(v.tensor_tensor(al_v, al_v, chunked(sig), ALU.mult), wait=False)
                dve.wait_ge(a_exp, upto(i * 3 + 2))
                prep(v.tensor_tensor(rt_v, rt_v, chunked(t2), ALU.mult), wait=False)
                dve.wait_ge(a_exp, upto(i * 3 + 3))
                prep(v.tensor_tensor(bn, bn, L, ALU.mult), wait=False)
                prep(v.tensor_tensor(kt, kt, L, ALU.mult), wait=False)
                assert count[0] == VC
                dve.wait_ge(r_bon, upto(i + 1))
                v.tensor_tensor(halves(rw["bv"]), ps[:, 4:6, :], halves(rw["v"]), ALU.mult).then_inc(v_fin, 1)
                dve.wait_ge(a_f, upto(i + 1))
                for cc in range(CHUNKS // PLACES):
                    chunks = round_of(cc)
                    for c, s, b0 in chunks:
                        dve.wait_ge(r_am, upto(i * 8 + c + 1))
                        for h in range(2):
                            v.tensor_tensor(am[s][:, h, :, :].rearrange("p (q o) n -> p q (o n)", q=2), ps[:, b0 + h, :].rearrange("p (q n) -> p q n", q=2),
                                            am_mask.bitcast(F32).unsqueeze(1).broadcast_to([P, 2, 256]), ALU.mult).then_inc(v_am, 1)
                    for c, s, b0 in chunks:
                        n = i * 8 + c
                        dve.wait_ge(v_am, upto(n * 2 + 2))
                        dve.wait_ge(a_xi, upto(n + 1))
                        wait_alone(dve)
                        v.copy_predicated(blocks_of(xx[s][:, 1, :, :], 0, 1), level_mask(0, 1), blocks_of(am[s][:, :, 0, :], 0, 1)).then_inc(v_x0, 1)
                        dve.wait_ge(r_x0, upto(n + 1))
                        wait_alone(dve)
                        v.copy_predicated(blocks_of(xx[s][:, 0, :, :], 0, 0), level_mask(0, 0), blocks_of(ps[:, b0:b0 + 2, 0:P], 0, 0)).then_inc(v_x0, 1)
                    for lv in range(1, LEVELS):
                        for c, s, b0 in chunks:
                            dve.wait_ge(r_xu, upto(lv_count(i, cc, lv, s) + 1))
                            for o in range(2):
                                if o == 1 or lv < LEVELS - 1:
                                    wait_alone(dve)
                                    part = per_head(ps[:, b0 + 1, o * 256:(o + 1) * 256])
                                    v.copy_predicated(blocks_of(xx[s][:, o, :, :], lv, o), level_mask(lv, o), blocks_of(part, lv, o)).then_inc(v_xu, 1)
                    for c, s, b0 in chunks:
                        dve.wait_ge(r_gq, upto(i * 8 + c + 1))
                        v.tensor_tensor(gt[s], ps[:, b0 + 1, 0:P], rt_v[:, c, :], ALU.add).then_inc(v_gt, 1)
                        for h in range(2):
                            hp = slice(64 * h, 64 * h + 64)
                            v.tensor_tensor(qq[hp, s, hp], ps[hp, b0 + 1, P + 64 * h:P + 64 * h + 64], ident[hp, hp], ALU.add).then_inc(v_q, 1)
                    for c, s, b0 in chunks:
                        dve.wait_ge(r_s, upto(i * 8 + c + 1))
                        v.tensor_scalar(SS[:, (c + 1) % 2, :], ps[:, b0, 0:P], rw["ff"][:, c:c + 1], None, ALU.mult).then_inc(v_s, 1)
                post = [0]

                def after(ins):
                    post[0] += 1
                    ins.then_inc(v_post, 1)
                    dve.wait_ge(v_post, upto(i * 6 + post[0]))
                dve.wait_ge(r_mean, upto(i + 1))
                after(v.scalar_tensor_tensor(halves(t2), ps[:, 4:6, :], -1.0 / RW_H, halves(A), ALU.mult, ALU.add))
                dve.wait_ge(a_yr, upto(i + 1))
                after(v.reciprocal(t1, t1))
                after(v.tensor_tensor(t2, t2, t1, ALU.mult))
                after(v.tensor_scalar(t2, t2, par(PR_LNW), par(PR_LNB), ALU.mult, ALU.add))
                after(v.tensor_tensor(t2, t2, rw["bv"], ALU.add))
                after(v.tensor_tensor(t2, t2, rw["g"], ALU.mult))

            dve.wait_ge(s_yb, upto(PAIRS * 16))
            dve.wait_ge(s_gst, upto(PAIRS * 48))
            v.memset(lr["xp"][:, 0:3], 0.0).then_inc(l_z, 1)
            with dve.Fori(0, TURNS["lru"]) as i:
                for u in range(2):
                    n = i * 2 + u
                    lp = lambda c: lru_par[0:80, bass.ds(n + c, 1)]
                    xpv, xa, gx, a2, aa, hh, ya, gy = (lr[k][0:80] for k in ("xp", "xa", "gx", "a2", "aa", "h", "ya", "gy"))
                    ada_pair(4, n + ADA0)
                    dve.wait_ge(l_x, upto(n + 1))
                    v.tensor_scalar(xa, xpv[:, 3:3 + T], lp(LP_CW + 48), lp(LP_CB), ALU.mult, ALU.add).then_inc(l_cv, 1)
                    for j in range(3):
                        dve.wait_ge(l_cv, upto(n * 4 + j + 1))
                        v.scalar_tensor_tensor(xa, xpv[:, j:j + T], lp(LP_CW + 16 * j), xa, ALU.mult, ALU.add).then_inc(l_cv, 1)
                    dve.wait_ge(l_cv, upto(n * 4 + 4))
                    dve.wait_ge(l_exp, upto(n * 2 + 1))
                    v.tensor_scalar(a2, a2, 1.0, None, ALU.min).then_inc(l_sq, 1)
                    dve.wait_ge(l_sa, upto(n * 2 + 2))
                    v.tensor_tensor(gx, gx, xa, ALU.mult).then_inc(l_u, 1)
                    dve.wait_ge(l_u, upto(n * 3 + 1))
                    dve.wait_ge(l_rt, upto(n + 1))
                    v.tensor_tensor(gx, gx, a2, ALU.mult).then_inc(l_u, 1)
                    dve.wait_ge(l_u, upto(n * 3 + 2))
                    dve.wait_ge(l_exp, upto(n * 2 + 2))
                    v.tensor_tensor_scan(hh, aa, gx, 0.0, ALU.mult, ALU.add).then_inc(l_u, 1)
                    dve.wait_ge(l_u, upto(n * 3 + 3))
                    dve.wait_ge(l_gy, upto(n + 1))
                    dve.wait_ge(s_ya, upto(n * 16))
                    v.tensor_tensor(ya, hh, gy, ALU.mult).then_inc(l_out, 1)

            dve.wait_ge(l_out, upto(LRU_N))
            dve.wait_ge(s_ya, upto(LRU_N * 16))
            for g in range(2):
                v.memset(ak[:, g, 0:P], 0.0).then_inc(t_z, 1)
                v.memset(av[:, g, 0, :], 0.0).then_inc(t_z, 1)
            dve.wait_ge(s_am, 16)
            dve.wait_ge(gain_sem, 64)
            v.tensor_scalar(nsinks[:, :], sinks_b, -1.0, None, ALU.mult).then_inc(t_z, 1)
            dve.wait_ge(t_z, upto(5))
            t2 = at_["t2"]
            amask = at_["mask"].rearrange("p (o m) -> p o m", o=2)
            with dve.Fori(0, TURNS["att"]) as i:
                for g in range(2):
                    gg = i * 2 + g
                    for c in range(3):
                        dve.wait_ge(t_rt, upto(gg * 3 + c + 1))
                        v.reciprocal(t2, t2).then_inc(t_rc, 1)
                        dve.wait_ge(t_rc, upto(gg * 3 + c + 1))
                        if c == 0:
                            v.scalar_tensor_tensor(ak[0:64, g, P:T + P], at_["kvt"][0:64, :], gains[0:64, 1:2], t2[0:64, :], ALU.mult, ALU.mult).then_inc(t_n, 1)
                        else:
                            q = aq[:, c - 1, :]
                            v.scalar_tensor_tensor(q, q, gains[:, 0:1], t2, ALU.mult, ALU.mult).then_inc(t_n, 1)
                    for tick in range(17):
                        if tick < 16:
                            u, t, n = tick, tick // 8, tick % 8
                            U = gg * 16 + u
                            sm, sc = asm[:, u % 4, :], asc[:, u % 4, :, :]
                            sk = sinks_b[:, bass.ds(gg * 4 + 2 * t, 2)]
                            dve.wait_ge(t_sc, upto(U + 1))
                            if u >= 4:
                                dve.wait_ge(t_pt, upto(U - 3))
                            v.scalar_tensor_tensor(sc, ps[:, 4 - 2 * (u % 2):6 - 2 * (u % 2), 0:256], HEAD ** -0.5,
                                                   amask[:, min(n, 1), :].unsqueeze(1).broadcast_to([P, 2, 256]), ALU.mult, ALU.add).then_inc(t_d, 1)
                            dve.wait_ge(t_d, upto(U * 4 + 1))
                            v.tensor_reduce(sm[:, 0:2], sc, AX.X, ALU.max).then_inc(t_d, 1)
                            dve.wait_ge(t_d, upto(U * 4 + 2))
                            v.scalar_tensor_tensor(sm[:, 2:4], sm[:, 0:2], -1.0, nsink(gg, t), ALU.mult, ALU.min).then_inc(t_d, 1)
                            dve.wait_ge(t_d, upto(U * 4 + 3))
                            v.tensor_tensor(sm[:, 6:8], sk, sm[:, 2:4], ALU.add).then_inc(t_d, 1)
                        if tick >= 1:
                            u = tick - 1
                            U = gg * 16 + u
                            sm, sc = asm[:, u % 4, :], asc[:, u % 4, :, :]
                            dve.wait_ge(t_e, upto(U * 3 + 3))
                            v.tensor_tensor(sm[:, 8:10], sm[:, 4:6], sm[:, 6:8], ALU.add).then_inc(t_dc, 1)
                            dve.wait_ge(t_dc, upto(U * 2 + 1))
                            v.reciprocal(sm[:, 10:12], sm[:, 8:10]).then_inc(t_dc, 1)
                            dve.wait_ge(t_dc, upto(U * 2 + 2))
                            for h in range(2):
                                v.tensor_scalar(sc[:, h, :], sc[:, h, :], sm[:, 10 + h:11 + h], None, ALU.mult).then_inc(t_p, 1)

            v.tensor_scalar(mod[:, MOD_SC2:MOD_SC2 + 8], mod[:, MOD_SC2:MOD_SC2 + 8], 1.0, None, ALU.add).then_inc(ada_fix, 1)
            dve.wait_ge(ada_fix, upto(2))

            dve.wait_ge(s_yc, upto(8 * 16))
            gated = 0

            def split_y(g, part):
                if g < len(BR):
                    for k in range(BR[g][1])[part]:
                        at = HALF * (g % 2) + k
                        dve.wait_ge(m_hi, upto(Y0[g] + k + 1))
                        v.tensor_tensor(x_lo[:, at, :], yraw[:, (Y0[g] + k) % 2, :], x_hi[:, at, :].bitcast(F32), ALU.subtract).then_inc(m_lo, 1)
            for part in PARTS:
                split_y(0, part)
            for g, (nm, kts, _, _, _, gi) in enumerate(BR):
                for part in PARTS:
                    split_y(g + 1, part)
                    with dve.Fori(part.start, part.stop) as i:
                        for c in range(2):
                            blk = Block(nm, c, i)
                            part = halves2(x2[:, bass.ds(i * 2 + c, 1), :])
                            acc, t = mix[:, bass.ds(i * 2 + c, 1), :].rearrange("p o n -> p (o n)"), mt[:, c, :]
                            m0 = EV0[nm] + (i * 2 + c) * M_EV[nm]
                            dve.wait_ge(s_dense, upto(blk.before + 1))
                            if nm in ("oa0", "oc0", "ob0"):
                                v.tensor_copy(part, pair_of(blk.slot)).then_inc(m_ev, 1)
                            elif gi is None:
                                v.tensor_tensor(part, pair_of(blk.slot), part, ALU.add).then_inc(m_ev, 1)
                            else:
                                v.tensor_tensor(halves(t), pair_of(blk.slot), part, ALU.add).then_inc(m_ev, 1)
                                dve.wait_ge(m_ev, upto(m0 + 1))
                                dve.wait_ge(s_g[c], i * 16 + (gated * 64 + 16))
                                if gi == 0:
                                    v.tensor_tensor(acc, t, gtl[:, c, :], ALU.mult).then_inc(m_ev, 1)
                                else:
                                    v.tensor_tensor(t, t, gtl[:, c, :], ALU.mult).then_inc(m_ev, 1)
                                    dve.wait_ge(m_ev, upto(m0 + 2))
                                    v.tensor_tensor(acc, acc, t, ALU.add).then_inc(m_ev, 1)
                gated += gi is not None
            for m in range(KT):
                at = (HALF * (len(BR) % 2) + m) % KT
                dve.wait_ge(m_hi, upto(NY + m + 1))
                v.tensor_tensor(x_lo[:, at, :], mix[:, m, :], x_hi[:, at, :].bitcast(F32), ALU.subtract).then_inc(m_lo, 1)
            dve.wait_ge(m_xt, upto(8))
            for half in range(2):
                with dve.Fori(0, 4) as i:
                    for c in range(2):
                        blk = Block(f"wout{half}", c, i)
                        dve.wait_ge(s_dense, upto(blk.before + 1))
                        r = halves2(x2[:, bass.ds(i * 2 + c, 1), :])
                        v.scalar_tensor_tensor(r, pair_of(blk.slot), mod[:, bass.ds(i * 2 + (MOD_G1 + c), 1)], r, ALU.mult, ALU.add).then_inc(m_res, 1)
                dve.wait_ge(m_res, upto(8 * half + 8))
            rs = yraw[:, 0, :]
            dve.wait_ge(m_rt, upto(1))
            v.reciprocal(rs, rs).then_inc(m_n, 1)
            dve.wait_ge(m_n, upto(1))
            for k in range(KT):
                t = mt[:, k % 2, :]
                v.scalar_tensor_tensor(t, x2[:, k, :], mod[:, MOD_SC2 + k:MOD_SC2 + k + 1], rs, ALU.mult, ALU.mult).then_inc(m_nh, 1)
                dve.wait_ge(m_nh, upto(2 * k + 1))
                dve.wait_ge(m_hi, upto(NY + KT + k + 1))
                v.scalar_tensor_tensor(x_lo[:, k, :], t, mod[:, MOD_SH2 + k:MOD_SH2 + k + 1], x_hi[:, k, :].bitcast(F32), ALU.add, ALU.subtract).then_inc(m_nh, 1)

            def product(blk, tile, t):
                dve.wait_ge(s_dense, upto(blk.before + 1))
                dve.wait_ge(m_sil, upto(tile + 1))
                v.tensor_tensor(halves(mt[:, t, :]), pair_of(blk.slot), halves(gtl[:, 0, :]), ALU.mult).then_inc(m_act, 1)

            def hidden_low(tile, t):
                dve.wait_ge(m_act, upto(tile + 1))
                dve.wait_ge(m_hh, upto(tile + 1))
                v.tensor_tensor(hid_lo[:, t, :], mt[:, t, :], hid_hi[:, t, :].bitcast(F32), ALU.subtract).then_inc(m_hl, 1)

            def add_down(name, c0, i, turn):
                for m in range(8):
                    if m % 4 == 3:
                        dve.wait_ge(s_dense, upto(Block(name, c0 + m // 4, i).before + 1))
                    else:
                        dve.wait_ge(m_dd, upto(turn * 6 + m - m // 4 + 1))
                    if m == 0:
                        dve.wait_ge(m_dn, upto(turn * 8))
                    r = halves(x2[:, m, :])
                    v.scalar_tensor_tensor(r, ps[:, 4 + 2 * (m % 2):6 + 2 * (m % 2), :], mod[:, MOD_G2 + m:MOD_G2 + m + 1], r, ALU.mult, ALU.add).then_inc(m_dn, 1)
            product(Block("ffn_first", 1), 0, 0)
            hidden_low(0, 0)
            with dve.Fori(0, TURNS["ffn"]) as i:
                product(Block("ffn", 1, i), i * 2 + 1, 1)
                hidden_low(i * 2 + 1, 1)
                product(Block("ffn", 3, i), i * 2 + 2, 0)
                add_down("ffn", 4, i, i)
                hidden_low(i * 2 + 2, 0)
            product(Block("ffn_last", 1), 2 * TURNS["ffn"] + 1, 1)
            hidden_low(2 * TURNS["ffn"] + 1, 1)
            add_down("ffn_last", 2, 0, TURNS["ffn"])


INPUTS = ["x", "c", "w_ada", "b_ada", "w_in", "conv_w", "conv_b", "lru_wa", "lru_ba", "lru_wx", "lru_bx", "lru_lambda",
          "w_lru_o", "rw_mu", "rw_w0", "rw_w2", "rw_a0", "rw_a2", "rw_g2", "rw_kk", "rw_ka", "rw_rk", "rw_ln_w", "rw_ln_b",
          "w_rw_o", "q_gain", "k_gain", "sinks", "w_att_o", "w_out", "w_ffn_in", "w_ffn_out"]


def kernel(**inputs):
    import concourse.bacc as _bacc
    from concourse.bass_utils import run_bass_kernel_spmd as _run

    nc = _bacc.Bacc("TRN2", target_bir_lowering=False, num_devices=1)
    arrays, aps = {}, {}
    for name in INPUTS:
        arr = np.ascontiguousarray(inputs[name])
        arrays[f"in_{name}"] = arr
        aps[name] = nc.dram_tensor(f"in_{name}", arr.shape, F32, kind="ExternalInput").ap()
    arrays["in_consts"] = constants()
    aps["consts"] = nc.dram_tensor("in_consts", (P, C_N), F32, kind="ExternalInput").ap()
    out = nc.dram_tensor("out", (1, T, D), F32, kind="ExternalOutput").ap()
    build(nc, aps, out)
    return _run(nc, [arrays], core_ids=[0]).results[0]["out"]
```

```python
import math
from contextlib import ExitStack

import numpy as np

import concourse.bass as bass
from concourse import mybir

F32 = mybir.dt.float32
F32R = mybir.dt.float32r
I32 = mybir.dt.int32
ALU = mybir.AluOpType
ACT = mybir.ActivationFunctionType
AX = mybir.AxisListType

P = 128
T = 1024
D = 1024
KT = D // P
LRU_W, LRU_BLK = 1280, 80
LRU_N = LRU_W // LRU_BLK
RW_W, RW_H = 1024, 64
PAIRS = RW_W // P
KV_HEADS, HEAD = 4, 64
FF = 2816
FF_GROUP = 2
CHUNK = 128
CHUNKS = T // CHUNK
LEVELS = int(math.log2(CHUNK))
DECAY = math.exp(-0.5)
NEG = -1e30

COL_LX, COL_LY = 0, LRU_W
COL_RW = 2 * LRU_W
COL_LORA = COL_RW + 3 * RW_W
COL_Q = COL_LORA + 288
COL_K = COL_Q + 1024
COL_V = COL_K + 256
COL_G = COL_V + 256

PR_W0, PR_A0, PR_KK, PR_KA, PR_RK, PR_LNW, PR_LNB, PR_MU = range(0, 64, 8)
PR_MU_WA, PR_MU_G0, PR_MU_G1, PR_ROWS = 80, 81, 82, 83
LP_CW, LP_CB, LP_BA, LP_BX, LP_LAM = 0, 64, 80, 96, 112
MOD_SH1, MOD_SC1, MOD_G1, MOD_SH2, MOD_SC2, MOD_G2, MOD_N = range(0, 56, 8)

C_ID, C_BD, C_ONE, C_ATT, C_AM, C_LV = 0, 128, 256, 384, 896, 1152
C_N = C_LV + 2 * LEVELS * P
C_KEEP = C_ATT

STREAM = [("lora", 1, 3), ("rwkv", PAIRS, 6), ("lru", LRU_N // 2, 4), ("att", 1, 12),
          ("oa0", 4, 2), ("oa1", 4, 2), ("oa2", 4, 2), ("oc0", 4, 2), ("oc1", 4, 2), ("ob0", 4, 2), ("ob1", 4, 2),
          ("wout0", 4, 2), ("wout1", 4, 2), ("ffn_first", 1, 2), ("ffn", FF // P // FF_GROUP - 1, 6), ("ffn_last", 1, 4)]
STREAM_START = 2
BASE, _at = {}, STREAM_START
for _name, _turns, _per in STREAM:
    BASE[_name] = _at
    _at += _turns * _per
TURNS = {n: t for n, t, _ in STREAM}
PER = {n: p for n, _, p in STREAM}


def constants():
    c = np.zeros((P, C_N), np.float32)
    r, k = np.arange(P)[:, None], np.arange(P)[None, :]
    c[:, C_ID:C_ID + P] = r == k
    c[:, C_BD:C_BD + P] = r // 64 == k // 64
    c[:, C_ONE:C_ONE + P] = 1
    kj = np.arange(2 * P)[None, :]
    local = (kj <= r + P) & (r + P - kj < P)
    c[:, C_ATT:C_ATT + 256] = np.where(local & (kj >= P), 0, NEG)
    c[:, C_ATT + 256:C_ATT + 512] = np.where(local, 0, NEG)
    c[:, C_AM:C_AM + P] = k > r
    c[:, C_AM + P:C_AM + 2 * P] = k >= r
    for lv in range(LEVELS):
        s = 2 ** lv
        low = (r // s % 2 == 1) & (k // s == r // s - 1)
        c[:, C_LV + 2 * lv * P:C_LV + (2 * lv + 1) * P] = low
        c[:, C_LV + (2 * lv + 1) * P:C_LV + (2 * lv + 2) * P] = low.T
    return c


class Block:

    def __init__(self, name, c, i=0):
        at = BASE[name] + c
        self.slot = at % 2
        self.before = i * PER[name] + at
        self.loads = i * (PER[name] // 2) + at // 2 - STREAM_START // 2


def build(nc, a, out):
    ctx = ExitStack()
    with ctx:
        def sb(name, shape, dt=F32):
            return ctx.enter_context(nc.sbuf_tensor(name, shape, dt))

        def sem(name):
            return ctx.enter_context(nc.semaphore(name))

        def dram(name, rows):
            return nc.dram_tensor(name, (rows, T), F32, kind="Internal").ap()

        y_a, y_b, y_c, gates = dram("y_a", LRU_W), dram("y_b", RW_W), dram("y_c", D), dram("gates_sig", 3 * D)

        x_hi = sb("x_hi", [P, KT, T], F32R)
        x_lo = sb("x_lo", [P, KT, T], F32R)
        w_raw = sb("w_raw", [P, 2, 1024])
        w_hi = sb("w_hi", [P, 2, 1024], F32R)
        w_lo = sb("w_lo", [P, 2, 1024], F32R)
        hid_hi = sb("hid_hi", [P, 2, T], F32R)
        hid_lo = sb("hid_lo", [P, 2, T], F32R)
        keep = sb("keep", [P, C_KEEP])
        rw_par = sb("rw_par", [P, P])
        lru_par = sb("lru_par", [P, P])
        mod = sb("mod", [P, 56])
        small = sb("small", [P, 96])
        ARENA = 25100
        arena = sb("arena", [P, ARENA])
        ps = ctx.enter_context(nc.psum_tensor("ps", [P, 8, 512], F32))

        ident = keep[:, C_ID:C_ID + P]
        headsum = keep[:, C_BD:C_BD + P]
        ones = keep[:, C_ONE:C_ONE + P]

        def carve(sizes):
            at, got = 0, {}
            for name, n in sizes:
                got[name] = arena[:, at:at + n]
                at += n
            assert at <= ARENA, at
            return got

        def pair_of(slot):
            return ps[:, 2 * slot:2 * slot + 2, :]

        def halves(ap):
            return ap.rearrange("p (h n) -> p h n", h=2)

        s_const = sem("constants_loaded")
        s_par = sem("parameters_loaded")
        s_w = [sem("weights_loaded_0"), sem("weights_loaded_1")]
        s_whi = sem("weights_high_part")
        s_wsplit = sem("weights_split")
        s_dense = sem("dense_done")

        s_yb, s_gst, s_ya = (sem(n) for n in ("y_b_stored", "gate_stored", "y_a_stored"))
        s_yc = [sem(f"y_c_stored_{t}") for t in range(2)]
        stream_sems = [s_dense, s_whi, s_wsplit]
        engine_sems = {"pe": [s_dense], "act": [s_yb, s_gst, s_ya, *s_yc], "dve": [], "pool": [s_whi, s_wsplit]}

        def made_by(engine, *names):
            got = [sem(n) for n in names]
            engine_sems[engine] += got
            return got if len(got) > 1 else got[0]

        s_x = sem("x_loaded")
        p0_pe, p0_act, p0_dve = made_by("pe", "start_pe"), made_by("act", "start_act"), made_by("dve", "start_dve")
        ada_out, ada_pe = made_by("dve", "mod_columns_ready"), made_by("pe", "mod_columns_done")
        s_ada = [sem(f"ada_weights_loaded_{k}") for k in range(4)]
        ADA0 = 8
        ada_fix = made_by("dve", "mod_scales_ready")
        h_pe, h_tmp, h_hi, h_lo = made_by("pe", "xnT_done"), made_by("dve", "h_ready"), made_by("act", "h_high"), made_by("dve", "h_low")

        passed = {"SP": sem("sp_waits_passed"), "Pool": sem("pool_waits_passed"), "DVE": sem("dve_waits_passed"),
                  "PE": sem("pe_waits_passed")}

        def wait_alone(eng):
            eng.sem_inc(passed[eng.engine.name], 1)

        def upto(n):
            return max(n, 0) + 1 if isinstance(n, int) else n + 1

        def seed(eng, name):
            for s in engine_sems[name]:
                eng.sem_inc(s, 1 + STREAM_START if s in stream_sems else 1)

        def load_block(sp, blk, src, width):
            n = src.shape[1] * width
            dst = w_raw[:, blk.slot, 0:n].rearrange("p (k m) -> p k m", m=width)
            sp.wait_ge(s_wsplit, upto(blk.before - 1))
            wait_alone(sp)
            sp.dma_start(dst, src).then_inc(s_w[blk.slot], 16)

        def split_block(pool, blk, n):
            raw, hi, lo = (t[:, blk.slot, 0:n] for t in (w_raw, w_hi, w_lo))
            pool.wait_ge(s_w[blk.slot], blk.loads * 16 + 16)
            pool.wait_ge(s_dense, upto(blk.before - 1))
            wait_alone(pool)
            nc.gpsimd.tensor_copy(hi, raw).then_inc(s_whi, 1)
            pool.wait_ge(s_whi, upto(blk.before + 1))
            nc.gpsimd.tensor_tensor(lo, raw, hi.bitcast(F32), ALU.subtract).then_inc(s_wsplit, 1)

        def three_passes(dst, w, x, first, last):
            (wh, wl), (xh, xl) = w, x
            n = len(dst)
            for m, (wp, xp) in enumerate(((wh, xh), (wh, xl), (wl, xh))):
                for h in range(n):
                    ins = nc.tensor.matmul(dst[h], wp, xp[h], start=first and m == 0, stop=last and m == 2)
            return ins

        def dense(pe, blk, width=P, tiles=KT, first=0, ready=None):
            pe.wait_ge(s_wsplit, upto(blk.before + 1))
            dst = [ps[0:width, 2 * blk.slot + h, :] for h in range(2)]
            for k in range(tiles):
                if ready is not None:
                    made, before, steps = ready
                    pe.wait_ge(made, upto(before + (k + 1) * steps))
                w = [t[:, blk.slot, k * width:(k + 1) * width] for t in (w_hi, w_lo)]
                x = [[t[:, first + k, h * 512:(h + 1) * 512] for h in range(2)] for t in (x_hi, x_lo)]
                ins = three_passes(dst, w, x, k == 0, k == tiles - 1)
            ins.then_inc(s_dense, 1)

        def cols(w, c0, n):
            return w[:, bass.ds(c0, n)].rearrange("(k p) m -> p k m", p=P)

        st0 = carve([("row_rw", P), ("row_lru", P), ("row_mod", P), ("xs", 8 * D), ("tmp", 2 * T), ("sq", 2 * D),
                     ("ada", 4 * 2048)])
        ada_w0 = st0["ada"].rearrange("p (s k m) -> p s k m", s=4, k=KT)
        row_rw, row_lru, row_mod = st0["row_rw"], st0["row_lru"], st0["row_mod"]
        xs = st0["xs"].rearrange("p (t d) -> p t d", t=8)
        h_tmpb = st0["tmp"].rearrange("p (s n) -> p s n", s=2)
        sq0 = st0["sq"].rearrange("p (s n) -> p s n", s=2)
        sumsq, rstd = small[:, 0:8], small[:, 8:16]
        sinks_b = small[:, 16:32]
        gains = small[:, 32:34]
        rate, rate2 = small[:, 34:50], small[:, 50:66]

        def load_parameters(sp):
            for src, dst in (("rw_w0", PR_W0), ("rw_a0", PR_A0), ("rw_kk", PR_KK), ("rw_ka", PR_KA), ("rw_rk", PR_RK),
                             ("rw_ln_w", PR_LNW), ("rw_ln_b", PR_LNB)):
                sp.dma_start(row_rw[dst:dst + 8, :], a[src][0].rearrange("(t p) -> t p", p=P)).then_inc(s_par, 16)
            mu = a["rw_mu"][0]
            sp.dma_start(row_rw[PR_MU:PR_MU_G1, :], mu[0:26 * P].rearrange("(t p) -> t p", p=P)).then_inc(s_par, 16)
            sp.dma_start(row_rw[PR_MU_G1:PR_ROWS, 0:32], mu[26 * P:26 * P + 32].rearrange("(t p) -> t p", t=1)).then_inc(s_par, 16)
            sp.dma_start(row_lru[0:64, 0:80], a["conv_w"][0].rearrange("j (b n) -> (j b) n", n=80)).then_inc(s_par, 16)
            for src, dst in (("conv_b", LP_CB), ("lru_ba", LP_BA), ("lru_bx", LP_BX), ("lru_lambda", LP_LAM)):
                sp.dma_start(row_lru[dst:dst + 16, 0:80], a[src][0].rearrange("(b n) -> b n", n=80)).then_inc(s_par, 16)
            sp.dma_start(row_mod[0:48, :], a["b_ada"][0].rearrange("(t p) -> t p", p=P)).then_inc(s_par, 16)
            sp.dma_start(row_mod[48:56, :], a["c"][0].rearrange("(t p) -> t p", p=P)).then_inc(s_par, 16)
            sp.dma_start(sinks_b, a["sinks"].broadcast_to([P, 16])).then_inc(s_par, 16)

        gain_sem = sem("gains_loaded")

        def load_gains(sp):
            for col, name in ((0, "q_gain"), (1, "k_gain")):
                for h in range(2):
                    sp.dma_start(gains[64 * h:64 * h + 64, col:col + 1], a[name].rearrange("a (n o) -> n (a o)", o=1)).then_inc(gain_sem, 16)

        PLACES = 4
        PLACE_SIZE = 2560
        rw_at = {"t1": 5 * T + 8}
        rw = carve([("wa", T), ("g0", T), ("g1", T), ("xp", T + 8), ("A", T), ("t1", T), ("t2", T), ("sig", T), ("L", T),
                    ("ar", 2 * T), ("bn", T), ("kt", T), ("v", T), ("bv", T), ("g", T), ("gs", T),
                    ("lw", P), ("lg0", P), ("lg1", P), ("S", 2 * P), ("df", 16), ("ff", 8), ("q", PLACES * P),
                    ("place0", PLACE_SIZE), ("place1", PLACE_SIZE), ("place3", PLACE_SIZE - (4 * T - PLACE_SIZE))])
        ar = rw["ar"].rearrange("p (c s n) -> p c s n", c=CHUNKS, s=2)
        al_v, rt_v = ar[:, :, 0, :], ar[:, :, 1, :]
        chunked = lambda ap: ap.rearrange("p (c n) -> p c n", c=CHUNKS)
        scratch = arena[:, rw_at["t1"]:rw_at["t1"] + 4 * T]
        left = 4 * T - PLACE_SIZE
        parts = {"am": 1024, "xx": 512, "y1": 256, "tk": 512, "R": 256}
        places = []
        for base in (rw["place0"], rw["place1"], scratch[:, 0:PLACE_SIZE], None):
            at, got = 0, {}
            for name, n in parts.items():
                if base is not None:
                    got[name] = base[:, at:at + n]
                elif at + n <= left:
                    got[name] = scratch[:, PLACE_SIZE + at:PLACE_SIZE + at + n]
                    rest = at + n
                else:
                    got[name] = rw["place3"][:, at - rest:at - rest + n]
                at += n
            places.append(got)
        am = [g["am"].rearrange("p (h q n) -> p h q n", h=2, q=4) for g in places]
        xx = [g["xx"].rearrange("p (o h n) -> p o h n", o=2, h=2) for g in places]
        y1 = [g["y1"].rearrange("p (h n) -> p h n", h=2) for g in places]
        tk = [g["tk"].rearrange("p (q n) -> p q n", q=4) for g in places]
        RR = [g["R"].rearrange("p (h n) -> p h n", h=2) for g in places]
        uw = y1
        gt = [x[:, 0, 0, :] for x in xx]
        qq = rw["q"].rearrange("p (s n) -> p s n", s=PLACES)

        def blocks_of(ap, lv, odd):
            return ap.rearrange("p h (b two e) -> p h b two e", two=2, e=2 ** lv)[..., odd, :]

        def per_head(ap):
            return ap.rearrange("p (h n) -> p h n", h=2)
        SS = rw["S"].rearrange("p (s n) -> p s n", s=2)
        masks = hid_hi[:, :, :].rearrange("p a n -> p (a n)")
        am_mask = masks[:, 0:256]
        lv_mask = hid_lo[:, :, :].rearrange("p a n -> p (a n)")[:, 0:2 * LEVELS * P]
        s_mask, s_lw = sem("masks_loaded"), sem("lora_weights_loaded")
        mask_ready = made_by("dve", "masks_ready")
        (r_lwa, r_kks, r_g, r_bon, r_mean, r_var) = made_by("pe", "rw_lora_done", "rw_kk_sums", "rw_g_done", "rw_bonus_sums", "rw_mean_done", "rw_var_done")
        (r_tk, r_am, r_x0, r_y1, r_xu, r_ak, r_uw, r_gq, r_s, r_y) = made_by(
            "pe", "tokens_major_done", "pair_products_done", "level0_product_done", "level_product_done", "level_update_done", "ak_v_done",
            "solve_done", "g_q_done", "state_done", "y_chunk_done")
        (a_xp, a_sa, a_sqk, a_gate, a_rk, a_g, a_exp, a_f, a_wa) = made_by(
            "act", "rw_stream_copied", "rw_sigmoids_ready", "rw_kk_squared", "gate_ready", "rw_kk_root", "rw_g_ready",
            "rw_exponentials", "rw_state_scale", "rw_lora_in_ready")
        (a_tk, a_xi, a_y1, a_ak, a_uw, a_y, a_ysq, a_yr) = made_by(
            "act", "tokens_major_ready", "inverse_started", "level_product_ready", "ak_v_ready", "solve_ready", "y_chunk_ready",
            "y_squared", "y_root")
        (v_mix, v_kk, v_c, v_fin, v_am, v_x0, v_xu, v_gt, v_q, v_s, v_post, v_zero) = made_by(
            "dve", "rw_stream_mixed", "rw_kk_ready", "rw_prep", "rw_bonus_ready", "pair_products_ready", "level0_ready",
            "level_ready", "g_ready", "q_ready", "state_ready", "rw_post", "rw_zeroed")

        lr = carve([("xp", T + 8), ("xa", T), ("ga", T), ("gx", T), ("aa", T), ("a2", T), ("h", T), ("gy", T), ("ya", T),
                    ("wa", 2 * LRU_BLK), ("wx", 2 * LRU_BLK), ("ada", 2 * 2048)])
        ada_w1 = lr["ada"].rearrange("p (s k m) -> p s k m", s=2, k=KT)
        l_x, l_sa, l_rt, l_gy, l_exp = made_by("act", "lru_x_copied", "lru_gates_ready", "lru_root_ready", "lru_gelu_ready", "lru_decay_ready")
        l_pe = made_by("pe", "lru_gates_done")
        l_cv, l_sq, l_u, l_out, l_z = made_by("dve", "conv_steps", "decay_squared", "lru_input_steps", "lru_out_steps", "lru_zeroed")
        s_lw2 = [sem("lru_gate_weights_loaded_0"), sem("lru_gate_weights_loaded_1")]

        LRU_ARENA = 9 * T + 8 + 4 * LRU_BLK + 2 * 2048
        GROUPS = KV_HEADS
        UNITS = 16
        at_ = carve([("k", 2 * (T + P)), ("v", 2 * 9 * HEAD), ("q1", 2 * T), ("yc", 2 * T), ("mask", 512), ("s", 4 * 512),
                     ("pT", 4 * 512), ("sm", 64), ("pad", LRU_ARENA - 12224), ("kvt", T), ("t1", 2 * T), ("t2", 3 * T), ("q0", 2 * T)])
        squares = at_["t1"].rearrange("p (s n) -> p s n", s=2)
        roots = at_["t2"].rearrange("p (s n) -> p s n", s=3)
        ak = at_["k"].rearrange("p (g n) -> p g n", g=2)
        av = at_["v"].rearrange("p (g b d) -> p g b d", g=2, b=9)
        aq = [at_[f"q{k}"].rearrange("p (t n) -> p t n", t=2) for k in range(2)]
        ayc = at_["yc"].rearrange("p (t n) -> p t n", t=2)
        asc = at_["s"].rearrange("p (u h n) -> p u h n", u=4, h=2)
        apt = at_["pT"].rearrange("p (u m) -> p u m", u=4)
        asm = at_["sm"].rearrange("p (u m) -> p u m", u=4)
        s_am, s_kfirst = sem("attention_masks_loaded"), sem("k_half_loaded")
        t_ns, t_vt, t_sc, t_pt, t_o = made_by("pe", "norm_sums_done", "v_transposed", "scores_done", "probs_transposed", "attention_out_done")
        t_cp, t_sq, t_rt, t_v, t_e, t_ptc, t_oc, t_k2 = made_by(
            "act", "kv_copied", "head_squares", "head_root", "v_ready", "exp_done", "probs_t_ready", "attention_out_ready", "k_second_half")
        t_rc, t_n, t_d, t_p, t_z, t_dc = made_by("dve", "head_rsqrt", "head_normed", "softmax_steps", "probs_ready", "att_zeroed", "denominator_steps")

        mg = carve([("x2", KT * T), ("mix", KT * T), ("gt", 2 * T), ("t", 2 * T), ("pad", 1536), ("yraw", 2 * T)])
        assert 20 * T + 1536 >= LRU_ARENA + 8 * T
        x2 = mg["x2"].rearrange("p (k n) -> p k n", k=KT)
        mix = mg["mix"].rearrange("p (k n) -> p k n", k=KT)
        yraw = mg["yraw"].rearrange("p (s n) -> p s n", s=2)
        gtl = mg["gt"].rearrange("p (s n) -> p s n", s=2)
        mt = mg["t"].rearrange("p (s n) -> p s n", s=2)
        s_y = [sem("y_tile_loaded_0"), sem("y_tile_loaded_1")]
        s_g = [sem("gate_tile_loaded_0"), sem("gate_tile_loaded_1")]
        s_x2, s_out = [sem("x_loaded_again_0"), sem("x_loaded_again_1")], sem("out_stored")
        m_hi, m_sq, m_rt, m_sil, m_hh, m_o = made_by("act", "operand_high", "x2_squared", "x2_root", "silu_ready", "hidden_high", "out_copied")
        m_lo, m_ev, m_xt, m_res, m_n, m_nh, m_act, m_hl, m_dn = made_by(
            "dve", "operand_low", "merge_steps", "xT_ready", "residual_ready", "x2_rstd", "h2_steps", "hidden_ready", "hidden_low", "down_added")
        m_pe, m_ss, m_dd, m_op = made_by("pe", "xT_done", "x2_sums_done", "down_done", "out_transposed")

        BR = [("oa0", 4, "w_lru_o", 0, y_a, None), ("oa1", 3, "w_lru_o", 512, y_a, None), ("oa2", 3, "w_lru_o", 896, y_a, 0),
              ("oc0", 4, "w_att_o", 0, y_c, None), ("oc1", 4, "w_att_o", 512, y_c, 2),
              ("ob0", 4, "w_rw_o", 0, y_b, None), ("ob1", 4, "w_rw_o", 512, y_b, 1)]
        PARTS = (slice(0, 2), slice(2, 4))
        HALF = KT // 2
        NY = sum(kts for _, kts, *_ in BR)
        Y0 = [sum(kts for _, kts, *_ in BR[:g]) for g in range(len(BR))]
        M_EV = {"oa0": 1, "oa1": 1, "oa2": 2, "oc0": 1, "oc1": 3, "ob0": 1, "ob1": 3}
        Y_TICKS = (2, 5, 8, 11)
        EV0, _n = {}, 0
        for nm, *_ in BR:
            EV0[nm] = _n
            _n += 8 * M_EV[nm]
        EV_ALL = _n

        def first_step(n):
            nm = BR[n // 8][0]
            return EV0[nm] + n % 8 * M_EV[nm] + 1

        lam_s = made_by("dve", "lambda_steps")
        bias_t = sb("bias_t", [P, 4])
        eps_qk, eps_rms, eps_ln, one_b = bias_t[:, 0:1], bias_t[:, 0:1], bias_t[:, 1:2], bias_t[:, 2:3]
        lsc = sb("lsc", [P, 32])
        SOFT = 5 + 16 + 5 + 3
        VC = 24
        VZ = 5
        XP0, XM0 = 3, 6
        N_PAR_DMA = 7 + 2 + 1 + 4 + 2 + 1
        nsinks = sb("nsinks", [P, 16])

        def nsink(gg, t):
            return nsinks[:, gg * 4 + 2 * t:gg * 4 + 2 * t + 2]

        def halves2(ap):
            return ap.rearrange("p o (h n) -> p (o h) n", h=2)

        def lv_count(i, cc, lv, s):
            return i * (CHUNKS * (LEVELS - 1)) + (cc * (LEVELS - 1) + lv - 1) * PLACES + s

        def xu_count(i, cc, lv, s):
            last = LEVELS - 1
            turn = PLACES * (2 * (LEVELS - 2) + 1)
            return i * (CHUNKS // PLACES * turn) + cc * turn + ((lv - 1) * 2 * PLACES + 2 * s if lv < last else (last - 1) * 2 * PLACES + s)

        def round_of(cc):
            return [(PLACES * cc + s, s, 2 * s) for s in range(PLACES)]

        blockctx = ctx.enter_context(nc.Block())

        @blockctx.sync
        def _(sp):
            sp.dma_start(keep[:, :], a["consts"][:, 0:C_KEEP]).then_inc(s_const, 16)
            sp.wait_ge(p0_dve, upto(3))
            load_parameters(sp)
            w_in, w_ada = a["w_in"][0], a["w_ada"][0]

            def load_ada(r):
                for k in range(4):
                    sp.wait_ge(ada_pe, upto((r - 1) * 4 + k + 1))
                    sp.dma_start(ada_w0[:, k, :, :], cols(w_ada, (4 * r + k) * 256, 256)).then_inc(s_ada[k], 16)
            load_ada(0)
            for t in range(8):
                sp.dma_start(xs[:, t, :], a["x"][0, t * P:(t + 1) * P, :]).then_inc(s_x, 16)
            load_gains(sp)
            for c, (c0, n) in enumerate(((0, P), (P, P), (2 * P, 32))):
                load_block(sp, Block("lora", c), cols(w_in, COL_LORA + c0, n), n)
            for r in range(1, ADA0 // 4):
                load_ada(r)
            sp.wait_ge(h_lo, upto(KT))
            sp.dma_start(rw["ar"][:, 0:2 * LEVELS * P], a["consts"][:, C_LV:C_N]).then_inc(s_mask, 16)
            sp.dma_start(rw["bn"][:, 0:256], a["consts"][:, C_AM:C_AM + 256]).then_inc(s_mask, 16)
            w2, a2, g2 = a["rw_w2"][0], a["rw_a2"][0], a["rw_g2"][0]
            with sp.Fori(0, PAIRS) as i:
                for c in range(3):
                    load_block(sp, Block("rwkv", c, i), cols(w_in, COL_RW + c * RW_W + i * P, P), P)
                sp.wait_ge(r_g, upto(i))
                wait_alone(sp)
                sp.dma_start(rw["lw"][0:64, :], w2[:, bass.ds(i * P, P)]).then_inc(s_lw, 16)
                sp.dma_start(rw["lw"][64:128, :], a2[:, bass.ds(i * P, P)]).then_inc(s_lw, 16)
                sp.dma_start(rw["lg0"], g2[0:P, bass.ds(i * P, P)]).then_inc(s_lw, 16)
                sp.dma_start(rw["lg1"][0:32, :], g2[P:160, bass.ds(i * P, P)]).then_inc(s_lw, 16)
                for c in range(3):
                    load_block(sp, Block("rwkv", 3 + c, i), cols(w_in, COL_G + c * D + i * P, P), P)
            with sp.Fori(0, TURNS["lru"]) as i:
                for u in range(2):
                    for c, c0 in enumerate((COL_LX, COL_LY)):
                        load_block(sp, Block("lru", 2 * u + c, i), cols(w_in, c0 + u * 80 + i * 160, 80), 80)
                    sp.wait_ge(a_y, upto(PAIRS * CHUNKS))
                    sp.wait_ge(v_s, upto(PAIRS * CHUNKS))
                    sp.wait_ge(ada_pe, upto(i * 2 + (ADA0 + u - 1)))
                    wait_alone(sp)
                    sp.dma_start(ada_w1[:, u, :, :], cols(w_ada, (ADA0 + u) * 256 + i * 512, 256)).then_inc(s_ada[u], 16)
                    sp.wait_ge(l_pe, upto(i * 2))
                    wait_alone(sp)
                    for nm, dst in (("lru_wa", lr["wa"]), ("lru_wx", lr["wx"])):
                        sp.dma_start(dst[0:80, 80 * u:80 * u + 80], a[nm][0, bass.ds(i * 2 + u, 1)].rearrange("o n m -> (o n) m")).then_inc(s_lw2[u], 16)
            for gg in range(GROUPS):
                b = Block("att", 3 * gg)
                dst = w_raw[:, b.slot, :].rearrange("p (k s m) -> p k s m", k=KT, s=2)
                sp.wait_ge(s_wsplit, upto(b.before - 1))
                for s in range(2):
                    src = cols(w_in, COL_K + 256 * s + HEAD * gg, HEAD)
                    sp.dma_start(dst[:, :, s, :], src).then_inc(s_w[b.slot] if s else s_kfirst, 16)
                for t in range(2):
                    load_block(sp, Block("att", 3 * gg + 1 + t), cols(w_in, COL_Q + 256 * gg + P * t, P), P)
                if gg == 0:
                    sp.wait_ge(l_out, upto(LRU_N))
                    sp.wait_ge(s_ya, upto(LRU_N * 16))
                    sp.dma_start(at_["mask"], a["consts"][:, C_ATT:C_ATT + 512]).then_inc(s_am, 16)
            def load_y(g, part):
                if g < len(BR):
                    _, kts, _, row0, y, _ = BR[g]
                    for k in range(kts)[part]:
                        n = Y0[g] + k
                        sp.wait_ge(m_lo, upto(n - 1))
                        sp.dma_start(yraw[:, n % 2, :], y[row0 + k * P:row0 + (k + 1) * P, :]).then_inc(s_y[n % 2], 16)
            for part in PARTS:
                load_y(0, part)
            for g, (nm, kts, wname, row0, _, gi) in enumerate(BR):
                wv = a[wname][0][row0:row0 + kts * P, :]
                if g == 1:
                    for t in range(2):
                        sp.wait_ge(s_yc[t], upto(GROUPS * 16))
                for part in PARTS:
                    with sp.Fori(part.start, part.stop) as i:
                        for c in range(2):
                            load_block(sp, Block(nm, c, i), cols(wv, c * P + i * 2 * P, P), P)
                            if gi is not None:
                                sp.wait_ge(m_ev, upto(EV0[nm] - M_EV[nm] + (i * 2 + c) * M_EV[nm]))
                                wait_alone(sp)
                                sp.dma_start(gtl[:, c, :], gates[bass.ds(gi * D + c * P + i * 2 * P, P), :]).then_inc(s_g[c], 16)
                    load_y(g + 1, part)
            for t in range(8):
                if t < 2:
                    sp.wait_ge(m_lo, upto(NY))
                else:
                    sp.wait_ge(m_pe, upto(t - 1))
                sp.dma_start(yraw[:, t % 2, :], a["x"][0, t * P:(t + 1) * P, :]).then_inc(s_x2[t % 2], 16)
            for half in range(2):
                wv = a["w_out"][0][half * 512:(half + 1) * 512, :]
                with sp.Fori(0, 4) as i:
                    for c in range(2):
                        load_block(sp, Block(f"wout{half}", c, i), cols(wv, c * P + i * 2 * P, P), P)
            wf, wo = a["w_ffn_in"][0], a["w_ffn_out"][0]

            def load_up(blk, tile, part):
                load_block(sp, blk, cols(wf, part * FF + tile * P, P), P)

            def load_down(blk, turn, part):
                rows = wo[bass.ds(turn * (2 * P), 2 * P), part * 512:(part + 1) * 512].rearrange("(k p) m -> p k m", p=P)
                load_block(sp, blk, rows, 512)
            for part in range(2):
                load_up(Block("ffn_first", part), 0, part)
            with sp.Fori(0, TURNS["ffn"]) as i:
                for part in range(2):
                    load_up(Block("ffn", part, i), i * 2 + 1, part)
                for part in range(2):
                    load_up(Block("ffn", 2 + part, i), i * 2 + 2, part)
                for part in range(2):
                    load_down(Block("ffn", 4 + part, i), i, part)
            for part in range(2):
                load_up(Block("ffn_last", part), 2 * TURNS["ffn"] + 1, part)
            for part in range(2):
                load_down(Block("ffn_last", 2 + part), TURNS["ffn"], part)
            for t in range(8):
                sp.wait_ge(m_o, upto(t + 1))
                sp.dma_start(out[0, t * P:(t + 1) * P, :], mix[:, t, :]).then_inc(s_out, 16)
            sp.wait_ge(s_out, 8 * 16)

        @blockctx.gpsimd
        def _(pool):
            seed(pool, "pool")

            def split_turns(name, sizes):
                with pool.Fori(0, TURNS[name]) as i:
                    for c, n in enumerate(sizes):
                        split_block(pool, Block(name, c, i), n)
            for c, n in enumerate((1024, 1024, 256)):
                split_block(pool, Block("lora", c), n)
            split_turns("rwkv", [1024] * 6)
            split_turns("lru", [640] * 4)
            for c in range(PER["att"]):
                if c % 3 == 0:
                    pool.wait_ge(s_kfirst, (c // 3 + 1) * 16)
                split_block(pool, Block("att", c), 1024)
            for nm, kts, *_ in BR:
                split_turns(nm, [kts * P] * 2)
            for half in range(2):
                split_turns(f"wout{half}", [512] * 2)
            for c in range(2):
                split_block(pool, Block("ffn_first", c), 1024)
            split_turns("ffn", [1024] * 6)
            for c in range(4):
                split_block(pool, Block("ffn_last", c), 1024)

        @blockctx.tensor
        def _(pe):
            mm = nc.tensor.matmul
            seed(pe, "pe")

            pe.wait_ge(s_const, 16)
            pe.wait_ge(p0_dve, upto(3))
            pe.wait_ge(s_par, N_PAR_DMA * 16)
            for k, row in enumerate((row_rw, row_lru, row_mod)):
                pe.transpose(ps[:, 4 + k, 0:P], row, ident).then_inc(p0_pe, 1)
            pe.wait_ge(p0_act, upto(1))

            def ada_columns(w, bank):
                for c in range(2):
                    for k in range(KT):
                        ins = mm(ps[:, bank, c:c + 1], w[:, k, c * P:(c + 1) * P], mod[:, 48 + k:49 + k], start=k == 0, stop=k == KT - 1)
                ins.then_inc(ada_pe, 1)

            for n in range(ADA0):
                pe.wait_ge(s_ada[n % 4], n // 4 * 16 + 16)
                pe.wait_ge(ada_out, upto(n - 3))
                ada_columns(ada_w0[:, n % 4, :, :], 4 + n % 4)
            for k in range(KT):
                if k == 0:
                    pe.wait_ge(p0_dve, upto(16))
                if k < 2:
                    pe.wait_ge(ada_out, upto(ADA0 - 2 + 2 * k))
                else:
                    pe.wait_ge(h_tmp, upto(k - 1))
                for t in range(8):
                    ins = pe.transpose(ps[:, 4 + 2 * (k % 2) + t // 4, (t % 4) * P:(t % 4 + 1) * P], xs[:, t, k * P:(k + 1) * P], ident)
                ins.then_inc(h_pe, 1)

            dense(pe, Block("lora", 0), ready=(h_lo, 0, 1))
            dense(pe, Block("lora", 1))
            pe.wait_ge(a_xp, upto(1))
            dense(pe, Block("lora", 2), width=32)
            pe.wait_ge(a_wa, upto(3))

            def sums(dst_bank, lhs, x):
                for h in range(2):
                    ins = mm(ps[:, dst_bank + h, :], lhs, x[:, h * 512:(h + 1) * 512], start=True, stop=True)
                return ins

            with pe.Fori(0, PAIRS) as i:
                pe.wait_ge(a_y, upto(i * 8))
                pe.wait_ge(v_s, upto(i * 8))
                dense(pe, Block("rwkv", 0, i))
                dense(pe, Block("rwkv", 1, i))
                pe.wait_ge(a_xp, upto(XP0 + i * 3 + 1))
                dense(pe, Block("rwkv", 2, i))
                pe.wait_ge(s_lw, i * 64 + 64)
                pe.wait_ge(v_post, upto(i * 6))
                for h in range(2):
                    hs = slice(h * 512, (h + 1) * 512)
                    mm(ps[:, 4 + h, :], rw["lw"][0:64, :], rw["wa"][0:64, hs], start=True, stop=True)
                    ins = mm(ps[:, 6 + h, :], rw["lw"][64:128, :], rw["wa"][64:128, hs], start=True, stop=True)
                ins.then_inc(r_lwa, 1)
                pe.wait_ge(a_xp, upto(XP0 + i * 3 + 2))
                dense(pe, Block("rwkv", 3, i))
                pe.wait_ge(a_sa, upto(i * 2 + 1))
                pe.wait_ge(a_sqk, upto(i + 1))
                sums(4, headsum, rw["t2"]).then_inc(r_kks, 1)
                pe.wait_ge(a_xp, upto(XP0 + i * 3 + 3))
                dense(pe, Block("rwkv", 4, i))
                pe.wait_ge(a_sa, upto(i * 2 + 2))
                for h in range(2):
                    hs = slice(h * 512, (h + 1) * 512)
                    mm(ps[:, 6 + h, :], rw["lg0"], rw["g0"][:, hs], start=True, stop=False)
                    ins = mm(ps[:, 6 + h, :], rw["lg1"][0:32, :], rw["g1"][0:32, hs], start=False, stop=True)
                ins.then_inc(r_g, 1)
                pe.wait_ge(a_gate, upto(i * 3 + 1))
                dense(pe, Block("rwkv", 5, i))
                pe.wait_ge(a_rk, upto(i + 1))
                pe.wait_ge(v_c, upto(i * VC + 7))
                sums(4, headsum, rw["t1"]).then_inc(r_bon, 1)
                pe.wait_ge(v_c, upto(i * VC + VC))
                pe.wait_ge(v_fin, upto(i + 1))
                pe.wait_ge(a_g, upto(i + 1))
                pe.wait_ge(a_gate, upto(i * 3 + 3))
                for cc in range(CHUNKS // PLACES):
                    chunks = round_of(cc)
                    for c, s, b0 in chunks:
                        if c >= PLACES:
                            pe.wait_ge(a_y, upto(i * 8 + (c - PLACES + 1)))
                            pe.wait_ge(v_s, upto(i * 8 + (c - PLACES + 1)))
                        tok = slice(c * P, (c + 1) * P)
                        for q, src in enumerate((rw["v"][:, tok], al_v[:, c, :], rw["bn"][:, tok], rw["kt"][:, tok])):
                            ins = pe.transpose(ps[:, b0 + 1, q * P:(q + 1) * P], src, ident)
                        ins.then_inc(r_tk, 1)
                    for c, s, b0 in chunks:
                        tok = slice(c * P, (c + 1) * P)
                        for h in range(2):
                            hp = slice(64 * h, 64 * h + 64)
                            if h == 1:
                                pe.wait_ge(a_tk, upto((i * 8 + c) * 2 + 2))
                            mm(ps[:, b0 + h, 0:256], rw["bn"][hp, tok], ar[hp, c, :, :], start=True, stop=True)
                            ins = mm(ps[:, b0 + h, 256:512], rw["kt"][hp, tok], ar[hp, c, :, :], start=True, stop=True)
                        ins.then_inc(r_am, 1)
                    for c, s, b0 in chunks:
                        pe.wait_ge(v_am, upto((i * 8 + c) * 2 + 2))
                        for h in range(2):
                            hp = slice(64 * h, 64 * h + 64)
                            ins = mm(ps[:, b0 + h, 0:P], al_v[hp, c, :], rw["bn"][hp, c * P:(c + 1) * P], start=True, stop=True)
                        ins.then_inc(r_x0, 1)
                    for c, s, b0 in chunks:
                        pe.wait_ge(v_x0, upto((i * 8 + c) * 2 + 2))
                        for h in range(2):
                            ins = mm(ps[:, b0 + 1, h * 64:(h + 1) * 64], am[s][:, h, 2, :], tk[s][:, 0, 64 * h:64 * h + 64], start=True, stop=True)
                        ins.then_inc(r_ak, 1)
                    for lv in range(1, LEVELS):
                        for c, s, b0 in chunks:
                            if lv > 1:
                                pe.wait_ge(v_xu, upto(xu_count(i, cc, lv - 1, s) + 2))
                            for h in range(2):
                                if lv < LEVELS - 1:
                                    ins = mm(ps[:, b0, h * P:(h + 1) * P], am[s][:, h, 0, :], xx[s][:, 0, h, :], start=True, stop=True)
                                else:
                                    ins = mm(ps[64:128, b0, h * P:h * P + 64], am[s][:, h, 0, 64:128], xx[s][:, 0, h, 0:64], start=True, stop=True)
                            ins.then_inc(r_y1, 1)
                        for c, s, b0 in chunks:
                            if lv == 1:
                                pe.wait_ge(a_ak, upto(i * 8 + c + 1))
                            pe.wait_ge(a_y1, upto(lv_count(i, cc, lv, s) + 1))
                            if lv == LEVELS - 1:
                                wait_alone(pe)
                            for h in range(2):
                                if lv < LEVELS - 1:
                                    mm(ps[:, b0 + 1, h * P:(h + 1) * P], xx[s][:, 1, h, :], y1[s][:, h, :], start=True, stop=True)
                            for h in range(2):
                                if lv < LEVELS - 1:
                                    ins = mm(ps[:, b0 + 1, (2 + h) * P:(3 + h) * P], y1[s][:, h, :], xx[s][:, 1, h, :], start=True, stop=True)
                                else:
                                    ins = mm(ps[0:64, b0 + 1, h * 64:(h + 1) * 64], y1[s][64:128, h, 0:64], xx[s][64:128, 1, h, 64:128], start=True, stop=True)
                            ins.then_inc(r_xu, 1)
                    for c, s, b0 in chunks:
                        pe.wait_ge(v_xu, upto(xu_count(i, cc, LEVELS - 1, s) + 1))
                        for h in range(2):
                            ins = mm(ps[:, b0, h * P:(h + 1) * P], xx[s][:, 1, h, :], RR[s][:, h, :], start=True, stop=True)
                        ins.then_inc(r_uw, 1)
                    for c, s, b0 in chunks:
                        pe.wait_ge(a_uw, upto(i * 8 + c + 1))
                        for h in range(2):
                            hp = slice(64 * h, 64 * h + 64)
                            mm(ps[hp, b0 + 1, 0:P], uw[s][:, h, 64:128], am[s][:, h, 1, :], start=True, stop=True)
                        for h in range(2):
                            hp = slice(64 * h, 64 * h + 64)
                            ins = mm(ps[hp, b0 + 1, P + 64 * h:P + 64 * h + 64], uw[s][:, h, 64:128], tk[s][:, 2, hp], start=True, stop=True)
                        ins.then_inc(r_gq, 1)
                    for c, s, b0 in chunks:
                        pe.wait_ge(v_q, upto((i * 8 + c) * 2 + 2))
                        if c == 0:
                            pe.wait_ge(v_zero, upto(VZ + i + 1))
                        else:
                            pe.wait_ge(v_s, upto(i * 8 + c))
                        mm(ps[:, b0, 0:P], qq[:, s, :], SS[:, c % 2, :], start=True, stop=False)
                        for h in range(2):
                            hp = slice(64 * h, 64 * h + 64)
                            mm(ps[hp, b0, hp], tk[s][:, 2, hp], uw[s][:, h, 0:64], start=False, stop=False)
                            ins = mm(ps[hp, b0, hp], tk[s][:, 3, hp], tk[s][:, 0, hp], start=False, stop=True)
                        ins.then_inc(r_s, 1)
                        mm(ps[:, b0 + 1, 0:P], SS[:, c % 2, :], gt[s], start=True, stop=False)
                        for h in range(2):
                            hp = slice(64 * h, 64 * h + 64)
                            mm(ps[hp, b0 + 1, 0:P], uw[s][:, h, 0:64], am[s][:, h, 1, :], start=False, stop=False)
                            ins = mm(ps[hp, b0 + 1, 0:P], tk[s][:, 0, hp], am[s][:, h, 3, :], start=False, stop=True)
                        ins.then_inc(r_y, 1)
                pe.wait_ge(a_y, upto(i * 8 + 8))
                pe.wait_ge(v_s, upto(i * 8 + 8))
                sums(4, headsum, rw["A"]).then_inc(r_mean, 1)
                pe.wait_ge(a_ysq, upto(i + 1))
                sums(6, headsum, rw["t1"]).then_inc(r_var, 1)

            with pe.Fori(0, TURNS["lru"]) as i:
                for u in range(2):
                    n = i * 2 + u
                    pe.wait_ge(l_x, upto(n))
                    dense(pe, Block("lru", 2 * u, i), width=80)
                    pe.wait_ge(s_ada[u], i * 16 + (ADA0 // 4 * 16 + 16))
                    pe.wait_ge(v_post, upto(PAIRS * 6))
                    pe.wait_ge(l_sa, upto(n * 2))
                    ada_columns(ada_w1[:, u, :, :], 4)
                    pe.wait_ge(l_gy, upto(n))
                    dense(pe, Block("lru", 2 * u + 1, i), width=80)
                    pe.wait_ge(l_cv, upto(n * 4 + 4))
                    pe.wait_ge(ada_out, upto(n + (ADA0 + 1)))
                    pe.wait_ge(s_lw2[u], i * 32 + 32)
                    for q, w in enumerate(("wa", "wx")):
                        for h in range(2):
                            ins = mm(ps[0:80, 4 + 2 * q + h, :], lr[w][0:80, 80 * u:80 * u + 80], lr["xa"][0:80, h * 512:(h + 1) * 512], start=True, stop=True)
                    ins.then_inc(l_pe, 1)

            def project(gg):
                if gg >= 2:
                    before = (gg - 1) * UNITS
                    pe.wait_ge(t_oc, upto(before))
                    pe.wait_ge(t_d, upto(before * 4))
                    pe.wait_ge(t_ptc, upto(before))
                for c in range(3):
                    n = gg * 3 + c
                    if gg == 0 and c < 2:
                        pe.wait_ge((l_x, l_gy)[c], upto(LRU_N))
                        if c == 1:
                            pe.wait_ge(l_sa, upto(LRU_N * 2))
                    else:
                        pe.wait_ge(t_cp, upto(n - 1))
                    dense(pe, Block("att", n))
                    if c == 1:
                        pe.wait_ge(t_cp, upto(n))
                        for b in range(8):
                            ins = pe.transpose(ps[:, 6 + b // 4, (b % 4) * P:(b % 4 + 1) * P], at_["kvt"][:, b * P:(b + 1) * P], ident)
                        ins.then_inc(t_vt, 1)
                    if c > 0:
                        pe.wait_ge(t_sq, upto(n))
                        pe.wait_ge(t_rt, upto(n - 1))
                        sums(4, headsum, squares[:, (n - 1) % 2, :]).then_inc(t_ns, 1)
                pe.wait_ge(t_sq, upto(n + 1))
                pe.wait_ge(t_v, upto(gg + 1))
                sums(6, headsum, squares[:, n % 2, :]).then_inc(t_ns, 1)

            def attend(gg):
                pe.wait_ge(t_n, upto(gg * 3 + 3))
                pe.wait_ge(t_k2, upto(gg + 1))
                pe.wait_ge(t_v, upto(gg + 1))
                done = min(gg + 2, GROUPS) * 3
                pe.wait_ge(t_cp, upto(done))
                pe.wait_ge(t_rt, upto(done))
                for tick in range(UNITS + 3):
                    if tick < UNITS:
                        u, t, n = tick, tick // 8, tick % 8
                        if u >= 2:
                            pe.wait_ge(t_d, upto((gg * UNITS + u - 2) * 4 + 1))
                        for h in range(2):
                            hp = slice(64 * h, 64 * h + 64)
                            ins = mm(ps[:, 4 - 2 * (u % 2) + h, 0:256], aq[gg % 2][hp, t, n * P:(n + 1) * P], ak[hp, gg % 2, n * P:n * P + 256], start=True, stop=True)
                        ins.then_inc(t_sc, 1)
                    if 0 <= tick - 2 < UNITS:
                        u = tick - 2
                        pe.wait_ge(t_p, upto((gg * UNITS + u) * 2 + 2))
                        if u >= 2:
                            pe.wait_ge(t_ptc, upto(gg * UNITS + u - 1))
                        for h in range(2):
                            for kb in range(2):
                                ins = pe.transpose(ps[:, 6 + u % 2, (2 * h + kb) * P:(2 * h + kb + 1) * P], asc[:, u % 4, h, kb * P:(kb + 1) * P], ident)
                        ins.then_inc(t_pt, 1)
                    if 0 <= tick - 3 < UNITS:
                        u, t, n = tick - 3, (tick - 3) // 8, (tick - 3) % 8
                        pe.wait_ge(t_ptc, upto(gg * UNITS + u + 1))
                        if u >= 2:
                            pe.wait_ge(t_oc, upto(gg * UNITS + u - 1))
                        for h in range(2):
                            hp = slice(64 * h, 64 * h + 64)
                            for kb in range(2):
                                ins = mm(ps[hp, u % 2, 0:P], av[:, gg % 2, n + kb, :], apt[:, u % 4, (2 * h + kb) * P:(2 * h + kb + 1) * P], start=kb == 0, stop=kb == 1)
                        ins.then_inc(t_o, 1)

            project(0)
            for gg in range(GROUPS):
                if gg + 1 < GROUPS:
                    project(gg + 1)
                attend(gg)

            pe.wait_ge(t_oc, upto(64))
            pe.wait_ge(t_ptc, upto(64))
            for g, (nm, kts, *_) in enumerate(BR):
                for i in range(4):
                    for c in range(2):
                        n = g * 8 + i * 2 + c
                        if n >= 2:
                            pe.wait_ge(m_ev, upto(first_step(n - 2)))
                        dense(pe, Block(nm, c, i), tiles=kts, first=HALF * (g % 2), ready=(m_lo, Y0[g], 1))
            for t in range(8):
                pe.wait_ge(s_x2[t % 2], 16 * (t // 2 + 1))
                if t >= 2:
                    pe.wait_ge(m_xt, upto(t - 1))
                for k in range(KT):
                    ins = pe.transpose(ps[:, 4 + 2 * (t % 2) + k // 4, (k % 4) * P:(k % 4 + 1) * P], yraw[:, t % 2, k * P:(k + 1) * P], ident)
                ins.then_inc(m_pe, 1)
            for half in range(2):
                first = (HALF * (len(BR) % 2) + HALF * half) % KT
                for i in range(4):
                    for c in range(2):
                        if half == 0:
                            pe.wait_ge(m_ev, upto(EV_ALL))
                        pe.wait_ge(m_res, upto(half * 8 + i * 2 + c - 1))
                        dense(pe, Block(f"wout{half}", c, i), tiles=HALF, first=first, ready=(m_lo, NY + HALF * half, 1))
            for k in range(KT):
                pe.wait_ge(m_sq, upto(k + 1))
                for h in range(2):
                    ins = mm(ps[:, 4 + h, :], ones, mt[:, k % 2, h * 512:(h + 1) * 512], start=k == 0, stop=k == KT - 1)
                ins.then_inc(m_ss, 1)

            def up(blk_gate, blk_up, tile, ready=None):
                pe.wait_ge(m_sil, upto(tile))
                dense(pe, blk_gate, ready=ready)
                pe.wait_ge(m_act, upto(tile))
                dense(pe, blk_up)

            def down(name, c0, i, turn):
                pe.wait_ge(m_hl, upto(turn * 2 + 2))
                for m in range(8):
                    blk = Block(name, c0 + m // 4, i)
                    if m % 4 == 0:
                        pe.wait_ge(s_wsplit, upto(blk.before + 1))
                    if m < 2:
                        pe.wait_ge(m_dn, upto(turn * 8))
                    else:
                        pe.wait_ge(m_dn, upto(turn * 8 + m - 1))
                    dst = [ps[:, 4 + 2 * (m % 2) + h, :] for h in range(2)]
                    for k in range(FF_GROUP):
                        at = k * 512 + (m % 4) * P
                        w = [t[:, blk.slot, at:at + P] for t in (w_hi, w_lo)]
                        x = [[t[:, k, h * 512:(h + 1) * 512] for h in range(2)] for t in (hid_hi, hid_lo)]
                        ins = three_passes(dst, w, x, k == 0, k == FF_GROUP - 1)
                    ins.then_inc(s_dense if m % 4 == 3 else m_dd, 1)
            up(Block("ffn_first", 0), Block("ffn_first", 1), 0, ready=(m_nh, 0, 2))
            with pe.Fori(0, TURNS["ffn"]) as i:
                up(Block("ffn", 0, i), Block("ffn", 1, i), i * 2 + 1)
                up(Block("ffn", 2, i), Block("ffn", 3, i), i * 2 + 2)
                down("ffn", 4, i, i)
            up(Block("ffn_last", 0), Block("ffn_last", 1), 2 * TURNS["ffn"] + 1)
            down("ffn_last", 2, 0, TURNS["ffn"])
            pe.wait_ge(m_dn, upto((TURNS["ffn"] + 1) * 8))
            for t in range(8):
                if t >= 2:
                    pe.wait_ge(m_o, upto(t - 1))
                for k in range(KT):
                    ins = pe.transpose(ps[:, 4 + 2 * (t % 2) + k // 4, (k % 4) * P:(k % 4 + 1) * P], x2[:, k, t * P:(t + 1) * P], ident)
                ins.then_inc(m_op, 1)

        @blockctx.scalar
        def _(act):
            fn = nc.scalar.activation
            seed(act, "act")
            act.wait_ge(p0_dve, upto(6))
            fn(mod[:, 48:56], mod[:, 48:56], ACT.Silu).then_inc(p0_act, 1)
            fn(rate2[0:80, :], rate[0:80, :], ACT.Exp, scale=-1.0).then_inc(p0_act, 1)
            for t in range(8):
                act.wait_ge(s_x, 16 * 8)
                if t >= 2:
                    act.wait_ge(p0_act, upto(t + 1))
                fn(sq0[:, t % 2, :], xs[:, t, :], ACT.Square, accum_out=sumsq[:, t:t + 1]).then_inc(p0_act, 1)
            act.wait_ge(p0_dve, upto(7))
            fn(rstd, rstd, ACT.Sqrt).then_inc(p0_act, 1)
            for k in range(KT):
                act.wait_ge(h_tmp, upto(k + 1))
                fn(x_hi[:, k, :], h_tmpb[:, k % 2, :], ACT.Copy).then_inc(h_hi, 1)

            xp = rw["xp"]

            def copy_stream(blk, count, mixed, width=P):
                act.wait_ge(s_dense, upto(blk.before + 1))
                act.wait_ge(v_mix, upto(mixed))
                fn(halves(xp[0:width, 1:T + 1]), ps[0:width, 2 * blk.slot:2 * blk.slot + 2, :], ACT.Copy).then_inc(a_xp, 1)

            act.wait_ge(v_zero, upto(VZ))
            for c, width in enumerate((P, P, 32)):
                copy_stream(Block("lora", c), c, 2 * c, width)
                act.wait_ge(v_mix, upto(2 * c + 2))
                if c == 0:
                    fn(rw["wa"][0:64, :], rw["wa"][0:64, :], ACT.Tanh).then_inc(a_wa, 1)
                else:
                    t = rw["g0"] if c == 1 else rw["g1"][0:32, :]
                    fn(t, t, ACT.Sigmoid).then_inc(a_wa, 1)

            with act.Fori(0, PAIRS) as i:
                par = lambda c: rw_par[:, bass.ds(i + c, 1)]
                for s in range(3):
                    copy_stream(Block("rwkv", s, i), None, XM0 + i * 6 + 2 * s)

                def gate(c):
                    blk = Block("rwkv", 3 + c, i)
                    act.wait_ge(s_dense, upto(blk.before + 1))
                    act.wait_ge(s_gst, upto(i * 48 + c * 16))
                    fn(halves(rw["gs"]), pair_of(blk.slot), ACT.Sigmoid).then_inc(a_gate, 1)
                    act.wait_ge(a_gate, upto(i * 3 + c + 1))
                    act.dma_start(gates[bass.ds(c * D + i * P, P), :], rw["gs"]).then_inc(s_gst, 16)

                act.wait_ge(r_lwa, upto(i + 1))
                fn(halves(rw["sig"]), ps[:, 4:6, :], ACT.Sigmoid, bias=par(PR_W0)).then_inc(a_sa, 1)
                fn(halves(rw["A"]), ps[:, 6:8, :], ACT.Sigmoid, bias=par(PR_A0)).then_inc(a_sa, 1)
                act.wait_ge(v_kk, upto(i + 1))
                act.wait_ge(s_yb, upto(i * 16))
                fn(rw["t2"], rw["t1"], ACT.Square).then_inc(a_sqk, 1)
                gate(0)
                act.wait_ge(r_kks, upto(i + 1))
                fn(halves(rw["t2"]), ps[:, 4:6, :], ACT.Sqrt).then_inc(a_rk, 1)
                gate(1)
                act.wait_ge(r_g, upto(i + 1))
                fn(halves(rw["g"]), ps[:, 6:8, :], ACT.Copy).then_inc(a_g, 1)
                act.wait_ge(v_c, upto(i * VC + 18))
                fn(rw["ff"], rw["df"][:, 0:8], ACT.Exp, scale=-DECAY).then_inc(a_f, 1)
                act.wait_ge(v_c, upto(i * VC + 20))
                fn(rw["sig"], rw["sig"], ACT.Exp, scale=-DECAY).then_inc(a_exp, 1)
                fn(rw["t2"], rw["L"], ACT.Exp, scale=-DECAY).then_inc(a_exp, 1)
                act.wait_ge(a_exp, upto(i * 3 + 2))
                fn(rw["L"], rw["L"], ACT.Exp, scale=DECAY).then_inc(a_exp, 1)
                gate(2)
                for cc in range(CHUNKS // PLACES):
                    chunks = round_of(cc)
                    for c, s, b0 in chunks:
                        act.wait_ge(r_tk, upto(i * 8 + c + 1))
                        fn(tk[s], ps[:, b0 + 1, :].rearrange("p (q n) -> p q n", q=4), ACT.Copy).then_inc(a_tk, 1)
                        fn(RR[s][:, :, 64:128], ps[:, b0 + 1, P:2 * P].rearrange("p (h n) -> p h n", h=2), ACT.Copy).then_inc(a_tk, 1)
                        fn(xx[s].rearrange("p o h n -> p (o h) n"), ident.unsqueeze(1).broadcast_to([P, 4, P]), ACT.Copy).then_inc(a_xi, 1)
                    for c, s, b0 in chunks:
                        act.wait_ge(r_ak, upto(i * 8 + c + 1))
                        fn(RR[s][:, :, 0:64], ps[:, b0 + 1, 0:P].rearrange("p (h n) -> p h n", h=2), ACT.Copy).then_inc(a_ak, 1)
                    for lv in range(1, LEVELS):
                        for c, s, b0 in chunks:
                            act.wait_ge(r_y1, upto(lv_count(i, cc, lv, s) + 1))
                            rows = slice(0, P) if lv < LEVELS - 1 else slice(64, P)
                            fn(blocks_of(y1[s][rows], lv, 0), blocks_of(per_head(ps[rows, b0, 0:256]), lv, 0), ACT.Copy).then_inc(a_y1, 1)
                    for c, s, b0 in chunks:
                        act.wait_ge(r_uw, upto(i * 8 + c + 1))
                        fn(uw[s], ps[:, b0, 0:256].rearrange("p (h n) -> p h n", h=2), ACT.Copy).then_inc(a_uw, 1)
                    for c, s, b0 in chunks:
                        act.wait_ge(r_y, upto(i * 8 + c + 1))
                        fn(rw["A"][:, c * P:(c + 1) * P], ps[:, b0 + 1, 0:P], ACT.Copy).then_inc(a_y, 1)
                act.wait_ge(v_post, upto(i * 6 + 1))
                fn(rw["t1"], rw["t2"], ACT.Square).then_inc(a_ysq, 1)
                act.wait_ge(r_var, upto(i + 1))
                fn(halves(rw["t1"]), ps[:, 6:8, :], ACT.Sqrt, scale=1.0 / RW_H, bias=eps_ln).then_inc(a_yr, 1)
                act.wait_ge(v_post, upto(i * 6 + 6))
                act.dma_start(y_b[bass.ds(i * P, P), :], rw["t2"]).then_inc(s_yb, 16)

            with act.Fori(0, TURNS["lru"]) as i:
                for u in range(2):
                    n = i * 2 + u
                    lp = lambda c: lru_par[0:80, bass.ds(n + c, 1)]
                    act.wait_ge(s_dense, upto(Block("lru", 2 * u, i).before + 1))
                    act.wait_ge(l_cv, upto(n * 4))
                    act.wait_ge(l_z, upto(1))
                    fn(halves(lr["xp"][0:80, 3:T + 3]), pair_of(Block("lru", 2 * u, i).slot)[0:80], ACT.Copy).then_inc(l_x, 1)
                    act.wait_ge(l_pe, upto(n + 1))
                    act.wait_ge(l_u, upto(n * 3))
                    fn(halves(lr["ga"][0:80]), ps[0:80, 4:6, :], ACT.Sigmoid, bias=lp(LP_BA)).then_inc(l_sa, 1)
                    fn(halves(lr["gx"][0:80]), ps[0:80, 6:8, :], ACT.Sigmoid, bias=lp(LP_BX)).then_inc(l_sa, 1)
                    act.wait_ge(l_sa, upto(n * 2 + 2))
                    fn(lr["a2"][0:80], lr["ga"][0:80], ACT.Exp, scale=rate2[0:80, bass.ds(n, 1)]).then_inc(l_exp, 1)
                    fn(lr["aa"][0:80], lr["ga"][0:80], ACT.Exp, scale=rate[0:80, bass.ds(n, 1)]).then_inc(l_exp, 1)
                    act.wait_ge(l_sq, upto(n + 1))
                    fn(lr["a2"][0:80], lr["a2"][0:80], ACT.Sqrt, scale=-1.0, bias=one_b[0:80, :]).then_inc(l_rt, 1)
                    act.wait_ge(l_out, upto(n))
                    fn(halves(lr["gy"][0:80]), pair_of(Block("lru", 2 * u + 1, i).slot)[0:80], ACT.Gelu_apprx_tanh).then_inc(l_gy, 1)
                    act.wait_ge(l_out, upto(n + 1))
                    act.dma_start(y_a[bass.ds(n * 80, 80), :], lr["ya"][0:80]).then_inc(s_ya, 16)

            def project(gg):
                def copy_and_square(c):
                    n = gg * 3 + c
                    blk = Block("att", n)
                    tile = at_["kvt"] if c == 0 else aq[gg % 2][:, c - 1, :]
                    act.wait_ge(s_dense, upto(blk.before + 1))
                    if c == 0 and gg > 0:
                        act.wait_ge(t_n, upto(n - 2))
                        act.wait_ge(t_vt, upto(gg))
                    if c > 0 and gg >= 2:
                        act.wait_ge(t_sc, upto((gg - 1) * UNITS))
                    fn(halves(tile), pair_of(blk.slot), ACT.Copy).then_inc(t_cp, 1)
                    act.wait_ge(t_cp, upto(n + 1))
                    if n >= 2:
                        act.wait_ge(t_ns, upto(n - 1))
                    fn(squares[:, n % 2, :], tile, ACT.Square).then_inc(t_sq, 1)

                def root(c):
                    n = gg * 3 + c
                    act.wait_ge(t_ns, upto(n + 1))
                    if gg > 0:
                        act.wait_ge(t_n, upto(n - 2))
                    banks = ps[:, 6:8, :] if c == 2 else ps[:, 4:6, :]
                    fn(halves(roots[:, c, :]), banks, ACT.Sqrt, scale=1.0 / HEAD, bias=eps_qk).then_inc(t_rt, 1)
                copy_and_square(0)
                copy_and_square(1)
                act.wait_ge(t_vt, upto(gg + 1))
                act.wait_ge(t_z, upto(4))
                fn(av[:, gg % 2, 1:9, :], ps[:, 6:8, :].rearrange("p b (n e) -> p (b n) e", e=P)[:, :, 64:128], ACT.Copy).then_inc(t_v, 1)
                root(0)
                copy_and_square(2)
                root(1)
                root(2)
                act.wait_ge(t_n, upto(gg * 3 + 1))
                fn(ak[64:128, gg % 2, P:T + P], ak[0:64, gg % 2, P:T + P], ACT.Copy).then_inc(t_k2, 1)

            def attend(gg):
                for tick in range(UNITS + 3):
                    if tick < UNITS:
                        u = tick
                        act.wait_ge(t_d, upto((gg * UNITS + u) * 4 + 4))
                        sm = asm[:, u % 4, :]
                        for h in range(2):
                            fn(asc[:, u % 4, h, :], asc[:, u % 4, h, :], ACT.Exp, bias=sm[:, 2 + h:3 + h], accum_out=sm[:, 4 + h:5 + h]).then_inc(t_e, 1)
                        fn(sm[:, 6:8], sm[:, 6:8], ACT.Exp).then_inc(t_e, 1)
                    if 0 <= tick - 2 < UNITS:
                        u = tick - 2
                        act.wait_ge(t_pt, upto(gg * UNITS + u + 1))
                        fn(apt[:, u % 4, :], ps[:, 6 + u % 2, :], ACT.Copy).then_inc(t_ptc, 1)
                    if 0 <= tick - 3 < UNITS:
                        u, t, n = tick - 3, (tick - 3) // 8, (tick - 3) % 8
                        act.wait_ge(t_o, upto(gg * UNITS + u + 1))
                        if n == 0:
                            act.wait_ge(s_yc[t], upto(gg * 16))
                        fn(ayc[:, t, n * P:(n + 1) * P], ps[:, u % 2, 0:P], ACT.Copy).then_inc(t_oc, 1)
                        if n == 7:
                            act.wait_ge(t_oc, upto(gg * UNITS + u + 1))
                            act.dma_start(y_c[(gg * 2 + t) * P:(gg * 2 + t + 1) * P, :], ayc[:, t, :]).then_inc(s_yc[t], 16)
                    if gg == GROUPS - 1 and tick in Y_TICKS:
                        high_y(0, Y_TICKS.index(tick))

            def high_y(g, k):
                act.wait_ge(s_dense, upto(Block(BR[max(g - 1, 0)][0], 0).before))
                act.wait_ge(s_y[(Y0[g] + k) % 2], 16 * ((Y0[g] + k) // 2 + 1))
                fn(x_hi[:, HALF * (g % 2) + k, :], yraw[:, (Y0[g] + k) % 2, :], ACT.Copy).then_inc(m_hi, 1)
            project(0)
            for gg in range(GROUPS):
                if gg + 1 < GROUPS:
                    project(gg + 1)
                attend(gg)

            for g in range(1, len(BR)):
                for k in range(BR[g][1]):
                    high_y(g, k)
            for m in range(KT):
                at = (HALF * (len(BR) % 2) + m) % KT
                if m == 0:
                    act.wait_ge(s_dense, upto(Block("ob1", 0).before))
                if m == HALF:
                    act.wait_ge(s_dense, upto(Block("wout0", 0).before))
                act.wait_ge(m_ev, upto(EV0["ob1"] + 3 * (m + 1)))
                fn(x_hi[:, at, :], mix[:, m, :], ACT.Copy).then_inc(m_hi, 1)
            act.wait_ge(m_ev, upto(EV_ALL))
            for t in range(8):
                act.wait_ge(m_pe, upto(t + 1))
                fn(x2[:, :, t * P:(t + 1) * P], ps[:, 4 + 2 * (t % 2):6 + 2 * (t % 2), :].rearrange("p b (k n) -> p (b k) n", n=P), ACT.Copy).then_inc(m_xt, 1)
            for k in range(KT):
                act.wait_ge(m_res, upto(KT + k + 1))
                if k >= 2:
                    act.wait_ge(m_ss, upto(k - 1))
                fn(mt[:, k % 2, :], x2[:, k, :], ACT.Square).then_inc(m_sq, 1)
            act.wait_ge(m_ss, upto(KT))
            fn(halves(yraw[:, 0, :]), ps[:, 4:6, :], ACT.Sqrt, scale=1.0 / D, bias=eps_rms).then_inc(m_rt, 1)
            for k in range(KT):
                act.wait_ge(m_nh, upto(2 * k + 1))
                fn(x_hi[:, k, :], mt[:, k % 2, :], ACT.Identity, bias=mod[:, MOD_SH2 + k:MOD_SH2 + k + 1]).then_inc(m_hi, 1)

            def hidden(blk, tile, t):
                act.wait_ge(s_dense, upto(blk.before + 1))
                act.wait_ge(m_act, upto(tile))
                fn(halves(gtl[:, 0, :]), pair_of(blk.slot), ACT.Silu).then_inc(m_sil, 1)

            def hidden_high(tile, t):
                act.wait_ge(m_act, upto(tile + 1))
                fn(hid_hi[:, t, :], mt[:, t, :], ACT.Copy).then_inc(m_hh, 1)
            hidden(Block("ffn_first", 0), 0, 0)
            hidden_high(0, 0)
            with act.Fori(0, TURNS["ffn"]) as i:
                hidden(Block("ffn", 0, i), i * 2 + 1, 1)
                hidden_high(i * 2 + 1, 1)
                hidden(Block("ffn", 2, i), i * 2 + 2, 0)
                act.wait_ge(s_dense, upto(Block("ffn", 5, i).before + 1))
                hidden_high(i * 2 + 2, 0)
            hidden(Block("ffn_last", 0), 2 * TURNS["ffn"] + 1, 1)
            hidden_high(2 * TURNS["ffn"] + 1, 1)
            for t in range(8):
                act.wait_ge(m_op, upto(t + 1))
                fn(halves(mix[:, t, :]), ps[:, 4 + 2 * (t % 2):6 + 2 * (t % 2), :], ACT.Copy).then_inc(m_o, 1)

        @blockctx.vector
        def _(dve):
            v = nc.vector
            seed(dve, "dve")
            steps = [0]

            def step(ins):
                steps[0] += 1
                ins.then_inc(p0_dve, 1)
                dve.wait_ge(p0_dve, upto(steps[0]))

            for row in (row_rw, row_lru, row_mod):
                step(v.memset(row, 0.0))
            for k, dst in enumerate((rw_par, lru_par)):
                dve.wait_ge(p0_pe, upto(k + 1))
                step(v.tensor_copy(dst[:, :], ps[:, 4 + k, 0:P]))
            dve.wait_ge(p0_pe, upto(3))
            lam = lru_par[0:80, LP_LAM:LP_LAM + 16]
            v.tensor_scalar(rate[0:80, :], lam, -1.0, None, ALU.mult).then_inc(lam_s, 1)
            dve.wait_ge(lam_s, upto(1))
            v.tensor_tensor(rate[0:80, :], rate[0:80, :], lam, ALU.max).then_inc(lam_s, 1)
            dve.wait_ge(lam_s, upto(2))
            step(v.tensor_copy(mod[:, :], ps[:, 6, 0:56]))
            def ada_pair(bank, n):
                dve.wait_ge(ada_pe, upto(n + 1))
                cols2 = mod[:, bass.ds(n * 2, 2)]
                v.tensor_tensor(cols2, ps[:, bank, 0:2], cols2, ALU.add).then_inc(ada_out, 1)

            for n in range(4):
                ada_pair(4 + n % 4, n)
            dve.wait_ge(p0_act, upto(10))
            step(v.tensor_scalar(rstd, sumsq, 1.0 / D, 1e-6, ALU.mult, ALU.add))
            dve.wait_ge(p0_act, upto(11))
            step(v.reciprocal(rstd, rstd))
            for t in range(8):
                step(v.tensor_scalar(xs[:, t, :], xs[:, t, :], rstd[:, t:t + 1], None, ALU.mult))
            for n in range(4, ADA0):
                ada_pair(4 + n % 4, n)
            dve.wait_ge(ada_out, upto(ADA0))
            v.tensor_scalar(mod[:, MOD_SC1:MOD_SC1 + 8], mod[:, MOD_SC1:MOD_SC1 + 8], 1.0, None, ALU.add).then_inc(ada_fix, 1)
            dve.wait_ge(ada_fix, upto(1))

            def modulate(k):
                dve.wait_ge(h_pe, upto(k + 1))
                if k >= 2:
                    dve.wait_ge(h_lo, upto(k - 1))
                v.tensor_scalar(halves(h_tmpb[:, k % 2, :]), pair_of(2 + k % 2), mod[:, MOD_SC1 + k:MOD_SC1 + k + 1], mod[:, MOD_SH1 + k:MOD_SH1 + k + 1],
                                ALU.mult, ALU.add).then_inc(h_tmp, 1)
            modulate(0)
            for k in range(KT):
                if k + 1 < KT:
                    modulate(k + 1)
                dve.wait_ge(h_hi, upto(k + 1))
                v.tensor_tensor(x_lo[:, k, :], h_tmpb[:, k % 2, :], x_hi[:, k, :].bitcast(F32), ALU.subtract).then_inc(h_lo, 1)
            e, z = rate2[0:80, :], small[0:80, 66:82]
            z2 = lsc[0:80, 0:16]
            acc = lsc[0:80, 16:32]
            step(v.tensor_scalar(z, e, 2.0, None, ALU.add))
            step(v.reciprocal(z, z))
            step(v.tensor_tensor(z, z, e, ALU.mult))
            step(v.tensor_tensor(z2, z, z, ALU.mult))
            step(v.tensor_scalar(acc, z2, 2.0 / 19, 2.0 / 17, ALU.mult, ALU.add))
            for m in (15, 13, 11, 9, 7, 5, 3, 1):
                step(v.tensor_tensor(acc, acc, z2, ALU.mult))
                step(v.tensor_scalar(acc, acc, 2.0 / m, None, ALU.add))
            step(v.tensor_tensor(acc, acc, z, ALU.mult))
            step(v.tensor_scalar(z, lam, -1.0, 0.0, ALU.mult, ALU.max))
            step(v.tensor_tensor(acc, acc, z, ALU.add))
            step(v.tensor_scalar(rate[0:80, :], acc, -8.0, None, ALU.mult))
            step(v.tensor_scalar(rate2[0:80, :], acc, -16.0, None, ALU.mult))
            for k, val in enumerate((1e-6, 64e-5, 1.0)):
                step(v.memset(bias_t[:, k:k + 1], val))
            assert steps[0] == 6 + 1 + 1 + 8 + SOFT, steps[0]

            dve.wait_ge(h_lo, upto(KT))
            v.memset(rw["xp"][:, 0:1], 0.0).then_inc(v_zero, 1)
            v.memset(rw["q"], 0.0).then_inc(v_zero, 1)
            for s in (0, 1, 3):
                v.memset(places[s]["y1"], 0.0).then_inc(v_zero, 1)
            dve.wait_ge(s_mask, 32)
            v.tensor_copy(hid_lo[:, :, :].rearrange("p a n -> p (a n)")[:, 0:2 * LEVELS * P], rw["ar"][:, 0:2 * LEVELS * P]).then_inc(mask_ready, 1)
            v.tensor_copy(masks[:, 0:256], rw["bn"][:, 0:256]).then_inc(mask_ready, 1)
            dve.wait_ge(mask_ready, upto(2))

            def level_mask(lv, o):
                m = lv_mask[:, (2 * lv + o) * P:(2 * lv + o + 1) * P].bitcast(I32).unsqueeze(1).broadcast_to([P, 2, P])
                return blocks_of(m, lv, o)
            xp = rw["xp"]

            def mix_stream(copied, mixed, dst, mu, width=P, view=None):
                dve.wait_ge(a_xp, upto(copied))
                x0, x1, t = xp[0:width, 0:T], xp[0:width, 1:T + 1], rw["t1"][0:width, :]
                v.tensor_tensor(t, x0, x1, ALU.subtract).then_inc(v_mix, 1)
                dve.wait_ge(v_mix, upto(mixed + 1))
                if view is not None:
                    t, x1 = view(t), view(x1)
                v.scalar_tensor_tensor(dst, t, mu, x1, ALU.mult, ALU.add).then_inc(v_mix, 1)
                dve.wait_ge(v_mix, upto(mixed + 2))
            for c, (dst, width) in enumerate(((rw["wa"], P), (rw["g0"], P), (rw["g1"][0:32, :], 32))):
                mix_stream(c + 1, 2 * c, dst, rw_par[0:width, PR_MU_WA + c:PR_MU_WA + c + 1], width)

            with dve.Fori(0, PAIRS) as i:
                par = lambda c: rw_par[:, bass.ds(i + c, 1)]
                count = [0]

                def prep(ins, wait=True):
                    count[0] += 1
                    ins.then_inc(v_c, 1)
                    if wait:
                        dve.wait_ge(v_c, upto(i * VC + count[0]))

                for s, (dst, view) in enumerate(((rt_v, chunked), (rw["kt"], None), (rw["v"], None))):
                    mix_stream(XP0 + i * 3 + s + 1, XM0 + i * 6 + 2 * s, dst, par(PR_MU + 8 * s), view=view)
                t1, t2, A, L, sig, bn, kt = (rw[n] for n in ("t1", "t2", "A", "L", "sig", "bn", "kt"))
                v.tensor_scalar(t1, kt, par(PR_KK), None, ALU.mult).then_inc(v_kk, 1)
                v.memset(SS[:, 0, :], 0.0).then_inc(v_zero, 1)
                dve.wait_ge(a_sa, upto(i * 2 + 2))
                prep(v.tensor_scalar(bn, A, -1.0, par(PR_KA), ALU.add, ALU.mult))
                dve.wait_ge(a_rk, upto(i + 1))
                prep(v.tensor_scalar(t2, t2, 1e-12, None, ALU.max))
                prep(v.reciprocal(t2, t2))
                prep(v.tensor_tensor(al_v, chunked(t1), chunked(t2), ALU.mult))
                prep(v.scalar_tensor_tensor(kt, bn, 1.0, kt, ALU.add, ALU.mult))
                prep(v.scalar_tensor_tensor(chunked(bn), al_v, -1.0, chunked(A), ALU.mult, ALU.mult))
                prep(v.scalar_tensor_tensor(chunked(t1), rt_v, par(PR_RK), chunked(kt), ALU.mult, ALU.mult))
                for c in range(CHUNKS):
                    tok = slice(c * P, (c + 1) * P)
                    prep(v.tensor_tensor_scan(L[:, tok], sig[:, tok], sig[:, tok], 0.0, ALU.add, ALU.max), wait=c == CHUNKS - 1)
                Lc, df, mid = chunked(L), rw["df"][:, 0:8], rw["df"][:, 8:16]
                prep(v.tensor_copy(mid.unsqueeze(2), Lc[:, :, 63:64]))
                prep(v.tensor_tensor(df.unsqueeze(2), Lc[:, :, 127:128], mid.unsqueeze(2), ALU.subtract))
                prep(v.tensor_tensor(df[:, 0:7], df[:, 0:7], mid[:, 1:8], ALU.add))
                prep(v.tensor_tensor(Lc, Lc, mid.unsqueeze(2).broadcast_to([P, CHUNKS, P]), ALU.subtract))
                prep(v.tensor_tensor(sig, L, sig, ALU.subtract))
                dve.wait_ge(a_exp, upto(i * 3 + 1))
                prep(v.tensor_tensor(al_v, al_v, chunked(sig), ALU.mult), wait=False)
                dve.wait_ge(a_exp, upto(i * 3 + 2))
                prep(v.tensor_tensor(rt_v, rt_v, chunked(t2), ALU.mult), wait=False)
                dve.wait_ge(a_exp, upto(i * 3 + 3))
                prep(v.tensor_tensor(bn, bn, L, ALU.mult), wait=False)
                prep(v.tensor_tensor(kt, kt, L, ALU.mult), wait=False)
                assert count[0] == VC
                dve.wait_ge(r_bon, upto(i + 1))
                v.tensor_tensor(halves(rw["bv"]), ps[:, 4:6, :], halves(rw["v"]), ALU.mult).then_inc(v_fin, 1)
                dve.wait_ge(a_f, upto(i + 1))
                for cc in range(CHUNKS // PLACES):
                    chunks = round_of(cc)
                    for c, s, b0 in chunks:
                        dve.wait_ge(r_am, upto(i * 8 + c + 1))
                        for h in range(2):
                            v.tensor_tensor(am[s][:, h, :, :].rearrange("p (q o) n -> p q (o n)", q=2), ps[:, b0 + h, :].rearrange("p (q n) -> p q n", q=2),
                                            am_mask.bitcast(F32).unsqueeze(1).broadcast_to([P, 2, 256]), ALU.mult).then_inc(v_am, 1)
                    for c, s, b0 in chunks:
                        n = i * 8 + c
                        dve.wait_ge(v_am, upto(n * 2 + 2))
                        dve.wait_ge(a_xi, upto(n + 1))
                        wait_alone(dve)
                        v.copy_predicated(blocks_of(xx[s][:, 1, :, :], 0, 1), level_mask(0, 1), blocks_of(am[s][:, :, 0, :], 0, 1)).then_inc(v_x0, 1)
                        dve.wait_ge(r_x0, upto(n + 1))
                        wait_alone(dve)
                        v.copy_predicated(blocks_of(xx[s][:, 0, :, :], 0, 0), level_mask(0, 0), blocks_of(ps[:, b0:b0 + 2, 0:P], 0, 0)).then_inc(v_x0, 1)
                    for lv in range(1, LEVELS):
                        for c, s, b0 in chunks:
                            dve.wait_ge(r_xu, upto(lv_count(i, cc, lv, s) + 1))
                            if lv == LEVELS - 1:
                                v.tensor_copy(xx[s][0:64, 1, :, 64:128], per_head(ps[0:64, b0 + 1, 0:P])).then_inc(v_xu, 1)
                            else:
                                for o in range(2):
                                    wait_alone(dve)
                                    part = per_head(ps[:, b0 + 1, o * 256:(o + 1) * 256])
                                    v.copy_predicated(blocks_of(xx[s][:, o, :, :], lv, o), level_mask(lv, o), blocks_of(part, lv, o)).then_inc(v_xu, 1)
                    for c, s, b0 in chunks:
                        dve.wait_ge(r_gq, upto(i * 8 + c + 1))
                        v.tensor_tensor(gt[s], ps[:, b0 + 1, 0:P], rt_v[:, c, :], ALU.add).then_inc(v_gt, 1)
                        for h in range(2):
                            hp = slice(64 * h, 64 * h + 64)
                            v.tensor_tensor(qq[hp, s, hp], ps[hp, b0 + 1, P + 64 * h:P + 64 * h + 64], ident[hp, hp], ALU.add).then_inc(v_q, 1)
                    for c, s, b0 in chunks:
                        dve.wait_ge(r_s, upto(i * 8 + c + 1))
                        v.tensor_scalar(SS[:, (c + 1) % 2, :], ps[:, b0, 0:P], rw["ff"][:, c:c + 1], None, ALU.mult).then_inc(v_s, 1)
                post = [0]

                def after(ins):
                    post[0] += 1
                    ins.then_inc(v_post, 1)
                    dve.wait_ge(v_post, upto(i * 6 + post[0]))
                dve.wait_ge(r_mean, upto(i + 1))
                after(v.scalar_tensor_tensor(halves(t2), ps[:, 4:6, :], -1.0 / RW_H, halves(A), ALU.mult, ALU.add))
                dve.wait_ge(a_yr, upto(i + 1))
                after(v.reciprocal(t1, t1))
                after(v.tensor_tensor(t2, t2, t1, ALU.mult))
                after(v.tensor_scalar(t2, t2, par(PR_LNW), par(PR_LNB), ALU.mult, ALU.add))
                after(v.tensor_tensor(t2, t2, rw["bv"], ALU.add))
                after(v.tensor_tensor(t2, t2, rw["g"], ALU.mult))

            v.memset(lr["xp"][:, 0:3], 0.0).then_inc(l_z, 1)
            with dve.Fori(0, TURNS["lru"]) as i:
                for u in range(2):
                    n = i * 2 + u
                    lp = lambda c: lru_par[0:80, bass.ds(n + c, 1)]
                    xpv, xa, gx, a2, aa, hh, ya, gy = (lr[k][0:80] for k in ("xp", "xa", "gx", "a2", "aa", "h", "ya", "gy"))
                    ada_pair(4, n + ADA0)
                    dve.wait_ge(l_x, upto(n + 1))
                    v.tensor_scalar(xa, xpv[:, 3:3 + T], lp(LP_CW + 48), lp(LP_CB), ALU.mult, ALU.add).then_inc(l_cv, 1)
                    for j in range(3):
                        dve.wait_ge(l_cv, upto(n * 4 + j + 1))
                        v.scalar_tensor_tensor(xa, xpv[:, j:j + T], lp(LP_CW + 16 * j), xa, ALU.mult, ALU.add).then_inc(l_cv, 1)
                    dve.wait_ge(l_cv, upto(n * 4 + 4))
                    dve.wait_ge(l_exp, upto(n * 2 + 1))
                    v.tensor_scalar(a2, a2, 1.0, None, ALU.min).then_inc(l_sq, 1)
                    dve.wait_ge(s_yb, upto(PAIRS * 16))
                    dve.wait_ge(s_gst, upto(PAIRS * 48))
                    dve.wait_ge(l_sa, upto(n * 2 + 2))
                    v.tensor_tensor(gx, gx, xa, ALU.mult).then_inc(l_u, 1)
                    dve.wait_ge(l_u, upto(n * 3 + 1))
                    dve.wait_ge(l_rt, upto(n + 1))
                    v.tensor_tensor(gx, gx, a2, ALU.mult).then_inc(l_u, 1)
                    dve.wait_ge(l_u, upto(n * 3 + 2))
                    dve.wait_ge(l_exp, upto(n * 2 + 2))
                    v.tensor_tensor_scan(hh, aa, gx, 0.0, ALU.mult, ALU.add).then_inc(l_u, 1)
                    dve.wait_ge(l_u, upto(n * 3 + 3))
                    dve.wait_ge(l_gy, upto(n + 1))
                    dve.wait_ge(s_ya, upto(n * 16))
                    v.tensor_tensor(ya, hh, gy, ALU.mult).then_inc(l_out, 1)

            dve.wait_ge(l_out, upto(LRU_N))
            dve.wait_ge(s_ya, upto(LRU_N * 16))
            for g in range(2):
                v.memset(ak[:, g, 0:P], 0.0).then_inc(t_z, 1)
                v.memset(av[:, g, 0, :], 0.0).then_inc(t_z, 1)
            dve.wait_ge(gain_sem, 64)
            v.tensor_scalar(nsinks[:, :], sinks_b, -1.0, None, ALU.mult).then_inc(t_z, 1)
            dve.wait_ge(t_z, upto(5))
            amask = at_["mask"].rearrange("p (o m) -> p o m", o=2)
            PIECES = 4

            def invert(gg, c, piece=slice(0, T)):
                n = gg * 3 + c
                dve.wait_ge(t_rt, upto(n + 1))
                t = roots[:, c, piece]
                v.reciprocal(t, t).then_inc(t_rc, 1)

            def norm(gg, c):
                r = roots[:, c, :]
                n = gg * 3 + c
                dve.wait_ge(t_rc, upto(n + 1 if gg == 0 else n + 1 + (PIECES - 1) * (gg - (c < 2))))
                if c == 0:
                    v.scalar_tensor_tensor(ak[0:64, gg % 2, P:T + P], at_["kvt"][0:64, :], gains[0:64, 1:2], r[0:64, :], ALU.mult, ALU.mult).then_inc(t_n, 1)
                else:
                    q = aq[gg % 2][:, c - 1, :]
                    v.scalar_tensor_tensor(q, q, gains[:, 0:1], r, ALU.mult, ALU.mult).then_inc(t_n, 1)

            def project(gg):
                for c in range(3 if gg == 0 else 2):
                    invert(gg, c)
                    if c == 0 and gg >= 2:
                        dve.wait_ge(t_sc, upto((gg - 1) * UNITS))
                    norm(gg, c)

            def attend(gg):
                for tick in range(UNITS + 1):
                    if tick < UNITS:
                        u, t, n = tick, tick // 8, tick % 8
                        U = gg * UNITS + u
                        sm, sc = asm[:, u % 4, :], asc[:, u % 4, :, :]
                        sk = sinks_b[:, gg * 4 + 2 * t:gg * 4 + 2 * t + 2]
                        dve.wait_ge(t_sc, upto(U + 1))
                        if u >= 4:
                            dve.wait_ge(t_pt, upto(U - 3))
                        v.scalar_tensor_tensor(sc, ps[:, 4 - 2 * (u % 2):6 - 2 * (u % 2), 0:256], HEAD ** -0.5,
                                               amask[:, min(n, 1), :].unsqueeze(1).broadcast_to([P, 2, 256]), ALU.mult, ALU.add).then_inc(t_d, 1)
                        dve.wait_ge(t_d, upto(U * 4 + 1))
                        v.tensor_reduce(sm[:, 0:2], sc, AX.X, ALU.max).then_inc(t_d, 1)
                        dve.wait_ge(t_d, upto(U * 4 + 2))
                        v.scalar_tensor_tensor(sm[:, 2:4], sm[:, 0:2], -1.0, nsink(gg, t), ALU.mult, ALU.min).then_inc(t_d, 1)
                        dve.wait_ge(t_d, upto(U * 4 + 3))
                        v.tensor_tensor(sm[:, 6:8], sk, sm[:, 2:4], ALU.add).then_inc(t_d, 1)
                    if tick >= 1:
                        u = tick - 1
                        U = gg * UNITS + u
                        sm, sc = asm[:, u % 4, :], asc[:, u % 4, :, :]
                        dve.wait_ge(t_e, upto(U * 3 + 3))
                        v.tensor_tensor(sm[:, 8:10], sm[:, 4:6], sm[:, 6:8], ALU.add).then_inc(t_dc, 1)
                        dve.wait_ge(t_dc, upto(U * 2 + 1))
                        v.reciprocal(sm[:, 10:12], sm[:, 8:10]).then_inc(t_dc, 1)
                        dve.wait_ge(t_dc, upto(U * 2 + 2))
                        for h in range(2):
                            v.tensor_scalar(sc[:, h, :], sc[:, h, :], sm[:, 10 + h:11 + h], None, ALU.mult).then_inc(t_p, 1)
                    if gg + 1 < GROUPS and 2 <= tick < 2 + PIECES:
                        width = T // PIECES
                        invert(gg + 1, 2, slice((tick - 2) * width, (tick - 1) * width))
                    if gg + 1 < GROUPS and tick == 2 + PIECES:
                        norm(gg + 1, 2)
                    if gg == GROUPS - 1 and tick - 1 in Y_TICKS:
                        low_y(0, Y_TICKS.index(tick - 1))

            def low_y(g, k):
                at = HALF * (g % 2) + k
                dve.wait_ge(m_hi, upto(Y0[g] + k + 1))
                v.tensor_tensor(x_lo[:, at, :], yraw[:, (Y0[g] + k) % 2, :], x_hi[:, at, :].bitcast(F32), ALU.subtract).then_inc(m_lo, 1)
            project(0)
            for gg in range(GROUPS):
                if gg + 1 < GROUPS:
                    project(gg + 1)
                if gg == 0:
                    dve.wait_ge(s_am, 16)
                attend(gg)

            v.tensor_scalar(mod[:, MOD_SC2:MOD_SC2 + 8], mod[:, MOD_SC2:MOD_SC2 + 8], 1.0, None, ALU.add).then_inc(ada_fix, 1)
            dve.wait_ge(ada_fix, upto(2))

            for t in range(2):
                dve.wait_ge(s_yc[t], upto(GROUPS * 16))
            gated = 0

            def split_y(g, part):
                if g < len(BR):
                    for k in range(BR[g][1])[part]:
                        low_y(g, k)
            for g, (nm, kts, _, _, _, gi) in enumerate(BR):
                for part in PARTS:
                    with dve.Fori(part.start, part.stop) as i:
                        for c in range(2):
                            blk = Block(nm, c, i)
                            partial = halves2(x2[:, bass.ds(i * 2 + c, 1), :])
                            acc, t = mix[:, bass.ds(i * 2 + c, 1), :].rearrange("p o n -> p (o n)"), mt[:, c, :]
                            m0 = EV0[nm] + (i * 2 + c) * M_EV[nm]
                            dve.wait_ge(s_dense, upto(blk.before + 1))
                            if nm in ("oa0", "oc0", "ob0"):
                                v.tensor_copy(partial, pair_of(blk.slot)).then_inc(m_ev, 1)
                            elif gi is None:
                                v.tensor_tensor(partial, pair_of(blk.slot), partial, ALU.add).then_inc(m_ev, 1)
                            else:
                                v.tensor_tensor(halves(t), pair_of(blk.slot), partial, ALU.add).then_inc(m_ev, 1)
                                dve.wait_ge(m_ev, upto(m0 + 1))
                                dve.wait_ge(s_g[c], i * 16 + (gated * 64 + 16))
                                if gi == 0:
                                    v.tensor_tensor(acc, t, gtl[:, c, :], ALU.mult).then_inc(m_ev, 1)
                                else:
                                    v.tensor_tensor(t, t, gtl[:, c, :], ALU.mult).then_inc(m_ev, 1)
                                    dve.wait_ge(m_ev, upto(m0 + 2))
                                    v.tensor_tensor(acc, acc, t, ALU.add).then_inc(m_ev, 1)
                    split_y(g + 1, part)
                gated += gi is not None
            for m in range(KT):
                at = (HALF * (len(BR) % 2) + m) % KT
                dve.wait_ge(m_hi, upto(NY + m + 1))
                v.tensor_tensor(x_lo[:, at, :], mix[:, m, :], x_hi[:, at, :].bitcast(F32), ALU.subtract).then_inc(m_lo, 1)
            dve.wait_ge(m_xt, upto(8))
            for half in range(2):
                with dve.Fori(0, 4) as i:
                    for c in range(2):
                        blk = Block(f"wout{half}", c, i)
                        dve.wait_ge(s_dense, upto(blk.before + 1))
                        r = halves2(x2[:, bass.ds(i * 2 + c, 1), :])
                        v.scalar_tensor_tensor(r, pair_of(blk.slot), mod[:, bass.ds(i * 2 + (MOD_G1 + c), 1)], r, ALU.mult, ALU.add).then_inc(m_res, 1)
                dve.wait_ge(m_res, upto(8 * half + 8))
            rs = yraw[:, 0, :]
            dve.wait_ge(m_rt, upto(1))
            v.reciprocal(rs, rs).then_inc(m_n, 1)
            dve.wait_ge(m_n, upto(1))
            for k in range(KT):
                t = mt[:, k % 2, :]
                v.scalar_tensor_tensor(t, x2[:, k, :], mod[:, MOD_SC2 + k:MOD_SC2 + k + 1], rs, ALU.mult, ALU.mult).then_inc(m_nh, 1)
                dve.wait_ge(m_nh, upto(2 * k + 1))
                dve.wait_ge(m_hi, upto(NY + KT + k + 1))
                v.scalar_tensor_tensor(x_lo[:, k, :], t, mod[:, MOD_SH2 + k:MOD_SH2 + k + 1], x_hi[:, k, :].bitcast(F32), ALU.add, ALU.subtract).then_inc(m_nh, 1)

            def product(blk, tile, t):
                dve.wait_ge(s_dense, upto(blk.before + 1))
                dve.wait_ge(m_sil, upto(tile + 1))
                v.tensor_tensor(halves(mt[:, t, :]), pair_of(blk.slot), halves(gtl[:, 0, :]), ALU.mult).then_inc(m_act, 1)

            def hidden_low(tile, t):
                dve.wait_ge(m_act, upto(tile + 1))
                dve.wait_ge(m_hh, upto(tile + 1))
                v.tensor_tensor(hid_lo[:, t, :], mt[:, t, :], hid_hi[:, t, :].bitcast(F32), ALU.subtract).then_inc(m_hl, 1)

            def add_down(name, c0, i, turn):
                for m in range(8):
                    if m % 4 == 3:
                        dve.wait_ge(s_dense, upto(Block(name, c0 + m // 4, i).before + 1))
                    else:
                        dve.wait_ge(m_dd, upto(turn * 6 + m - m // 4 + 1))
                    if m == 0:
                        dve.wait_ge(m_dn, upto(turn * 8))
                    r = halves(x2[:, m, :])
                    v.scalar_tensor_tensor(r, ps[:, 4 + 2 * (m % 2):6 + 2 * (m % 2), :], mod[:, MOD_G2 + m:MOD_G2 + m + 1], r, ALU.mult, ALU.add).then_inc(m_dn, 1)
            product(Block("ffn_first", 1), 0, 0)
            hidden_low(0, 0)
            with dve.Fori(0, TURNS["ffn"]) as i:
                product(Block("ffn", 1, i), i * 2 + 1, 1)
                hidden_low(i * 2 + 1, 1)
                product(Block("ffn", 3, i), i * 2 + 2, 0)
                add_down("ffn", 4, i, i)
                hidden_low(i * 2 + 2, 0)
            product(Block("ffn_last", 1), 2 * TURNS["ffn"] + 1, 1)
            hidden_low(2 * TURNS["ffn"] + 1, 1)
            add_down("ffn_last", 2, 0, TURNS["ffn"])


INPUTS = ["x", "c", "w_ada", "b_ada", "w_in", "conv_w", "conv_b", "lru_wa", "lru_ba", "lru_wx", "lru_bx", "lru_lambda",
          "w_lru_o", "rw_mu", "rw_w0", "rw_w2", "rw_a0", "rw_a2", "rw_g2", "rw_kk", "rw_ka", "rw_rk", "rw_ln_w", "rw_ln_b",
          "w_rw_o", "q_gain", "k_gain", "sinks", "w_att_o", "w_out", "w_ffn_in", "w_ffn_out"]


def kernel(**inputs):
    import concourse.bacc as _bacc
    from concourse.bass_utils import run_bass_kernel_spmd as _run

    nc = _bacc.Bacc("TRN2", target_bir_lowering=False, num_devices=1)
    arrays, aps = {}, {}
    for name in INPUTS:
        arr = np.ascontiguousarray(inputs[name])
        arrays[f"in_{name}"] = arr
        aps[name] = nc.dram_tensor(f"in_{name}", arr.shape, F32, kind="ExternalInput").ap()
    arrays["in_consts"] = constants()
    aps["consts"] = nc.dram_tensor("in_consts", (P, C_N), F32, kind="ExternalInput").ap()
    out = nc.dram_tensor("out", (1, T, D), F32, kind="ExternalOutput").ap()
    build(nc, aps, out)
    return _run(nc, [arrays], core_ids=[0]).results[0]["out"]
```
